# Optimizing a Trainium2 kernel written in Bass

```python
import math
import jax, jax.numpy as jnp
from jax import lax
import numpy as np

D_MODEL = 1024
BATCH = 1
SEQ = 512
DEPTH = 2
DEC_BATCH = 8
DEC_SEQ = 8
PAST_LEN = 1024
PAGE_SIZE = 128

D_A = D_MODEL // 2
CONV_W = 3
HD_B = 64
D_B = D_MODEL // 2
H_B = D_B // HD_B
R_W = 64
R_A = 64
R_G = 128
N_SHIFT = 3 * D_B + R_W + R_A + R_G
LNX_EPS = 64e-5
H_C = 4
DH_C = 64
Q_W = 2 * H_C * DH_C
K_W = 2 * H_C * DH_C
D_C = H_C * 2 * DH_C
SUBLN_EPS = 1e-5
Q_BLOCK = 128
N_IN = 3 * D_A + N_SHIFT + Q_W + K_W + D_C + 3 * D_MODEL
D_FF = 2816
NORM_EPS = 1e-6

kernel_name = 'hybrid_conv_rwkv7_diffattn_decoder_step'

def rms_norm(x, w, eps=NORM_EPS):
    xf = x.astype(jnp.float32)
    y = xf * lax.rsqrt(jnp.mean(xf * xf, axis=-1, keepdims=True) + eps)
    return (y * w.astype(jnp.float32)).astype(x.dtype)

def swiglu(h, w_gate, w_up, w_down):
    return (jax.nn.silu(h @ w_gate) * (h @ w_up)) @ w_down

def short_conv(xin, gb, gc, conv_w, conv_state):
    u = gc * xin
    ext = jnp.concatenate([conv_state.astype(u.dtype), u], axis=1)
    T = u.shape[1]
    y = ext[:, 0:T] * conv_w[0]
    for j in range(1, CONV_W):
        y = y + ext[:, j:j + T] * conv_w[j]
    return gb * y, ext[:, -(CONV_W - 1):]

def wkv7_scan(r, w, k, v, a, b, s0):
    def step(S, inp):
        r_t, w_t, k_t, v_t, a_t, b_t = inp
        sa = jnp.einsum('bhvk,bhk->bhv', S, a_t)
        S = S * w_t[:, :, None, :] + sa[..., None] * b_t[:, :, None, :] + v_t[..., None] * k_t[:, :, None, :]
        return S, jnp.einsum('bhvk,bhk->bhv', S, r_t)
    xs = (jnp.swapaxes(r, 0, 1), jnp.swapaxes(w, 0, 1), jnp.swapaxes(k, 0, 1),
          jnp.swapaxes(v, 0, 1), jnp.swapaxes(a, 0, 1), jnp.swapaxes(b, 0, 1))
    s_final, y = lax.scan(step, s0, xs)
    return jnp.swapaxes(y, 0, 1), s_final

def rwkv7_mix(z, shift_state, wkv_state, mu, w_up, w0, a_up, a0, g_up, k_k, k_a, r_k, lnx_w, lnx_b):
    B, T, _ = z.shape
    f32 = jnp.float32
    z_prev = jnp.concatenate([shift_state[:, None].astype(z.dtype), z[:, :-1]], axis=1)
    zm = z + (z_prev - z) * mu
    r, k, v, w_lo, a_lo, g_lo = jnp.split(
        zm, [D_B, 2 * D_B, 3 * D_B, 3 * D_B + R_W, 3 * D_B + R_W + R_A], axis=-1)
    heads = lambda t: t.reshape(B, T, H_B, HD_B)
    w_log = -jax.nn.softplus(-(w0 + jnp.tanh(w_lo) @ w_up).astype(f32)) - 0.5
    decay = jnp.exp(-jnp.exp(w_log))
    a = jax.nn.sigmoid(a0 + a_lo @ a_up)
    g = jax.nn.sigmoid(g_lo) @ g_up
    kk = heads(k * k_k).astype(f32)
    kk = kk * lax.rsqrt(jnp.maximum(jnp.sum(kk * kk, axis=-1, keepdims=True), 1e-24))
    k = k * (1 + (a - 1) * k_a)
    rh, kh, vh, ah = heads(r), heads(k), heads(v), heads(a)
    y, s_new = wkv7_scan(rh.astype(f32), heads(decay), kh.astype(f32), vh.astype(f32),
                         -kk, kk * ah.astype(f32), wkv_state.astype(f32))
    mean = jnp.mean(y, axis=-1, keepdims=True)
    var = jnp.mean(jnp.square(y - mean), axis=-1, keepdims=True)
    yn = ((y - mean) * lax.rsqrt(var + LNX_EPS)).reshape(B, T, D_B) * lnx_w + lnx_b
    bonus = (jnp.sum(rh * kh * r_k, axis=-1, keepdims=True) * vh).reshape(B, T, D_B)
    out = (yn.astype(z.dtype) + bonus) * g
    return out, z[:, -1], s_new.astype(wkv_state.dtype)

def alibi_slopes():
    return jnp.asarray([2.0 ** (-8.0 * (h + 1) / H_C) for h in range(H_C)], jnp.float32)

def diff_attn_block(q, k, v, q_pos, k_pos, lam, subln_w, lam_init):
    s = jnp.einsum('bqhd,bkhd->bhqk', q, k).astype(jnp.float32) * (DH_C ** -0.5)
    dist = (q_pos[:, None] - k_pos[None, :]).astype(jnp.float32)
    slopes = jnp.repeat(alibi_slopes(), 2)
    s = s - slopes[:, None, None] * dist
    s = jnp.where(dist >= 0, s, -jnp.inf)
    p = jax.nn.softmax(s, axis=-1)
    B, _, Tq, Tk = p.shape
    p = p.reshape(B, H_C, 2, Tq, Tk)
    attn = p[:, :, 0] - lam * p[:, :, 1]
    o = jnp.einsum('bhqk,bkhe->bqhe', attn.astype(v.dtype), v)
    o = rms_norm(o, subln_w, SUBLN_EPS) * (1.0 - lam_init)
    return o.reshape(B, Tq, D_C)

def prompt_attention(q, k, v, lam, subln_w, lam_init):
    B, T = q.shape[0], q.shape[1]
    nb = T // Q_BLOCK
    k_pos = jnp.arange(T)
    qb = jnp.swapaxes(q.reshape(B, nb, Q_BLOCK, 2 * H_C, DH_C), 0, 1)
    def blk(args):
        i, q_i = args
        q_pos = i * Q_BLOCK + jnp.arange(Q_BLOCK)
        return diff_attn_block(q_i, k, v, q_pos, k_pos, lam, subln_w, lam_init)
    o = lax.map(blk, (jnp.arange(nb), qb))
    return jnp.swapaxes(o, 0, 1).reshape(B, T, D_C)

def sample_attention(q, k_new, v_new, cache_k, cache_v, page_table, l, lam, subln_w, lam_init):
    Bd, Tn = q.shape[0], q.shape[1]
    past_len = page_table.shape[1] * PAGE_SIZE
    k_past = cache_k[l, page_table].reshape(Bd, past_len, 2 * H_C, DH_C)
    v_past = cache_v[l, page_table].reshape(Bd, past_len, H_C, 2 * DH_C)
    k_all = jnp.concatenate([k_past.astype(k_new.dtype), k_new], axis=1)
    v_all = jnp.concatenate([v_past.astype(v_new.dtype), v_new], axis=1)
    q_pos = past_len + jnp.arange(Tn)
    k_pos = jnp.arange(past_len + Tn)
    return diff_attn_block(q, k_all, v_all, q_pos, k_pos, lam, subln_w, lam_init)

def run_trunk(x, W, conv0, shift0, wkv0, attend):
    k_rows, v_rows, wkv_out, shift_out, conv_out = [], [], [], [], []
    B, T = x.shape[0], x.shape[1]
    for l in range(DEPTH):
        x = x + 0.5 * swiglu(rms_norm(x, W['ffn1_norm'][l]), W['ffn1_w_gate'][l], W['ffn1_w_up'][l], W['ffn1_w_down'][l])
        h = rms_norm(x, W['mix_norm'][l])
        proj = h @ W['w_in'][l]
        o1 = D_A; o2 = 2 * D_A; o3 = 3 * D_A; o4 = o3 + N_SHIFT
        o5 = o4 + Q_W; o6 = o5 + K_W; o7 = o6 + D_C
        xin, gb, gc, z, q, k, v, gates = jnp.split(proj, [o1, o2, o3, o4, o5, o6, o7], axis=-1)
        y_a, conv_new = short_conv(xin, gb, gc, W['conv_w'][l], conv0[l])
        y_b, shift_new, wkv_new = rwkv7_mix(
            z, shift0[l], wkv0[l], W['tm_mu'][l], W['w_up_w'][l], W['w0'][l], W['a_up_w'][l], W['a0'][l],
            W['g_up_w'][l], W['k_k'][l], W['k_a'][l], W['r_k'][l], W['lnx_w'][l], W['lnx_b'][l])
        q = q.reshape(B, T, 2 * H_C, DH_C)
        k = k.reshape(B, T, 2 * H_C, DH_C)
        v = v.reshape(B, T, H_C, 2 * DH_C)
        lam_init = 0.8 - 0.6 * math.exp(-0.3 * l)
        lam = (jnp.exp(jnp.sum(W['lam_q1'][l].astype(jnp.float32) * W['lam_k1'][l].astype(jnp.float32)))
               - jnp.exp(jnp.sum(W['lam_q2'][l].astype(jnp.float32) * W['lam_k2'][l].astype(jnp.float32)))
               + lam_init)
        y_c = attend(l, q, k, v, lam, W['subln_w'][l], lam_init)
        g_a, g_b, g_c = jnp.split(jax.nn.sigmoid(gates), 3, axis=-1)
        merged = (g_a * (y_a @ W['w_branch_a'][l]) + g_b * (y_b @ W['w_branch_b'][l])
                  + g_c * (y_c @ W['w_branch_c'][l]))
        x = x + merged @ W['w_out'][l]
        x = x + 0.5 * swiglu(rms_norm(x, W['ffn2_norm'][l]), W['ffn2_w_gate'][l], W['ffn2_w_up'][l], W['ffn2_w_down'][l])
        k_rows.append(k); v_rows.append(v); wkv_out.append(wkv_new)
        shift_out.append(shift_new); conv_out.append(conv_new)
    y = rms_norm(x, W['final_norm'])
    return (y, jnp.stack(k_rows), jnp.stack(v_rows), jnp.stack(wkv_out),
            jnp.stack(shift_out), jnp.stack(conv_out))

def setup_inputs(seed: int = 0) -> dict:
    key = jax.random.key(seed)
    keys = jax.random.split(key, 48)
    ks = iter([keys[i] for i in range(48)])
    def nrm(shape, scale=1.0):
        return jax.random.normal(next(ks), shape, jnp.float32) * scale
    L = DEPTH
    n_pages = PAST_LEN // PAGE_SIZE
    n_pool = (DEC_BATCH * n_pages * 5) // 4
    x_prompt = nrm((BATCH, SEQ, D_MODEL))
    x_sample = nrm((DEC_BATCH, DEC_SEQ, D_MODEL))
    cache_k = nrm((L, n_pool, PAGE_SIZE, 2 * H_C, DH_C))
    cache_v = nrm((L, n_pool, PAGE_SIZE, H_C, 2 * DH_C))
    state_wkv = nrm((L, DEC_BATCH, H_B, HD_B, HD_B), 0.1)
    state_shift = nrm((L, DEC_BATCH, N_SHIFT))
    state_conv = nrm((L, DEC_BATCH, CONV_W - 1, D_A))
    page_table = jax.random.permutation(next(ks), n_pool)[: DEC_BATCH * n_pages].reshape(DEC_BATCH, n_pages).astype(jnp.int32)
    return {
        'x_prompt': x_prompt, 'x_sample': x_sample,
        'cache_k': cache_k, 'cache_v': cache_v,
        'state_wkv': state_wkv, 'state_shift': state_shift, 'state_conv': state_conv,
        'page_table': page_table,
        'ffn1_norm': 1.0 + nrm((L, D_MODEL), 0.02),
        'ffn1_w_gate': nrm((L, D_MODEL, D_FF), D_MODEL ** -0.5),
        'ffn1_w_up': nrm((L, D_MODEL, D_FF), D_MODEL ** -0.5),
        'ffn1_w_down': nrm((L, D_FF, D_MODEL), D_FF ** -0.5),
        'mix_norm': 1.0 + nrm((L, D_MODEL), 0.02),
        'w_in': nrm((L, D_MODEL, N_IN), D_MODEL ** -0.5),
        'conv_w': nrm((L, CONV_W, D_A), CONV_W ** -0.5),
        'tm_mu': jax.random.uniform(next(ks), (L, N_SHIFT), jnp.float32),
        'w_up_w': nrm((L, R_W, D_B), R_W ** -0.5),
        'w0': nrm((L, D_B), 0.5),
        'a_up_w': nrm((L, R_A, D_B), R_A ** -0.5),
        'a0': nrm((L, D_B), 0.1),
        'g_up_w': nrm((L, R_G, D_B), R_G ** -0.5),
        'k_k': 0.85 + nrm((L, D_B), 0.02),
        'k_a': 1.0 + nrm((L, D_B), 0.02),
        'r_k': nrm((L, H_B, HD_B), 0.1),
        'lnx_w': 1.0 + nrm((L, D_B), 0.02),
        'lnx_b': nrm((L, D_B), 0.01),
        'lam_q1': nrm((L, DH_C), 0.1),
        'lam_k1': nrm((L, DH_C), 0.1),
        'lam_q2': nrm((L, DH_C), 0.1),
        'lam_k2': nrm((L, DH_C), 0.1),
        'subln_w': 1.0 + nrm((L, 2 * DH_C), 0.02),
        'w_branch_a': nrm((L, D_A, D_MODEL), D_A ** -0.5),
        'w_branch_b': nrm((L, D_B, D_MODEL), D_B ** -0.5),
        'w_branch_c': nrm((L, D_C, D_MODEL), D_C ** -0.5),
        'w_out': nrm((L, D_MODEL, D_MODEL), D_MODEL ** -0.5),
        'ffn2_norm': 1.0 + nrm((L, D_MODEL), 0.02),
        'ffn2_w_gate': nrm((L, D_MODEL, D_FF), D_MODEL ** -0.5),
        'ffn2_w_up': nrm((L, D_MODEL, D_FF), D_MODEL ** -0.5),
        'ffn2_w_down': nrm((L, D_FF, D_MODEL), D_FF ** -0.5),
        'final_norm': 1.0 + nrm((D_MODEL,), 0.02),
    }

def reference(x_prompt, x_sample, cache_k, cache_v, state_wkv, state_shift, state_conv, page_table,
              ffn1_norm, ffn1_w_gate, ffn1_w_up, ffn1_w_down, mix_norm, w_in, conv_w, tm_mu,
              w_up_w, w0, a_up_w, a0, g_up_w, k_k, k_a, r_k, lnx_w, lnx_b,
              lam_q1, lam_k1, lam_q2, lam_k2, subln_w, w_branch_a, w_branch_b, w_branch_c, w_out,
              ffn2_norm, ffn2_w_gate, ffn2_w_up, ffn2_w_down, final_norm):
    W = dict(ffn1_norm=ffn1_norm, ffn1_w_gate=ffn1_w_gate, ffn1_w_up=ffn1_w_up, ffn1_w_down=ffn1_w_down,
             mix_norm=mix_norm, w_in=w_in, conv_w=conv_w, tm_mu=tm_mu, w_up_w=w_up_w, w0=w0,
             a_up_w=a_up_w, a0=a0, g_up_w=g_up_w, k_k=k_k, k_a=k_a, r_k=r_k, lnx_w=lnx_w, lnx_b=lnx_b,
             lam_q1=lam_q1, lam_k1=lam_k1, lam_q2=lam_q2, lam_k2=lam_k2, subln_w=subln_w,
             w_branch_a=w_branch_a, w_branch_b=w_branch_b, w_branch_c=w_branch_c, w_out=w_out,
             ffn2_norm=ffn2_norm, ffn2_w_gate=ffn2_w_gate, ffn2_w_up=ffn2_w_up, ffn2_w_down=ffn2_w_down,
             final_norm=final_norm)
    bp = x_prompt.shape[0]
    conv0 = jnp.zeros((DEPTH, bp, CONV_W - 1, D_A), x_prompt.dtype)
    shift0 = jnp.zeros((DEPTH, bp, N_SHIFT), x_prompt.dtype)
    wkv0 = jnp.zeros((DEPTH, bp, H_B, HD_B, HD_B), x_prompt.dtype)
    attend_prompt = lambda l, q, k, v, lam, sw, li: prompt_attention(q, k, v, lam, sw, li)
    y_prompt, k_prompt, v_prompt, wkv_prompt, shift_prompt, conv_prompt = run_trunk(
        x_prompt, W, conv0, shift0, wkv0, attend_prompt)
    attend_sample = lambda l, q, k, v, lam, sw, li: sample_attention(q, k, v, cache_k, cache_v, page_table, l, lam, sw, li)
    y_sample, k_sample, v_sample, wkv_sample, shift_sample, conv_sample = run_trunk(
        x_sample, W, state_conv, state_shift, state_wkv, attend_sample)
    return (y_prompt, y_sample, k_prompt, v_prompt, k_sample, v_sample,
            wkv_prompt, wkv_sample, shift_prompt, shift_sample, conv_prompt, conv_sample)


_drawn_inputs = setup_inputs


def setup_inputs(seed=0):
    import zlib

    import numpy as np

    out = dict(_drawn_inputs(seed))
    spreads = {}
    factors = {'ffn1_norm': 3.411,
     'k_k': 200.0,
     'lnx_w': 28.029,
     'lnx_b': 55.402,
     'lam_q1': 21.897,
     'lam_k2': 18.801,
     'subln_w': 18.058,
     'ffn2_norm': 5.857,
     'final_norm': 20.365,
     'r_k': 5.104,
     'lam_q2': 8.0}
    for name, (base, spread) in spreads.items():
        noise = np.random.default_rng([zlib.crc32(name.encode()), seed]).standard_normal(out[name].shape)
        drawn = base * np.exp(spread * noise) if base else spread * noise
        out[name] = __import__('jax').numpy.asarray(drawn.astype(out[name].dtype))
    for name, factor in factors.items():
        out[name] = (out[name] * factor).astype(out[name].dtype)
    return out
```

```python
import math
from contextlib import ExitStack

import numpy as np
import concourse.bass as bass
from concourse import mybir

F32 = mybir.dt.float32
F32R = mybir.dt.float32r
I32 = mybir.dt.int32
ALU = mybir.AluOpType
ACT = mybir.ActivationFunctionType
AX = mybir.AxisListType
ds = bass.ds

P = 128
L = 2
D = 1024
KD = D // P
FF = 2816
KF = FF // P
HF = KF // 2
TP, NB, TS = 512, 8, 8
NS = NB * TS
NT = TP + NS
NH = NT // 2
DB = 512
CB = DB // P
NSHIFT = 3 * DB + 256
CZ = NSHIFT // P
N_IN = 3 * DB + NSHIFT + 3 * DB + 3 * D
COL_Z = 3 * DB // P
COL_Q = COL_Z + CZ
COL_G = COL_Q + 3 * CB
PAST, PAGE = 1024, 128
NPG = PAST // PAGE
HC, MAPS = 4, 8
W = 64
NW = NT // W
NEG = -1.0e30
BASE, LIMIT = 16512, 229344
VEC = {}
_at = 0
for _n, _c in (("ffn1_norm", KD), ("mix_norm", KD), ("ffn2_norm", KD), ("tm_mu", CZ), ("w0", CB), ("a0", CB),
               ("k_k", CB), ("k_a", CB), ("r_k", CB), ("lnx_w", CB), ("lnx_b", CB), ("conv_w", 3 * CB), ("subln_w", 1)):
    VEC[_n] = (_at, _c)
    _at += _c
NVEC = _at


def shape_constants():
    p = np.arange(P)
    half = p // W
    s64 = p % W
    same = (half[:, None] == half[None, :])
    c = {}
    c["ident"] = np.eye(P)
    c["halves"] = same
    slopes = np.array([2.0 ** (-8.0 * (h + 1) / HC) for h in range(HC)])
    t = np.arange(TP)
    dist = p[:, None] - (t[None, :] - (TP - P))
    c["alibi_prompt"] = np.stack([np.where(dist >= 0, -s * dist, NEG) for s in slopes], 1).reshape(P, -1)
    row = np.arange(P)
    m, q = (row % 64) // TS, row % TS
    sl = slopes[m // 2]
    c["alibi_past"] = -sl[:, None] * (PAST + q[:, None] - np.arange(PAST)[None, :])
    kb, ks = np.arange(NS) // TS, np.arange(NS) % TS
    new = np.full((P, NB, NS), NEG)
    for b in range(NB):
        ok = (kb[None, :] == b) & (ks[None, :] <= q[:, None])
        new[:, b] = np.where(ok, -sl[:, None] * (q[:, None] - ks[None, :]), NEG)
    c["alibi_new"] = new.reshape(P, -1)
    s_, t_ = s64[:, None], s64[None, :]
    strict = same & (s_ < t_)
    incl = s_ <= np.arange(W)[None, :]
    sb = (s_ // TS == t_ // TS)
    sbi = (s_ // TS == np.arange(W)[None, :] // TS)
    c["gram_mask"] = np.stack([np.concatenate([strict, incl], 1), np.concatenate([strict & sb, incl & sbi], 1)], 1).reshape(P, -1)
    lev = []
    for j in range(6):
        z = 1 << j
        lev.append(same & (s_ // (2 * z) == t_ // (2 * z)) & (s_ // z % 2 == 0) & (t_ // z % 2 == 1))
    c["level_mask"] = np.stack(lev, 1).reshape(P, -1)
    tt = np.arange(NT)
    first = np.where(tt < TP, tt % W == 0, tt % TS == 0)
    c["carry"] = np.broadcast_to(1.0 - first, (P, NT))
    c["batch_mask"] = (s64[:, None] // TS == np.arange(NB)[None, :])
    e = np.zeros((P, 2, HC * TS))
    for r in range(64):
        mm, qq = r // TS, r % TS
        e[r, mm % 2, (mm // 2) * TS + qq] = 1.0
    c["combine"] = e.reshape(P, -1)
    li = np.array([0.8 - 0.6 * math.exp(-0.3 * l) for l in range(L)])
    c["lam_init"] = np.broadcast_to(np.concatenate([li, 1.0 - li])[None, :], (P, 2 * L))
    return {k: np.ascontiguousarray(v, dtype=np.float32) for k, v in c.items()}


class Steps:

    def __init__(self, sem, stage, book, new):
        self.sem, self.stage, self.book, self.new = sem, stage, book, new
        self.n, self.per, self.it, self.start = 0, 0, None, 0
        self.credit = book.get((stage, "per"), 0)

    def loop(self, it):
        if self.it is None:
            self.start = self.n
        self.it, self.n = it, self.start
        self.per = self.book.get((self.stage, "per"), 0)

    def end(self, turns):
        per = self.n - self.start
        self.new[(self.stage, "per")] = per
        self.it, self.n = None, self.start + turns * per

    def did(self, ins, name=None):
        ins.then_inc(self.sem, 1)
        self.n += 1
        if name is not None:
            assert self.new.get((self.stage, name), self.n) == self.n, (self.stage, name)
            self.new[(self.stage, name)] = self.n

    def own(self, eng):
        v = self.credit + self.n
        if self.it is not None:
            v = self.it * self.per + v
        elif v == 0:
            return
        eng.wait_ge(self.sem, v)

    def wait(self, eng, name, it=0):
        v = self.credit + self.book.get((self.stage, name), 1)
        per = self.book.get((self.stage, "per"), 0)
        if not isinstance(it, int) or it:
            v = it * per + v
        eng.wait_ge(self.sem, v)


class Core:

    def __init__(self, nc, ctx, io, book):
        self.nc, self.io, self.book, self.new = nc, io, book, {}

        def sem(name):
            return ctx.enter_context(nc.semaphore(name))

        self.w_loaded = [sem("w_loaded0"), sem("w_loaded1")]
        self.w_hi = sem("w_hi")
        self.w_split = sem("w_split")
        self.mm_done = sem("mm_done")
        self.evac = [sem("evac0"), sem("evac1")]
        self.part_hi = sem("part_hi")
        self.part_lo = sem("part_lo")
        self.pe_steps, self.act_steps = sem("pe_steps"), sem("act_steps")
        self.dve_steps, self.pool_steps = sem("dve_steps"), sem("pool_steps")
        self.pe_turns, self.act_turns = sem("pe_turns"), sem("act_turns")
        self.dve_turns, self.pool_turns = sem("dve_turns"), sem("pool_turns")
        self.loads = [sem(f"loads{i}") for i in range(4)]
        self.stores = [sem(f"stores{i}") for i in range(2)]
        every = [self.w_hi, self.w_split, self.mm_done, self.part_hi, self.part_lo, self.pe_steps, self.act_steps,
                 self.dve_steps, self.pool_steps, self.pe_turns, self.act_turns, self.dve_turns, self.pool_turns,
                 *self.w_loaded, *self.evac, *self.loads, *self.stores]
        nums = sorted(s.num for s in every)
        assert nums == list(range(nums[0], nums[0] + len(nums)))
        self.all_sems = range(nums[0], nums[-1] + 1)

        at = BASE

        def fixed(name, shape, dt=F32):
            nonlocal at
            t = self.place(name, shape, at, dt)
            at += (4 * int(np.prod(shape[1:])) + 31) // 32 * 32
            return t

        self.ident = fixed("ident", [P, P])
        self.ones = fixed("ones", [P, P])
        self.halves = fixed("halves", [P, P])
        self.vec_all = fixed("vec_all", [P, L, NVEC + KD])
        self.vec = fixed("vec", [P, NVEC])
        self.neg_lam = fixed("neg_lam", [P, L])
        self.lam_init = fixed("lam_init", [P, 2 * L])
        self.nlam = fixed("nlam", [P, 1])
        self.one_li = fixed("one_li", [P, 1])
        self.eps = fixed("eps", [P, 4])
        self.pages = fixed("pages", [1, NB * NPG], I32)
        self.junk = fixed("junk", [P, 16])
        assert at <= BASE + 5120
        at = BASE + 5120
        self.x = fixed("x", [P, KD, NT])
        self.h_hi = fixed("h_hi", [P, KD, NT], F32R)
        self.h_lo = fixed("h_lo", [P, KD, NT], F32R)
        self.ring = at
        self.raw = [fixed(f"raw{s}", [P, KD, P]) for s in range(2)]
        self.whi = [fixed(f"whi{s}", [P, KD, P], F32R) for s in range(2)]
        self.wlo = [fixed(f"wlo{s}", [P, KD, P], F32R) for s in range(2)]
        self.r0 = at
        self.D = [ctx.enter_context(nc.psum_tensor(f"dense{s}", [P, 2, 512], F32)) for s in range(2)]
        self.E = [ctx.enter_context(nc.psum_tensor(f"extra{s}", [P, 2, 512], F32)) for s in range(2)]

    def place(self, name, shape, offset, dt=F32):
        return self.nc.alloc_sbuf_tensor_at(name, shape, dt, offset=offset)

    def region(self, prefix, at):
        here = [at]

        def tile(name, shape, dt=F32):
            t = self.place(f"{prefix}_{name}", shape, here[0], dt)
            here[0] += (4 * int(np.prod(shape[1:])) + 31) // 32 * 32
            assert here[0] <= LIMIT, (prefix, name, here[0])
            return t
        tile.at = here
        return tile

    def steps(self, sem, stage):
        return Steps(sem, stage, self.book, self.new)

    def barrier(self):
        self.nc.all_engine_barrier(sems_to_clear=self.all_sems)

    def credits(self, pool, steps=()):
        give = [(self.part_lo, 1), (self.w_split, 2), (self.mm_done, 2), (self.evac[0], 1), (self.evac[1], 1)]
        give += [(s.sem, s.credit) for s in steps if s.credit]
        for i, (s, n) in enumerate(give):
            pool.memset(self.junk[:, i:i + 1], 0.0).then_inc(s, n)

    def load_w(self, sp, k, s, src):
        sp.wait_ge(self.w_split, 2 * k + s + 1)
        sp.dma_start(self.raw[s][:, 0:src.shape[1], :], src).then_inc(self.w_loaded[s], 16)

    def split_hi(self, act, k):
        for s in range(2):
            act.wait_ge(self.w_loaded[s], 16 * k + 16)
            act.wait_ge(self.mm_done, 2 * k + s + 1)
            act.activation(self.whi[s][:], self.raw[s][:], ACT.Copy).then_inc(self.w_hi, 1)

    def split_lo(self, dve, k):
        for s in range(2):
            dve.wait_ge(self.w_hi, 2 * k + s + 1)
            dve.tensor_tensor(self.wlo[s][:], self.raw[s][:], self.whi[s][:].bitcast(F32), ALU.subtract)\
               .then_inc(self.w_split, 1)

    def products(self, pe, k, s, hi, lo, out, bank_use=None, first=True, last=True):
        pe.wait_ge(self.w_split, 2 * k + s + 3)
        if bank_use is not None:
            pe.wait_ge(self.evac[bank_use[0]], bank_use[1])
        chunks = hi.shape[1]
        for half in range(2):
            t = slice(half * NH, (half + 1) * NH)
            o = out[:, half, 0:NH]
            for c in range(chunks):
                w_hi, w_lo = self.whi[s][:, c, :], self.wlo[s][:, c, :]
                pe.matmul(o, w_hi, hi[:, c, t], start=(first and c == 0), stop=False)
                pe.matmul(o, w_hi, lo[:, c, t], start=False, stop=False)
                mm = pe.matmul(o, w_lo, hi[:, c, t], start=False, stop=(last and c == chunks - 1))
        mm.then_inc(self.mm_done, 1)

    @staticmethod
    def chase(eng, split, segments):
        split(0)
        k0 = 0
        for n, (pairs, unroll, finish) in enumerate(segments):
            last = n == len(segments) - 1
            turns = pairs // unroll - last

            def turn(i, final=False):
                for j in range(unroll):
                    if not (final and j == unroll - 1):
                        split(i * unroll + (k0 + j + 1))
                    finish(i * unroll + j, j, i)
            if turns:
                with eng.Fori(0, turns) as i:
                    turn(i)
            if last:
                turn(pairs // unroll - 1, True)
            k0 += pairs

    def norm_tiles(self, tile):
        self.sq = [tile(f"sq{i}", [P, NT]) for i in range(2)]
        self.rstd = tile("rstd", [P, NT])
        self.hf = [tile(f"hf{i}", [P, NT]) for i in range(2)]

    def norm_act(self, act, A, V, Q):
        for c in range(KD):
            if c >= 2:
                Q.wait(act, f"sum{c - 2}")
            A.did(act.activation(self.sq[c % 2][:], self.x[:, c, :], ACT.Square), f"sq{c}")
        Q.wait(act, f"sum{KD - 1}")
        A.own(act)
        A.did(act.activation(self.rstd[:].rearrange("p (a t) -> p a t", a=2), self.E[0][:, :, 0:NH], ACT.Sqrt,
                             bias=self.eps[:, 0:1], scale=1.0 / D), "root")

    def norm_pe(self, pe, A, Q):
        for c in range(KD):
            A.wait(pe, f"sq{c}")
            for half in range(2):
                mm = pe.matmul(self.E[0][:, half, 0:NH], self.ones[:], self.sq[c % 2][:, half * NH:(half + 1) * NH],
                               start=(c == 0), stop=(c == KD - 1))
            Q.did(mm, f"sum{c}")

    def h_act(self, act, A, V):
        for c in range(KD):
            V.wait(act, f"h{c}")
            A.did(act.activation(self.h_hi[:, c, :], self.hf[c % 2][:], ACT.Copy), f"hhi{c}")

    def h_dve(self, dve, A, V, vec):
        A.wait(dve, "root")
        V.did(dve.reciprocal(self.rstd[:], self.rstd[:]), "rstd")
        V.own(dve)

        def low(c):
            A.wait(dve, f"hhi{c}")
            V.did(dve.tensor_tensor(self.h_lo[:, c, :], self.hf[c % 2][:], self.h_hi[:, c, :].bitcast(F32),
                                    ALU.subtract), f"hlo{c}")
        for c in range(KD):
            if c >= 2:
                V.own(dve)
            V.did(dve.scalar_tensor_tensor(self.hf[c % 2][:], self.x[:, c, :], vec[:, c:c + 1], self.rstd[:],
                                           ALU.mult, ALU.mult), f"h{c}")
            if c >= 1:
                low(c - 1)
        low(KD - 1)

    def ffn(self, l, which):
        nc, io, ev = self.nc, self.io, self.evac
        tile = self.region(which, self.r0)
        self.norm_tiles(tile)
        a_hi, a_lo = tile("a_hi", [P, HF, NT], F32R), tile("a_lo", [P, HF, NT], F32R)
        gate, prod = tile("gate", [P, NT]), tile("prod", [P, NT])
        wg = io[which + "_w_gate"].rearrange("l (c p) n -> p (l c) n", p=P)
        wu = io[which + "_w_up"].rearrange("l (c p) n -> p (l c) n", p=P)
        wd = io[which + "_w_down"].rearrange("l (c p) n -> p (l c) n", p=P)
        v0 = VEC[which + "_norm"][0]
        vec = self.vec[:, v0:v0 + KD]
        A, V, Q = (self.steps(s, which + n) for s, n in
                   ((self.act_steps, "A"), (self.dve_steps, "V"), (self.pe_steps, "Q")))
        KS = (HF + 1) // 2
        PAIRS = HF + KD
        pair = [h * PAIRS for h in range(2)]
        used = [h * (HF + KD // 2) for h in range(2)]

        with nc.Block() as block:
            @block.gpsimd
            def _(pool):
                self.credits(pool)

            @block.sync
            def _(sp):
                for h in range(2):
                    with sp.Fori(0, HF) as f:
                        for s, w in enumerate((wg, wu)):
                            self.load_w(sp, f + pair[h], s, w[:, ds(l * KD, KD), ds((f + h * HF) * P, P)])
                    with sp.Fori(0, KD) as c:
                        for s, (a, n) in enumerate(((0, KS), (KS, HF - KS))):
                            self.load_w(sp, c + (pair[h] + HF), s, wd[:, ds(l * KF + (h * HF + a), n), ds(c * P, P)])

            @block.tensor
            def _(pe):
                self.norm_pe(pe, A, Q)
                V.wait(pe, f"hlo{KD - 1}")
                for h in range(2):
                    with pe.Fori(0, HF) as f:
                        for s in range(2):
                            self.products(pe, f + pair[h], s, self.h_hi, self.h_lo, self.D[s], (s, f + (used[h] + 1)))
                    pe.wait_ge(self.part_lo, (h + 1) * HF + 1)
                    with pe.Fori(0, KD // 2) as c:
                        for u in range(2):
                            k = c * 2 + (pair[h] + HF + u)
                            out, use = self.D[u], (u, c + (used[h] + HF + 1))
                            self.products(pe, k, 0, a_hi[:, 0:KS], a_lo[:, 0:KS], out, use, last=False)
                            self.products(pe, k, 1, a_hi[:, KS:HF], a_lo[:, KS:HF], out, first=False)

            @block.scalar
            def _(act):
                self.norm_act(act, A, V, Q)
                self.h_act(act, A, V)

                def silu_and_high(h):
                    def finish(f, j, _):
                        act.wait_ge(self.mm_done, f * 2 + (2 * pair[h] + 3))
                        act.wait_ge(ev[1], f + (used[h] + 1))
                        act.activation(gate[:].rearrange("p (a t) -> p a t", a=2), self.D[0][:, :, 0:NH], ACT.Silu)\
                           .then_inc(ev[0], 1)
                        act.wait_ge(ev[1], f + (used[h] + 2))
                        act.activation(a_hi[:, ds(f, 1), :].rearrange("p a t -> p (a t)"), prod[:], ACT.Copy)\
                           .then_inc(self.part_hi, 1)
                    return finish
                none = lambda i, j, c: None
                self.chase(act, lambda k: self.split_hi(act, k),
                           [(HF, 1, silu_and_high(0)), (KD, 2, none), (HF, 1, silu_and_high(1)), (KD, 2, none)])

            @block.vector
            def _(dve):
                self.h_dve(dve, A, V, vec)

                def times_up(h):
                    def finish(f, j, _):
                        dve.wait_ge(self.mm_done, f * 2 + (2 * pair[h] + 4))
                        dve.wait_ge(ev[0], f + (used[h] + 2))
                        dve.wait_ge(self.part_lo, f + (h * HF + 1))
                        dve.tensor_tensor(prod[:].rearrange("p (a t) -> p a t", a=2), self.D[1][:, :, 0:NH],
                                          gate[:].rearrange("p (a t) -> p a t", a=2), ALU.mult).then_inc(ev[1], 1)
                        dve.wait_ge(self.part_hi, f + (h * HF + 1))
                        dve.tensor_tensor(a_lo[:, ds(f, 1), :].rearrange("p a t -> p (a t)"), prod[:],
                                          a_hi[:, ds(f, 1), :].rearrange("p a t -> p (a t)").bitcast(F32),
                                          ALU.subtract).then_inc(self.part_lo, 1)
                    return finish

                def add_down(h):
                    def finish(c, u, _):
                        dve.wait_ge(self.mm_done, c * 2 + (2 * (pair[h] + HF) + 4))
                        xs = self.x[:, ds(c, 1), :].rearrange("p a (b t) -> p (a b) t", b=2)
                        dve.scalar_tensor_tensor(xs, self.D[u][:, :, 0:NH], 0.5, xs, ALU.mult, ALU.add)\
                           .then_inc(ev[u], 1)
                    return finish
                self.chase(dve, lambda k: self.split_lo(dve, k),
                           [(HF, 1, times_up(0)), (KD, 2, add_down(0)), (HF, 1, times_up(1)), (KD, 2, add_down(1))])

    def setup(self):
        nc, io, ev = self.nc, self.io, self.evac
        tile = self.region("setup", self.r0)
        rows = [tile(f"rows{l}", [P, P]) for l in range(L)]
        xt = tile("xt", [P, TP // P + 1, D])
        lam = tile("lam", [1, 4, L * 64])
        lprod = tile("lprod", [1, 2, L * 64])
        lsum, lexp, lrow = tile("lsum", [1, 2 * L]), tile("lexp", [1, 2 * L]), tile("lrow", [1, L])
        A, V, Q, G = self.stage_steps("setup")
        consts, vectors, tokens, lams = self.loads
        views = {n: io[n].rearrange({"conv_w": "l j (c p) -> (l j c) p", "r_k": "l (c h) k -> (l c) (h k)"}
                                    .get(n, "l (c p) -> (l c) p"), **({"h": 2} if n == "r_k" else {"p": P})) for n in VEC}

        with nc.Block() as block:
            @block.gpsimd
            def _(pool):
                pool.memset(self.ones[:], 1.0)
                pool.memset(self.eps[:, 0:1], 1e-6)
                pool.memset(self.eps[:, 1:2], 1e-5)
                G.own(pool)
                G.did(pool.memset(self.eps[:, 2:3], 64e-5), "ones")

            @block.sync
            def _(sp):
                for n, t in (("ident", self.ident), ("halves", self.halves), ("lam_init", self.lam_init)):
                    sp.dma_start(t[:], io[n]).then_inc(consts, 16)
                for l in range(L):
                    for n, (r, c) in VEC.items():
                        sp.dma_start(rows[l][r:r + c, :], views[n][l * c:(l + 1) * c, :]).then_inc(vectors, 16)
                sp.dma_start(rows[L - 1][NVEC:NVEC + KD, :], io["final_norm"].rearrange("(c p) -> c p", p=P))\
                  .then_inc(vectors, 16)
                sp.dma_start(xt[:, 0:TP // P, :], io["x_prompt"].rearrange("a (b p) d -> p (a b) d", p=P))\
                  .then_inc(tokens, 16)
                sp.dma_start(xt[0:NS, TP // P, :], io["x_sample"].rearrange("b s d -> (b s) d")).then_inc(tokens, 16)
                for i, n in enumerate(("lam_q1", "lam_k1", "lam_q2", "lam_k2")):
                    sp.dma_start(lam[0:1, i, :], io[n].rearrange("(a l) d -> a (l d)", a=1)).then_inc(lams, 16)
                sp.dma_start(self.pages[:], io["page_table"].rearrange("(a b) n -> a (b n)", a=1)).then_inc(lams, 16)

            @block.tensor
            def _(pe):
                pe.wait_ge(consts, 16 * 3)
                pe.wait_ge(vectors, 16 * (L * len(VEC) + 1))
                for l in range(L):
                    n = NVEC + (KD if l == L - 1 else 0)
                    Q.did(pe.transpose(self.E[l][:, 0, 0:n], rows[l][0:n, :], self.ident[0:n, 0:n]), f"vec{l}")
                G.wait(pe, "ones")
                V.wait(pe, "lam")
                Q.did(pe.matmul(self.E[0][:, 1, 0:L], self.ones[0:1, :], lrow[:], start=True, stop=True), "lam")
                pe.wait_ge(tokens, 32)
                for c in range(KD):
                    if c >= 2:
                        V.wait(pe, f"x{c - 2}")
                    for b in range(TP // P):
                        pe.transpose(self.D[c % 2][:, 0, b * P:(b + 1) * P], xt[:, b, c * P:(c + 1) * P], self.ident[:])
                    Q.did(pe.transpose(self.D[c % 2][:, 1, 0:NS], xt[0:NS, TP // P, c * P:(c + 1) * P],
                                       self.ident[0:NS, 0:NS]), f"x{c}")

            @block.scalar
            def _(act):
                V.wait(act, "dots")
                A.own(act)
                A.did(act.activation(lexp[:], lsum[:], ACT.Exp), "exp")
                for l in range(L):
                    n = NVEC + (KD if l == L - 1 else 0)
                    Q.wait(act, f"vec{l}")
                    A.own(act)
                    A.did(act.activation(self.vec_all[:, l, 0:n], self.E[l][:, 0, 0:n], ACT.Copy), f"vec{l}")

            @block.vector
            def _(dve):
                dve.wait_ge(lams, 16 * 5)
                lv = lam[:].rearrange("a (i j) n -> a i j n", j=2)
                V.own(dve)
                V.did(dve.tensor_tensor(lprod[:], lv[:, :, 0, :], lv[:, :, 1, :], ALU.mult), "prods")
                V.own(dve)
                V.did(dve.tensor_reduce(lsum[:], lprod[:].rearrange("a i (l d) -> a (i l) d", l=L), AX.X, ALU.add), "dots")
                A.wait(dve, "exp")
                dve.wait_ge(consts, 16 * 3)
                V.own(dve)
                V.did(dve.tensor_tensor(lrow[:], lexp[:, L:2 * L], lexp[:, 0:L], ALU.subtract), "diff")
                V.own(dve)
                V.did(dve.tensor_tensor(lrow[:], lrow[:], self.lam_init[0:1, 0:L], ALU.subtract), "lam")
                Q.wait(dve, "lam")
                A.wait(dve, "vec0")
                V.own(dve)
                V.did(dve.tensor_copy(self.neg_lam[:], self.E[0][:, 1, 0:L]), "neg_lam")
                for c in range(KD):
                    Q.wait(dve, f"x{c}")
                    dve.tensor_copy(self.x[:, c, 0:TP], self.D[c % 2][:, 0, :])
                    V.own(dve)
                    V.did(dve.tensor_copy(self.x[:, c, TP:NT], self.D[c % 2][:, 1, 0:NS]), f"x{c}")

    def stage_steps(self, stage, turns=False):
        kinds = (self.act_turns, self.dve_turns, self.pe_turns, self.pool_turns) if turns else \
                (self.act_steps, self.dve_steps, self.pe_steps, self.pool_steps)
        return [self.steps(s, stage + n + "t" * turns) for s, n in zip(kinds, "AVQG")]

    def layer_vectors(self, l):
        A, V, Q, G = self.stage_steps("vectors")
        with self.nc.Block() as block:
            @block.vector
            def _(dve):
                dve.tensor_copy(self.vec[:], self.vec_all[:, ds(l, 1), 0:NVEC].rearrange("p a n -> p (a n)"))
                dve.tensor_copy(self.nlam[:], self.neg_lam[:, ds(l, 1)])
                V.own(dve)
                V.did(dve.tensor_copy(self.one_li[:], self.lam_init[:, ds(l + L, 1)]), "all")

    def project(self, l, name, runs, dest, norm):
        nc, io, ev = self.nc, self.io, self.evac
        A, V, Q, G = self.stage_steps(name)
        win = io["w_in"].rearrange("l (c p) n -> p (l c) n", p=P)
        pairs = sum(n for _, n in runs) // 2
        v0 = VEC["mix_norm"][0]

        with nc.Block() as block:
            @block.gpsimd
            def _(pool):
                self.credits(pool)

            @block.sync
            def _(sp):
                k0 = 0
                for first, count in runs:
                    with sp.Fori(0, count // 2) as k:
                        for s in range(2):
                            self.load_w(sp, k + k0, s, win[:, ds(l * KD, KD), ds((k * 2 + (first + s)) * P, P)])
                    k0 += count // 2

            @block.tensor
            def _(pe):
                if norm:
                    self.norm_pe(pe, A, Q)
                    V.wait(pe, f"hlo{KD - 1}")
                with pe.Fori(0, pairs) as k:
                    for s in range(2):
                        self.products(pe, k, s, self.h_hi, self.h_lo, self.D[s], (s, k + 1))

            @block.scalar
            def _(act):
                if norm:
                    self.norm_act(act, A, V, Q)
                    self.h_act(act, A, V)

                def copy_even(k, j, _):
                    act.wait_ge(self.mm_done, k * 2 + 3)
                    act.activation(dest[:, ds(k * 2, 1), :].rearrange("p a (b t) -> p (a b) t", b=2),
                                   self.D[0][:, :, 0:NH], ACT.Copy).then_inc(ev[0], 1)
                self.chase(act, lambda k: self.split_hi(act, k), [(pairs, 1, copy_even)])

            @block.vector
            def _(dve):
                if norm:
                    self.h_dve(dve, A, V, self.vec[:, v0:v0 + KD])

                def copy_odd(k, j, _):
                    dve.wait_ge(self.mm_done, k * 2 + 4)
                    dve.tensor_copy(dest[:, ds(k * 2 + 1, 1), :].rearrange("p a (b t) -> p (a b) t", b=2),
                                    self.D[1][:, :, 0:NH]).then_inc(ev[1], 1)
                self.chase(dve, lambda k: self.split_lo(dve, k), [(pairs, 1, copy_odd)])

    def prompt_attention(self, l, proj, y, vtok, tile):
        nc, io = self.nc, self.io
        A, V, Q, G = self.stage_steps("prompt")
        At, Vt, Qt, Gt = self.stage_steps("prompt", True)
        alibi = tile("alibi", [P, HC, TP])
        ring = self.region("prompt_ring", self.ring)
        ktok = ring("ktok", [P, TP // P + 1, DB])
        S = [tile(f"S{i}", [P, 2, TP]) for i in range(2)]
        qm = tile("qm", [P, 2, TP])
        kh = tile("kh", [P, TP])
        vh = tile("vh", [P, TP // P, P])
        attn_t = tile("attn_t", [P, TP])
        mx, ex, ri = tile("mx", [P, 4]), tile("ex", [P, 2]), tile("ri", [P, 2])
        rows_in = ring("rows_in", [NB * 2, DB])
        state = ring("state", [P, CB, NB * 2])
        ext = ring("ext", [P, 2 + TP])
        ext_s = ring("ext_s", [P, NB, 2 + TS])
        tmp, tmp2 = ring("tmp", [P, NT]), ring("tmp2", [P, NT])
        last = ring("last", [P, CB, 2 + NB * 2])
        rows_out = ring("rows_out", [2 + NB * 2, DB])
        tables, states = self.loads[0:2]
        kv_out, conv_out = self.stores
        nblk = TP // P + 1
        cw = VEC["conv_w"][0]
        kv = [(b, w) for b in range(nblk) for w in range(2)]
        slot = lambda n: self.E[n % 4 // 2][:, n % 2, :]

        def evac_kv(eng, w):
            for n, (b, w_) in enumerate(kv):
                if w_ != w:
                    continue
                m = P if b < nblk - 1 else NS
                Q.wait(eng, f"kv{n}")
                dst = (ktok, vtok)[w][0:m, b, :]
                if w == 0:
                    A.own(eng)
                    A.did(eng.activation(dst, slot(n)[0:m, :], ACT.Copy), f"kv{n}")
                else:
                    V.own(eng)
                    V.did(eng.tensor_copy(dst, slot(n)[0:m, :]), f"kv{n}")

        with nc.Block() as block:
            @block.sync
            def _(sp):
                sp.dma_start(rows_in[:], io["state_conv"].rearrange("l b j n -> (l b j) n")[ds(l * (2 * NB), 2 * NB), :])\
                  .then_inc(states, 16)
                sp.dma_start(alibi[:].rearrange("p h t -> p (h t)"), io["alibi_prompt"]).then_inc(tables, 16)
                for eng, led, t, out in ((None, A, ktok, "k"), (None, V, vtok, "v")):
                    w = 0 if t is ktok else 1
                    led.wait(sp, f"kv{2 * (nblk - 1) + w}")
                    sp.dma_start(io[f"{out}_prompt"].rearrange("l a (b p) h d -> p (l a b) (h d)", p=P)
                                 [:, ds(l * (nblk - 1), nblk - 1), :], t[:, 0:nblk - 1, :]).then_inc(kv_out, 16)
                    sp.dma_start(io[f"{out}_sample"].rearrange("l b s h d -> (l b s) (h d)")[ds(l * NS, NS), :],
                                 t[0:NS, nblk - 1, :]).then_inc(kv_out, 16)
                A.wait(sp, "conv_rows")
                sp.dma_start(io["conv_prompt"].rearrange("l a j n -> (l a j) n")[ds(l * 2, 2), :], rows_out[0:2, :])\
                  .then_inc(conv_out, 16)
                sp.dma_start(io["conv_sample"].rearrange("l b j n -> (l b j) n")[ds(l * (2 * NB), 2 * NB), :],
                             rows_out[2:2 + 2 * NB, :]).then_inc(conv_out, 16)
                sp.wait_ge(kv_out, 64)
                sp.wait_ge(conv_out, 32)

            @block.tensor
            def _(pe):
                for n, (b, w) in enumerate(kv):
                    m = P if b < nblk - 1 else NS
                    if n >= 4:
                        (A, V)[w].wait(pe, f"kv{n - 4}")
                    for c in range(CB):
                        tr = pe.transpose(slot(n)[0:m, c * P:(c + 1) * P],
                                          proj[:, 16 + 4 * w + c, b * P:b * P + m], self.ident[:])
                    Q.did(tr, f"kv{n}")
                pe.wait_ge(states, 16)
                for c in range(CB):
                    tr = pe.transpose(self.D[0][:, 0, c * 16:(c + 1) * 16], rows_in[:, c * P:(c + 1) * P],
                                      self.ident[0:16, 0:16])
                Q.did(tr, "state")
                V.wait(pe, f"kv{len(kv) - 1}")
                A.wait(pe, "state")
                with pe.Fori(0, HC) as h:
                    Qt.loop(h)
                    for i in range(TP // P):
                        nk = (i + 1) * P
                        if i == 0:
                            Gt.wait(pe, "staged", h)
                        if i >= 2:
                            Vt.wait(pe, f"scaled{i - 2}", h)
                        else:
                            Vt.wait(pe, f"scaled{i + 2}", h - 1)
                        for m in range(2):
                            mm = pe.matmul(self.E[i % 2][:, m, 0:nk], qm[:, m, i * P:(i + 1) * P], kh[:, 0:nk],
                                           start=True, stop=True)
                        Qt.did(mm, f"scores{i}")
                        Vt.wait(pe, f"attn{i}", h)
                        if i >= 1:
                            At.wait(pe, f"turned{i - 1}", h)
                        for b in range(i + 1):
                            tr = pe.transpose(self.D[0][:, 0, b * P:(b + 1) * P], S[i % 2][:, 0, b * P:(b + 1) * P],
                                              self.ident[:])
                        Qt.did(tr, f"turn{i}")
                        At.wait(pe, f"turned{i}", h)
                        if i >= 1:
                            At.wait(pe, f"out{i - 1}", h)
                        else:
                            At.wait(pe, f"out{TP // P - 1}", h - 1)
                        for b in range(i + 1):
                            mm = pe.matmul(self.D[1][:, 0, 0:P], vh[:, b, :], attn_t[:, b * P:(b + 1) * P],
                                           start=(b == 0), stop=(b == i))
                        Qt.did(mm, f"pv{i}")
                Qt.end(HC)
                Gt.wait(pe, "conv", HC - 1)
                for c in range(CB):
                    tr = pe.transpose(self.D[0][0:18, 1, c * P:(c + 1) * P], last[:, c, :], self.ident[:])
                Q.did(tr, "conv_rows")

            @block.scalar
            def _(act):
                evac_kv(act, 0)
                Q.wait(act, "state")
                A.own(act)
                A.did(act.activation(state[:].rearrange("p c n -> p (c n)"), self.D[0][:, 0, 0:CB * 16], ACT.Copy), "state")
                with act.Fori(0, HC) as h:
                    At.loop(h)
                    for i in range(TP // P):
                        nk = (i + 1) * P
                        Vt.wait(act, f"negmax{i}", h)
                        At.own(act)
                        for m in range(2):
                            e = act.activation(S[i % 2][:, m, 0:nk], S[i % 2][:, m, 0:nk], ACT.Exp, bias=mx[:, 2 + m:3 + m],
                                               scale=1.0, accum_out=ex[:, m:m + 1])
                        At.did(e, f"exp{i}")
                        Qt.wait(act, f"turn{i}", h)
                        At.own(act)
                        At.did(act.activation(attn_t[:, 0:nk], self.D[0][:, 0, 0:nk], ACT.Copy), f"turned{i}")
                        Qt.wait(act, f"pv{i}", h)
                        At.own(act)
                        At.did(act.activation(y[:, ds(h + 8, 1), i * P:(i + 1) * P].rearrange("p a t -> p (a t)"),
                                              self.D[1][:, 0, 0:P], ACT.Copy), f"out{i}")
                At.end(HC)
                Q.wait(act, "conv_rows")
                A.own(act)
                A.did(act.activation(rows_out[:], self.D[0][0:18, 1, :], ACT.Copy), "conv_rows")

            @block.vector
            def _(dve):
                evac_kv(dve, 1)
                dve.wait_ge(self.loads[0], 16)
                with dve.Fori(0, HC) as h:
                    Vt.loop(h)
                    for i in range(TP // P):
                        nk = (i + 1) * P
                        s = S[i % 2]
                        Qt.wait(dve, f"scores{i}", h)
                        if i >= 2:
                            Qt.wait(dve, f"turn{i - 2}", h)
                        else:
                            Qt.wait(dve, f"turn{i + 2}", h - 1)
                        bias = alibi[:, ds(h, 1), TP - nk:TP].to_broadcast([P, 2, nk])
                        Vt.own(dve)
                        Vt.did(dve.scalar_tensor_tensor(s[:, :, 0:nk], self.E[i % 2][:, :, 0:nk], 0.125, bias,
                                                        ALU.mult, ALU.add), f"scaled{i}")
                        Vt.own(dve)
                        if i >= 1:
                            At.wait(dve, f"exp{i - 1}", h)
                        else:
                            At.wait(dve, "exp3", h - 1)
                        Vt.own(dve)
                        Vt.did(dve.tensor_reduce(mx[:, 0:2], s[:, :, 0:nk], AX.X, ALU.max))
                        Vt.own(dve)
                        Vt.did(dve.tensor_scalar(mx[:, 2:4], mx[:, 0:2], -1.0, None, ALU.mult), f"negmax{i}")
                        At.wait(dve, f"exp{i}", h)
                        Vt.own(dve)
                        Vt.did(dve.reciprocal(ri[:], ex[:]))
                        Vt.own(dve)
                        Vt.did(dve.tensor_scalar(ri[:, 1:2], ri[:, 1:2], self.nlam[:], None, ALU.mult))
                        Vt.own(dve)
                        Vt.did(dve.tensor_scalar(s[:, 0, 0:nk], s[:, 0, 0:nk], ri[:, 0:1], None, ALU.mult))
                        Vt.own(dve)
                        Vt.did(dve.scalar_tensor_tensor(s[:, 0, 0:nk], s[:, 1, 0:nk], ri[:, 1:2], s[:, 0, 0:nk],
                                                        ALU.mult, ALU.add), f"attn{i}")
                Vt.end(HC)

            @block.gpsimd
            def _(pool):
                self.credits(pool, (At, Vt, Qt, Gt))
                G.own(pool)
                G.did(pool.memset(qm[:], 0.0))
                G.own(pool)
                G.did(pool.memset(ext[:, 0:2], 0.0), "zero")
                G.own(pool)
                A.wait(pool, "state")
                V.wait(pool, f"kv{len(kv) - 1}")
                for h in range(HC):
                    Gt.loop(h)
                    Qt.wait(pool, f"pv{TP // P - 1}", h - 1)
                    flat = lambda j, t=slice(0, TP), r=slice(0, P): proj[r, ds(h + j, 1), t].rearrange("p a t -> p (a t)")
                    Gt.own(pool)
                    Gt.did(pool.tensor_copy(qm[0:64, 0, :], flat(12, r=slice(0, 64))))
                    Gt.own(pool)
                    Gt.did(pool.tensor_copy(qm[64:128, 1, :], flat(12, r=slice(64, 128))))
                    Gt.own(pool)
                    Gt.did(pool.tensor_copy(kh[:], flat(16)))
                    Gt.own(pool)
                    Gt.did(pool.tensor_copy(vh[:], vtok[:, 0:TP // P, ds(h * P, P)]), "staged")
                    xs = lambda j: flat(j, slice(TP, NT)).rearrange("p (b s) -> p b s", b=NB)
                    Gt.own(pool)
                    Gt.did(pool.tensor_copy(ext_s[:, :, 0:2], state[:, ds(h, 1), :].rearrange("p a (b j) -> p (a b) j", b=NB)))
                    Gt.own(pool)
                    Gt.did(pool.tensor_tensor(ext[:, 2:], flat(8), flat(0), ALU.mult))
                    Gt.own(pool)
                    Gt.did(pool.tensor_tensor(ext_s[:, :, 2:], xs(8), xs(0), ALU.mult))
                    Gt.own(pool)
                    ty, tys = tmp[:, 0:TP], tmp[:, TP:NT].rearrange("p (b s) -> p b s", b=NB)
                    for j in range(3):
                        wj = self.vec[:, ds(h + (cw + CB * j), 1)]
                        o, os = (ty, tys) if j == 0 else (tmp2[:, 0:TP], tmp2[:, TP:NT].rearrange("p (b s) -> p b s", b=NB))
                        Gt.own(pool)
                        Gt.did(pool.tensor_scalar(o, ext[:, j:j + TP], wj, None, ALU.mult))
                        Gt.own(pool)
                        Gt.did(pool.tensor_scalar(os, ext_s[:, :, j:j + TS], wj, None, ALU.mult))
                        Gt.own(pool)
                        if j:
                            Gt.own(pool)
                            Gt.did(pool.tensor_tensor(tmp[:], tmp[:], tmp2[:], ALU.add))
                            Gt.own(pool)
                    Gt.own(pool)
                    Gt.did(pool.tensor_tensor(y[:, ds(h, 1), :].rearrange("p a t -> p (a t)"), tmp[:], flat(4, slice(0, NT)), ALU.mult))
                    Gt.own(pool)
                    Gt.did(pool.tensor_copy(last[:, ds(h, 1), 0:2].rearrange("p a j -> p (a j)"), ext[:, TP:TP + 2]))
                    Gt.own(pool)
                    Gt.did(pool.tensor_copy(last[:, ds(h, 1), 2:18].rearrange("p a (b j) -> p (a b) j", b=NB),
                                            ext_s[:, :, TS:TS + 2]), "conv")
                    Gt.own(pool)
                    Gt.did(pool.memset(self.junk[:, 15:16], 0.0))
                Gt.end(HC)

    def sample_attention(self, l, proj, y, vtok, tile):
        nc, io = self.nc, self.io
        A, V, Q, G = self.stage_steps("sample")
        At, Vt, Qt, Gt = self.stage_steps("sample", True)
        ring = self.region("sample_ring", self.ring)
        over = self.region("sample_over", self.r0 + 4 * 12 * NT)
        vp = ring("vp", [P, NPG, DB])
        kp = over("kp", [P, NPG, DB])
        kt = tile("kt", [P, CB, PAST])
        past, new = tile("past", [64, PAST]), tile("new", [64, NB, NS])
        S = tile("S", [64, PAST + NS])
        qs = tile("qs", [P, 80 * CB])
        comb = tile("comb", [64, 2, HC * TS])
        e0, e1 = tile("e0", [64, HC * TS]), tile("e1", [64, HC * TS])
        mx, ex = tile("mx", [64, 2]), tile("ex", [64, 2])
        at = ring("at", [P, (NPG + 1) * HC * TS])
        sq, rstd = ring("sq", [P, NT]), ring("rstd", [P, NT])
        tables, kload, vload = self.loads[0:3]
        n_at = HC * TS

        with nc.Block() as block:
            @block.sync
            def _(sp):
                sp.dma_start(past[:], io["alibi_past"][0:64, :]).then_inc(tables, 16)
                sp.dma_start(new[:].rearrange("p b k -> p (b k)"), io["alibi_new"][0:64, :]).then_inc(tables, 16)
                sp.dma_start(comb[:].rearrange("p b k -> p (b k)"), io["combine"][0:64, :]).then_inc(tables, 16)
                with sp.Fori(0, NB) as b:
                    ck = io["cache_k"].rearrange("l g t m d -> t (l g) (m d)")
                    cv = io["cache_v"].rearrange("l g t m d -> t (l g) (m d)")
                    pool_n = io["cache_k"].shape[1]
                    pg = [sp.value_load(self.pages[0:1, ds(b * NPG + j, 1)], min_val=0, max_val=pool_n - 1)
                          for j in range(NPG)]
                    for j in range(NPG):
                        if j == 0:
                            Qt.wait(sp, "kturn7", b - 1)
                        sp.dma_start(kp[:, j:j + 1, :], ck[:, ds(l * pool_n + pg[j], 1), :]).then_inc(kload, 16)
                    for j in range(NPG):
                        if j == 0:
                            Qt.wait(sp, "pv", b - 1)
                        sp.dma_start(vp[:, j:j + 1, :], cv[:, ds(l * pool_n + pg[j], 1), :]).then_inc(vload, 16)

            @block.gpsimd
            def _(pool):
                self.credits(pool, (At, Vt, Qt, Gt))
                G.own(pool)
                G.did(pool.memset(qs[:], 0.0), "zero")
                G.own(pool)
                qv = qs[:].rearrange("p (c x) -> p c x", c=CB)
                with pool.Fori(0, NB) as b:
                    Gt.loop(b)
                    Qt.wait(pool, "scores", b - 1)
                    for hf in range(2):
                        r = slice(64 * hf, 64 * hf + 64)
                        Gt.own(pool)
                        Gt.did(pool.tensor_copy(qv[r, :, hf * TS:hf * TS + TS], proj[r, 12:16, ds(b * TS + TP, TS)]),
                               "q" if hf else None)
                Gt.end(NB)

            @block.tensor
            def _(pe):
                with pe.Fori(0, NB) as b:
                    Qt.loop(b)
                    for n in range(2 * CB):
                        hf, c = divmod(n, CB)
                        if n == 0:
                            pe.wait_ge(kload, b * (16 * NPG) + 16 * NPG)
                        eng = (At, Vt)[n % 2]
                        if n >= 2:
                            eng.wait(pe, f"kt{n - 2}", b)
                        else:
                            eng.wait(pe, f"kt{n + 6}", b - 1)
                        for j in range(4):
                            tr = pe.transpose(self.E[n % 2][:, 0, j * P:(j + 1) * P],
                                              kp[:, hf * 4 + j, c * P:(c + 1) * P], self.ident[:])
                        Qt.did(tr, f"kturn{n}")
                    Gt.wait(pe, "q", b)
                    At.wait(pe, "kt6", b)
                    Vt.wait(pe, "kt7", b)
                    Vt.wait(pe, "scaled", b - 1)
                    for hf in range(2):
                        for c in range(CB):
                            pe.matmul(self.D[0][0:64, hf, :], qs[:, c * 64:(c + 1) * 64], kt[:, c, hf * 512:(hf + 1) * 512],
                                      start=(c == 0), stop=(c == CB - 1))
                    for c in range(CB):
                        mm = pe.matmul(self.D[1][0:64, 0, 0:NS], qs[:, c * 64:(c + 1) * 64], proj[:, 16 + c, TP:NT],
                                       start=(c == 0), stop=(c == CB - 1))
                    Qt.did(mm, "scores")
                    Vt.wait(pe, "weights", b)
                    At.wait(pe, "turned", b - 1)
                    for j in range(NPG + 1):
                        m = P if j < NPG else NS
                        mm = pe.matmul(self.E[0][0:m, 1, j * n_at:(j + 1) * n_at], S[:, j * P:j * P + m], e1[:],
                                       start=True, stop=True)
                    Qt.did(mm, "turn")
                    At.wait(pe, "turned", b)
                    pe.wait_ge(vload, b * (16 * NPG) + 16 * NPG)
                    At.wait(pe, "out", b - 1)
                    for h in range(HC):
                        for j in range(NPG + 1):
                            m = P if j < NPG else NS
                            v = vp[:, j, h * P:(h + 1) * P] if j < NPG else vtok[0:NS, TP // P, h * P:(h + 1) * P]
                            mm = pe.matmul(self.E[1][:, 1, h * TS:(h + 1) * TS], v,
                                           at[0:m, j * n_at + h * TS:j * n_at + (h + 1) * TS],
                                           start=(j == 0), stop=(j == NPG))
                    Qt.did(mm, "pv")
                Qt.end(NB)
                At.wait(pe, "out", NB - 1)
                for h in range(HC):
                    A.wait(pe, f"sq{h}")
                    for half in range(2):
                        mm = pe.matmul(self.D[h % 2][:, half, 0:NH], self.ones[:], sq[:, half * NH:(half + 1) * NH],
                                       start=True, stop=True)
                    Q.did(mm, f"sum{h}")

            @block.scalar
            def _(act):
                with act.Fori(0, NB) as b:
                    At.loop(b)
                    for n in range(0, 2 * CB, 2):
                        hf, c = divmod(n, CB)
                        Qt.wait(act, f"kturn{n}", b)
                        if n == 0:
                            Qt.wait(act, "scores", b - 1)
                        At.own(act)
                        At.did(act.activation(kt[:, c, hf * 512:(hf + 1) * 512], self.E[0][:, 0, :], ACT.Copy), f"kt{n}")
                    Vt.wait(act, "negmax", b)
                    At.own(act)
                    At.did(act.activation(S[:], S[:], ACT.Exp, bias=mx[:, 1:2], scale=1.0, accum_out=ex[:, 0:1]), "exp")
                    Qt.wait(act, "turn", b)
                    act.activation(at[:, 0:NPG * n_at], self.E[0][:, 1, 0:NPG * n_at], ACT.Copy)
                    At.own(act)
                    At.did(act.activation(at[0:NS, NPG * n_at:], self.E[0][0:NS, 1, NPG * n_at:(NPG + 1) * n_at], ACT.Copy),
                           "turned")
                    Qt.wait(act, "pv", b)
                    At.own(act)
                    At.did(act.activation(y[:, 8:12, ds(b * TS + TP, TS)],
                                          self.E[1][:, 1, 0:HC * TS].rearrange("p (h s) -> p h s", h=HC), ACT.Copy), "out")
                At.end(NB)
                At.own(act)
                for h in range(HC):
                    if h:
                        V.wait(act, f"y{h - 1}")
                    A.own(act)
                    A.did(act.activation(sq[:], y[:, 8 + h, :], ACT.Square), f"sq{h}")
                    Q.wait(act, f"sum{h}")
                    A.own(act)
                    A.did(act.activation(rstd[:].rearrange("p (a t) -> p a t", a=2), self.D[h % 2][:, :, 0:NH], ACT.Sqrt,
                                         bias=self.eps[:, 1:2], scale=1.0 / P), f"root{h}")

            @block.vector
            def _(dve):
                dve.wait_ge(tables, 48)
                V.own(dve)
                V.did(dve.scalar_tensor_tensor(e0[:], comb[:, 1, :], self.nlam[0:64, :], comb[:, 0, :], ALU.mult, ALU.add))
                with dve.Fori(0, NB) as b:
                    Vt.loop(b)
                    for n in range(1, 2 * CB, 2):
                        hf, c = divmod(n, CB)
                        Qt.wait(dve, f"kturn{n}", b)
                        if n == 1:
                            Qt.wait(dve, "scores", b - 1)
                        Vt.own(dve)
                        Vt.did(dve.tensor_copy(kt[:, c, hf * 512:(hf + 1) * 512], self.E[1][:, 0, :]), f"kt{n}")
                    Qt.wait(dve, "scores", b)
                    Qt.wait(dve, "turn", b - 1)
                    dve.scalar_tensor_tensor(S[:, 0:PAST].rearrange("p (a k) -> p a k", a=2), self.D[0][0:64, :, :], 0.125,
                                             past[:].rearrange("p (a k) -> p a k", a=2), ALU.mult, ALU.add)
                    Vt.own(dve)
                    Vt.did(dve.scalar_tensor_tensor(S[:, PAST:], self.D[1][0:64, 0, 0:NS], 0.125,
                                                    new[:, ds(b, 1), :].rearrange("p a k -> p (a k)"), ALU.mult, ALU.add),
                           "scaled")
                    Vt.own(dve)
                    Vt.did(dve.tensor_reduce(mx[:, 0:1], S[:], AX.X, ALU.max))
                    Vt.own(dve)
                    Vt.did(dve.tensor_scalar(mx[:, 1:2], mx[:, 0:1], -1.0, None, ALU.mult), "negmax")
                    At.wait(dve, "exp", b)
                    Vt.own(dve)
                    Vt.did(dve.reciprocal(ex[:, 1:2], ex[:, 0:1]))
                    Vt.own(dve)
                    Vt.did(dve.tensor_scalar(e1[:], e0[:], ex[:, 1:2], None, ALU.mult), "weights")
                Vt.end(NB)
                for h in range(HC):
                    yh = y[:, 8 + h, :]
                    A.wait(dve, f"root{h}")
                    V.own(dve)
                    V.did(dve.reciprocal(rstd[:], rstd[:]))
                    V.own(dve)
                    V.did(dve.tensor_tensor(rstd[:], rstd[:], yh, ALU.mult))
                    V.own(dve)
                    sw = VEC["subln_w"][0]
                    V.own(dve)
                    V.did(dve.tensor_scalar(yh, rstd[:], self.vec[:, sw:sw + 1], self.one_li[:], ALU.mult, ALU.mult), f"y{h}")

    def token_shift(self, l, z):
        nc, io = self.nc, self.io
        A, V, Q, G = self.stage_steps("shift")
        At, Vt, Qt, Gt = self.stage_steps("shift", True)
        ring = self.region("shift", self.ring)
        rows_in, state = ring("rows_in", [NB, NSHIFT]), ring("state", [P, CZ, NB])
        last, rows_out = ring("last", [P, CZ, 1 + NB]), ring("rows_out", [1 + NB, NSHIFT])
        diff = ring("diff", [P, NT])
        mu0 = VEC["tm_mu"][0]
        banks = [self.E[1][:, 0, :], self.E[1][:, 1, :], self.D[0][:, 0, :], self.D[0][:, 1, :]]

        with nc.Block() as block:
            @block.sync
            def _(sp):
                sp.dma_start(rows_in[:], io["state_shift"].rearrange("l b n -> (l b) n")[ds(l * NB, NB), :])\
                  .then_inc(self.loads[0], 16)
                A.wait(sp, "rows")
                sp.dma_start(io["shift_prompt"].rearrange("l b n -> (l b) n")[ds(l, 1), :], rows_out[0:1, :])\
                  .then_inc(self.stores[0], 16)
                sp.dma_start(io["shift_sample"].rearrange("l b n -> (l b) n")[ds(l * NB, NB), :], rows_out[1:1 + NB, :])\
                  .then_inc(self.stores[0], 16)
                sp.wait_ge(self.stores[0], 32)

            @block.gpsimd
            def _(pool):
                self.credits(pool, (Vt,))
                G.own(pool)
                G.did(pool.tensor_copy(last[:, :, 0:1], z[:, :, TP - 1:TP]))
                G.own(pool)
                G.did(pool.tensor_copy(last[:, :, 1:], z[:, :, TP + TS - 1:NT:TS]), "last")

            @block.tensor
            def _(pe):
                pe.wait_ge(self.loads[0], 16)
                for c in range(CZ):
                    tr = pe.transpose(self.E[0][:, 0, c * NB:(c + 1) * NB], rows_in[:, c * P:(c + 1) * P],
                                      self.ident[0:NB, 0:NB])
                Q.did(tr, "state")
                G.wait(pe, "last")
                for c in range(CZ):
                    tr = pe.transpose(banks[c // 4][0:1 + NB, c % 4 * P:(c % 4 + 1) * P], last[:, c, :], self.ident[:])
                Q.did(tr, "rows")

            @block.scalar
            def _(act):
                Q.wait(act, "state")
                A.own(act)
                A.did(act.activation(state[:].rearrange("p c b -> p (c b)"), self.E[0][:, 0, 0:CZ * NB], ACT.Copy), "state")
                Q.wait(act, "rows")
                for i, bank in enumerate(banks):
                    n = min(512, NSHIFT - i * 512)
                    a = act.activation(rows_out[:, i * 512:i * 512 + n], bank[0:1 + NB, 0:n], ACT.Copy)
                A.did(a, "rows")
                Vt.wait(act, "mixed", CZ - 1)
                act.activation(z[0:64, 3 * CB, :], z[0:64, 3 * CB, :], ACT.Tanh)
                A.own(act)
                A.did(act.activation(z[:, 3 * CB + 1, :], z[:, 3 * CB + 1, :], ACT.Sigmoid), "low")

            @block.vector
            def _(dve):
                A.wait(dve, "state")
                G.wait(dve, "last")
                with dve.Fori(0, CZ) as c:
                    Vt.loop(c)
                    zc = z[:, ds(c, 1), :].rearrange("p a t -> p (a t)")
                    zs, dsm = (t[:, TP:NT].rearrange("p (b s) -> p b s", b=NB) for t in (zc, diff))
                    Vt.own(dve)
                    dve.tensor_tensor(diff[:, 1:TP], zc[:, 0:TP - 1], zc[:, 1:TP], ALU.subtract)
                    dve.tensor_scalar(diff[:, 0:1], zc[:, 0:1], -1.0, None, ALU.mult)
                    dve.tensor_tensor(dsm[:, :, 1:TS], zs[:, :, 0:TS - 1], zs[:, :, 1:TS], ALU.subtract)
                    Vt.own(dve)
                    Vt.did(dve.tensor_tensor(dsm[:, :, 0:1], state[:, ds(c, 1), :].rearrange("p a (b o) -> p (a b) o", o=1),
                                             zs[:, :, 0:1], ALU.subtract))
                    Vt.own(dve)
                    Vt.did(dve.scalar_tensor_tensor(zc, diff[:], self.vec[:, ds(c + mu0, 1)], zc, ALU.mult, ALU.add), "mixed")
                Vt.end(CZ)

    def recurrence(self, l, z, y, tile):
        nc, io = self.nc, self.io
        A, V, Q, G = self.stage_steps("rwkv")
        At, Vt, Qt, Gt = self.stage_steps("rwkv", True)
        E, D = self.E, self.D
        ring = self.region("rwkv_ring", self.ring)
        NG, GW = 3, 3
        temps = tile.at[0]
        kk, kp, a, lw, cum, pinv, pprev, tmp = (tile(n, [P, NT]) for n in
                                                ("kk", "kp", "a", "lw", "cum", "pinv", "pprev", "tmp"))
        over = self.region("rwkv_over", temps)
        T, TT, W1, Lm = (over(n, [P, NW, P]) for n in ("T", "TT", "W1", "Lm"))
        assert over.at[0] <= tile.at[0]
        AR = tile("AR", [P, NW, P + W])
        Bb, Kb, Vb = (tile(n, [P, NW, P]) for n in ("Bb", "Kb", "Vb"))
        GM = tile("GM", [P, NW, 2, P + W])
        TM = ring("TM", [P, NW, 3, P])
        gg, bonus = tile("gg", [P, NT]), tile("bonus", [P, NT])
        pin, yt = tile("pin", [P, NT]), tile("yt", [P, NT])
        sq = ring("sq", [P, NT])
        carry = ring("carry", [P, NT])
        lev = ring("lev", [P, 6, P])
        gmask = ring("gmask", [P, 2, P + W])
        bmask = ring("bmask", [P, NB])
        wa, gup = tile("wa", [P, 2, P]), tile("gup", [P, P])
        S = [tile(f"S{i}", [P, P]) for i in range(2)]
        SP, Xs, Us, so = (tile(n, [P, P]) for n in ("SP", "Xs", "Us", "so"))
        omka = tile("omka", [P, CB])
        low, glow = z[:, 3 * CB, :], z[:, 3 * CB + 1, :]
        tables, wload, sload = self.loads[0:3]
        store = self.stores[0]
        two = lambda t: t.rearrange("p (a t) -> p a t", a=2)
        win = lambda t, r=slice(0, P): t[r, :].rearrange("p (w s) -> p w s", w=NW)
        cmul = -math.exp(-0.5)
        tok_bank = lambda w: D[w % 2][:, 0, 0:3 * P]
        gram_bank = lambda w: E[w % 2][:, 0, 0:2 * (P + W)]
        grp = lambda g: slice(g * GW, (g + 1) * GW)
        inv_bank = lambda g: (E[0][:, 1, 0:GW * P], E[1][:, 1, 0:GW * P], D[0][:, 1, 0:GW * P])[g]
        blocks = lambda t: t.rearrange("p (i n) -> p i n", n=P)

        with nc.Block() as block:
            @block.sync
            def _(sp):
                for n, t in (("carry", carry[:]), ("batch_mask", bmask[:]), ("level_mask", lev[:].rearrange("p j n -> p (j n)")),
                             ("gram_mask", gmask[:].rearrange("p j n -> p (j n)"))):
                    sp.dma_start(t, io[n]).then_inc(tables, 16)
                G.wait(sp, "zero")
                with sp.Fori(0, CB) as p:
                    Vt.wait(sp, "out", p - 1)
                    sp.dma_start(wa[0:64, 0, :], io["w_up_w"].rearrange("l r n -> r l n")[:, ds(l, 1), ds(p * P, P)]
                                 .rearrange("r a n -> r (a n)")).then_inc(wload, 16)
                    sp.dma_start(wa[64:128, 1, :], io["a_up_w"].rearrange("l r n -> r l n")[:, ds(l, 1), ds(p * P, P)]
                                 .rearrange("r a n -> r (a n)")).then_inc(wload, 16)
                    sp.dma_start(gup[:], io["g_up_w"].rearrange("l r n -> r l n")[:, ds(l, 1), ds(p * P, P)]
                                 .rearrange("r a n -> r (a n)")).then_inc(wload, 16)
                    Vt.wait(sp, f"gm{NW - 1}", p)
                    At.wait(sp, f"tm{NW - 1}", p)
                    st = io["state_wkv"].rearrange("l b h v k -> h v (l b) k")
                    so_d = io["wkv_sample"].rearrange("l b h v k -> h v (l b) k")
                    po_d = io["wkv_prompt"].rearrange("l a h v k -> (l a h) v k")
                    for hf in range(2):
                        r = slice(64 * hf, 64 * hf + 64)
                        sp.dma_start(Bb[r, 0:NB, r], st[ds(p * 2 + hf, 1), :, ds(l * NB, NB), :]
                                     .rearrange("a v b k -> (a v) b k")).then_inc(sload, 16)
                    At.wait(sp, "final", p)
                    for hf in range(2):
                        r = slice(64 * hf, 64 * hf + 64)
                        sp.dma_start(po_d[ds(l * (2 * CB) + p * 2 + hf, 1), :, :].rearrange("a v k -> (a v) k"), so[r, r])\
                          .then_inc(store, 16)
                    At.wait(sp, "finals", p)
                    for hf in range(2):
                        r = slice(64 * hf, 64 * hf + 64)
                        sp.dma_start(so_d[ds(p * 2 + hf, 1), :, ds(l * NB, NB), :].rearrange("a v b k -> (a v) b k"),
                                     Bb[r, 0:NB, r]).then_inc(store, 16)
                sp.wait_ge(store, 64 * CB + 64)

            @block.tensor
            def _(pe):
                pe.wait_ge(tables, 64)
                G.wait(pe, "zero")
                with pe.Fori(0, CB) as p:
                    Qt.loop(p)
                    Vt.wait(pe, "out", p - 1)

                    def spread(out, lhs, rhs, name):
                        for half in range(2):
                            mm = pe.matmul(out[:, half, 0:NH], lhs, rhs[:, half * NH:(half + 1) * NH], start=True, stop=True)
                        Qt.did(mm, name)
                    pe.wait_ge(wload, p * 48 + 48)
                    spread(D[0], wa[:, 0, :], low, "w")
                    spread(D[1], wa[:, 1, :], low, "a")
                    spread(E[1], gup[:], glow, "g")
                    At.wait(pe, "kksq", p)
                    spread(E[0], self.halves[:], sq[:], "ss")
                    Gt.wait(pe, "rkr", p)
                    At.wait(pe, "decay", p)
                    spread(D[0], self.halves[:], tmp, "bonus")
                    Gt.wait(pe, "r", p)
                    Vt.wait(pe, "operands", p)
                    Vt.wait(pe, "bonus", p)
                    At.wait(pe, "gg", p)
                    for w in range(NW):
                        if w >= 2:
                            Vt.wait(pe, f"gm{w - 2}", p)
                        for i, b in enumerate((Bb, Kb)):
                            mm = pe.matmul(gram_bank(w)[:, i * (P + W):(i + 1) * (P + W)], b[:, w, :], AR[:, w, :],
                                           start=True, stop=True)
                        Qt.did(mm, f"gram{w}")
                        if w >= 2:
                            At.wait(pe, f"tm{w - 2}", p)
                        for i, b in enumerate((Bb, Kb, Vb)):
                            tr = pe.transpose(tok_bank(w)[:, i * P:(i + 1) * P], b[:, w, :], self.ident[:])
                        Qt.did(tr, f"tok{w}")

                    def turn(j, g):
                        for i in range(GW):
                            tr = pe.transpose(inv_bank(g)[:, i * P:(i + 1) * P], TT[:, g * GW + i, :], self.ident[:])
                        Qt.did(tr, f"tr{j}_{g}")
                    for g in range(NG):
                        Gt.wait(pe, f"tt0_{g}", p)
                        turn(0, g)
                    for j in range(1, 6):
                        for g in range(NG):
                            At.wait(pe, f"t{j - 1}_{g}", p)
                            Gt.wait(pe, f"lm{j}_{g}", p)
                            for i in range(GW):
                                mm = pe.matmul(inv_bank(g)[:, i * P:(i + 1) * P], Lm[:, g * GW + i, :], T[:, g * GW + i, :],
                                               start=True, stop=True)
                            Qt.did(mm, f"w{j}_{g}")
                        for g in range(NG):
                            Vt.wait(pe, f"w{j}_{g}", p)
                            for i in range(GW):
                                mm = pe.matmul(inv_bank(g)[:, i * P:(i + 1) * P], W1[:, g * GW + i, :], TT[:, g * GW + i, :],
                                               start=True, stop=True)
                            Qt.did(mm, f"dt{j}_{g}")
                        for g in range(NG):
                            Vt.wait(pe, f"tt{j}_{g}", p)
                            if j < 5:
                                turn(j, g)
                    At.wait(pe, f"tm{NW - 1}", p)
                    for w in range(NW - 1):
                        s = S[w % 2]
                        if w:
                            Vt.wait(pe, f"s{w}", p)
                        else:
                            Gt.wait(pe, "s0", p)
                        pe.matmul(D[0][:, 0, 0:P], AR[:, w, 0:P], s[:], start=True, stop=False)
                        Qt.did(pe.matmul(D[0][:, 0, 0:P], GM[:, w, 1, 0:P], TM[:, w, 2, :], start=False, stop=True), f"x{w}")
                        At.wait(pe, f"xs{w}", p)
                        Qt.did(pe.matmul(D[0][:, 1, 0:P], TT[:, w, :], Xs[:], start=True, stop=True), f"u{w}")
                        Vt.wait(pe, f"us{w}", p)
                        pe.matmul(D[1][:, 0, 0:P], TM[:, w, 0, :], Us[:], start=True, stop=False)
                        Qt.did(pe.matmul(D[1][:, 0, 0:P], TM[:, w, 1, :], TM[:, w, 2, :], start=False, stop=True), f"st{w}")
                        if w:
                            At.wait(pe, f"yo{w - 1}", p)
                        pe.matmul(D[1][:, 1, 0:W], s[:], AR[:, w, P:], start=True, stop=False)
                        pe.matmul(D[1][:, 1, 0:W], Us[:], GM[:, w, 0, P:], start=False, stop=False)
                        Qt.did(pe.matmul(D[1][:, 1, 0:W], TM[:, w, 2, :], GM[:, w, 1, P:], start=False, stop=True), f"y{w}")
                    w = NW - 1
                    Vt.wait(pe, f"s{w}", p)
                    Qt.did(pe.transpose(E[0][:, 0, 0:P], S[w % 2][:], self.ident[:]), "final")
                    pe.wait_ge(sload, p * 32 + 32)
                    for b in range(NB):
                        tr = pe.transpose(E[1][:, b // 4, b % 4 * P:(b % 4 + 1) * P], Bb[:, b, :], self.ident[:])
                    Qt.did(tr, "sturn")
                    At.wait(pe, "s0s", p)
                    heads = lambda t: t.rearrange("p (h s) -> p h s", h=2)
                    for b in range(NB):
                        t = slice(b * TS, (b + 1) * TS)
                        mm = pe.matmul(heads(D[0][:, 0, 0:P])[:, :, t], Kb[:, b, :], heads(AR[:, w, 0:P])[:, :, t],
                                       start=(b == 0), stop=(b == NB - 1), skip_group_check=True)
                    Qt.did(mm, "from_states")
                    At.wait(pe, "from_states", p)
                    pe.matmul(D[0][:, 1, 0:P], so[:], self.ident[:], start=True, stop=False)
                    Qt.did(pe.matmul(D[0][:, 1, 0:P], GM[:, w, 1, 0:P], TM[:, w, 2, :], start=False, stop=True), f"x{w}")
                    At.wait(pe, f"xs{w}", p)
                    Qt.did(pe.matmul(D[1][:, 0, 0:P], TT[:, w, :], Xs[:], start=True, stop=True), f"u{w}")
                    At.wait(pe, f"yo{w - 1}", p)
                    Vt.wait(pe, f"us{w}", p)
                    for b in range(NB):
                        t = slice(b * TS, (b + 1) * TS)
                        pe.matmul(D[1][:, 1, t], Kb[:, b, :], AR[:, w, P + b * TS:P + (b + 1) * TS],
                                  start=(b == 0), stop=False, skip_group_check=True)
                    pe.matmul(D[1][:, 1, 0:W], Us[:], GM[:, w, 0, P:], start=False, stop=False, skip_group_check=True)
                    Qt.did(pe.matmul(D[1][:, 1, 0:W], TM[:, w, 2, :], GM[:, w, 1, P:], start=False, stop=True,
                                     skip_group_check=True), f"y{w}")
                    Vt.wait(pe, "masked", p)
                    At.wait(pe, "final", p)
                    for half in range(2):
                        r = slice(4 * half, 4 * half + 4)
                        pe.matmul(E[0][:, half, :], TM[:, w, 0, :], Bb[:, r, :].rearrange("p b n -> p (b n)"),
                                  start=True, stop=False)
                        mm = pe.matmul(E[0][:, half, :], TM[:, w, 1, :], Vb[:, r, :].rearrange("p b n -> p (b n)"),
                                       start=False, stop=True)
                    Qt.did(mm, f"st{w}")
                    Vt.wait(pe, "snew", p)
                    for b in range(NB):
                        tr = pe.transpose(E[1][:, b // 4, b % 4 * P:(b % 4 + 1) * P], Kb[:, b, :], self.ident[:])
                    Qt.did(tr, "finals")
                    At.wait(pe, f"yo{w}", p)
                    spread(D[0], self.halves[:], yt[:], "mean")
                    At.wait(pe, "ysq", p)
                    spread(D[1], self.halves[:], sq[:], "var")
                Qt.end(CB)

            @block.scalar
            def _(act):
                with act.Fori(0, CB) as p:
                    At.loop(p)
                    Vt.wait(act, "out", p - 1)
                    v0 = lambda n: self.vec[:, ds(p + VEC[n][0], 1)]
                    Qt.wait(act, "w", p)
                    At.own(act)
                    At.did(act.activation(two(lw[:]), D[0][:, :, 0:NH], ACT.Sigmoid, bias=v0("w0"), scale=1.0), "decay")
                    Qt.wait(act, "a", p)
                    At.own(act)
                    At.did(act.activation(two(a[:]), D[1][:, :, 0:NH], ACT.Sigmoid, bias=v0("a0"), scale=1.0), "a")
                    Vt.wait(act, "kk", p)
                    At.own(act)
                    At.did(act.activation(sq[:], kk[:], ACT.Square), "kksq")
                    Qt.wait(act, "g", p)
                    At.own(act)
                    At.did(act.activation(two(gg[:]), E[1][:, :, 0:NH], ACT.Copy), "gg")
                    Vt.wait(act, "ssmax", p)
                    At.own(act)
                    At.did(act.activation(pprev[:], pprev[:], ACT.Sqrt), "ssroot")
                    Vt.wait(act, "cum", p)
                    act.activation(pin[:], cum[:], ACT.Exp)
                    At.own(act)
                    At.did(act.activation(pinv[:], cum[:], ACT.Exp, scale=-1.0), "pinv")
                    Vt.wait(act, "rss", p)
                    At.own(act)
                    At.did(act.activation(pprev[:], lw[:], ACT.Exp), "pprev")
                    for w in range(NW):
                        Qt.wait(act, f"tok{w}", p)
                        At.own(act)
                        At.did(act.activation(TM[:, w].rearrange("p i n -> p (i n)"), tok_bank(w), ACT.Copy), f"tm{w}")
                    for j in range(5):
                        for g in range(NG):
                            Qt.wait(act, f"tr{j}_{g}", p)
                            At.own(act)
                            At.did(act.activation(T[:, grp(g), :], blocks(inv_bank(g)), ACT.Copy), f"t{j}_{g}")
                    for w in range(NW - 1):
                        Qt.wait(act, f"x{w}", p)
                        At.own(act)
                        At.did(act.activation(Xs[:], D[0][:, 0, 0:P], ACT.Copy), f"xs{w}")
                        Qt.wait(act, f"y{w}", p)
                        At.own(act)
                        At.did(act.activation(yt[:, w * W:(w + 1) * W], D[1][:, 1, 0:W], ACT.Copy), f"yo{w}")
                    w = NW - 1
                    Qt.wait(act, "final", p)
                    act.wait_ge(store, p * 64 + 64)
                    At.own(act)
                    At.did(act.activation(so[:], E[0][:, 0, 0:P], ACT.Copy), "final")
                    Qt.wait(act, "sturn", p)
                    At.own(act)
                    At.did(act.activation(Kb[:, 0:NB, :].rearrange("p (a b) n -> p a (b n)", a=2), E[1][:], ACT.Copy), "s0s")
                    Qt.wait(act, "from_states", p)
                    act.wait_ge(store, p * 64 + 96)
                    At.own(act)
                    At.did(act.activation(so[:], D[0][:, 0, 0:P], ACT.Copy), "from_states")
                    Qt.wait(act, f"x{w}", p)
                    At.own(act)
                    At.did(act.activation(Xs[:], D[0][:, 1, 0:P], ACT.Copy), f"xs{w}")
                    Qt.wait(act, f"y{w}", p)
                    At.own(act)
                    At.did(act.activation(yt[:, w * W:(w + 1) * W], D[1][:, 1, 0:W], ACT.Copy), f"yo{w}")
                    Qt.wait(act, "finals", p)
                    At.own(act)
                    At.did(act.activation(Bb[:, 0:NB, :].rearrange("p (a b) n -> p a (b n)", a=2), E[1][:], ACT.Copy), "finals")
                    Vt.wait(act, "centred", p)
                    At.own(act)
                    At.did(act.activation(sq[:], yt[:], ACT.Square), "ysq")
                    Qt.wait(act, "var", p)
                    At.own(act)
                    At.did(act.activation(two(pin[:]), D[1][:, :, 0:NH], ACT.Sqrt, bias=self.eps[:, 2:3], scale=1.0 / W), "ydev")
                At.end(CB)

            @block.vector
            def _(dve):
                dve.wait_ge(tables, 64)
                ka0 = VEC["k_a"][0]
                V.own(dve)
                V.did(dve.tensor_scalar(omka[:], self.vec[:, ka0:ka0 + CB], -1.0, 1.0, ALU.mult, ALU.add), "omka")
                G.wait(dve, "zero")
                with dve.Fori(0, CB) as p:
                    Vt.loop(p)
                    v0 = lambda n: self.vec[:, ds(p + VEC[n][0], 1)]
                    zr = lambda i, r=slice(0, P): z[r, ds(p + i * CB, 1), :].rearrange("p a t -> p (a t)")
                    Vt.own(dve)
                    Vt.did(dve.tensor_scalar(kk[:], zr(1), v0("k_k"), None, ALU.mult), "kk")
                    At.wait(dve, "decay", p)
                    Vt.own(dve)
                    Vt.did(dve.tensor_scalar(lw[:], lw[:], cmul, None, ALU.mult))
                    Vt.own(dve)
                    Vt.did(dve.tensor_tensor_scan(cum[:], carry[:], lw[:], 0.0, ALU.mult, ALU.add), "cum")
                    Vt.own(dve)
                    Qt.wait(dve, "ss", p)
                    Vt.did(dve.tensor_scalar(two(pprev[:]), E[0][:, :, 0:NH], 1e-24, None, ALU.max), "ssmax")
                    Vt.own(dve)
                    Vt.did(dve.tensor_tensor(lw[:], cum[:], lw[:], ALU.subtract), "before")
                    At.wait(dve, "ssroot", p)
                    Vt.own(dve)
                    Vt.did(dve.reciprocal(sq[:], pprev[:]), "rss")
                    Vt.own(dve)
                    Vt.did(dve.tensor_tensor(kk[:], kk[:], sq[:], ALU.mult), "kkn")
                    Vt.own(dve)
                    Qt.wait(dve, "bonus", p)
                    Vt.did(dve.tensor_tensor(two(bonus[:]), D[0][:, :, 0:NH], two(zr(2)), ALU.mult), "bonus")
                    At.wait(dve, "pprev", p)
                    for hf in range(2):
                        r = slice(64 * hf, 64 * hf + 64)
                        dve.scalar_tensor_tensor(AR[r, :, r], win(kk, r), -1.0, win(pprev, r), ALU.mult, ALU.mult)
                    Gt.wait(dve, "kp", p)
                    for hf in range(2):
                        r = slice(64 * hf, 64 * hf + 64)
                        o = dve.tensor_tensor(Kb[r, :, r], win(kp, r), win(pinv, r), ALU.mult)
                    Vt.did(o)
                    Vt.own(dve)
                    Vt.did(dve.tensor_tensor(kk[:], kk[:], a[:], ALU.mult))
                    Vt.own(dve)
                    dve.wait_ge(store, p * 64 + 64)
                    for hf in range(2):
                        r = slice(64 * hf, 64 * hf + 64)
                        o = dve.tensor_tensor(Bb[r, :, r], win(kk, r), win(pinv, r), ALU.mult)
                    Vt.did(o, "operands")
                    for w in range(NW):
                        Qt.wait(dve, f"gram{w}", p)
                        m = gmask[:, w // (NW - 1):w // (NW - 1) + 1, :].to_broadcast([P, 2, P + W])
                        Vt.own(dve)
                        Vt.did(dve.tensor_tensor(GM[:, w], gram_bank(w).rearrange("p (i n) -> p i n", i=2), m, ALU.mult), f"gm{w}")
                    for j in range(1, 6):
                        for g in range(NG):
                            Qt.wait(dve, f"w{j}_{g}", p)
                            Vt.own(dve)
                            Vt.did(dve.tensor_copy(W1[:, grp(g), :], blocks(inv_bank(g))), f"w{j}_{g}")
                        for g in range(NG):
                            Qt.wait(dve, f"dt{j}_{g}", p)
                            if j > 1:
                                Vt.own(dve)
                            Vt.did(dve.tensor_tensor(TT[:, grp(g), :], TT[:, grp(g), :], blocks(inv_bank(g)), ALU.add), f"tt{j}_{g}")
                    for w in range(NW - 1):
                        Qt.wait(dve, f"u{w}", p)
                        Vt.own(dve)
                        Vt.did(dve.tensor_copy(Us[:], D[0][:, 1, 0:P]), f"us{w}")
                        Qt.wait(dve, f"st{w}", p)
                        Gt.wait(dve, f"sp{w}", p)
                        e = w * W + W - 1
                        Vt.own(dve)
                        Vt.did(dve.scalar_tensor_tensor(S[(w + 1) % 2][:], D[1][:, 0, 0:P], pin[:, e:e + 1], SP[:],
                                                        ALU.mult, ALU.add), f"s{w + 1}")
                        Qt.wait(dve, f"y{w}", p)
                    w = NW - 1
                    Qt.wait(dve, f"u{w}", p)
                    Vt.own(dve)
                    Vt.did(dve.tensor_copy(Us[:], D[1][:, 0, 0:P]), f"us{w}")
                    Vt.own(dve)
                    bm = bmask[:].unsqueeze(2).to_broadcast([P, NB, P])
                    dve.tensor_tensor(Bb[:, 0:NB, :], Us[:].unsqueeze(1).to_broadcast([P, NB, P]), bm, ALU.mult)
                    Vt.own(dve)
                    Vt.did(dve.tensor_tensor(Vb[:, 0:NB, :], TM[:, w, 2:3, :].to_broadcast([P, NB, P]), bm, ALU.mult), "masked")
                    Qt.wait(dve, f"st{w}", p)
                    kv = Kb[:, 0:NB, :].rearrange("p (a b) n -> p a (b n)", a=2)
                    Vt.own(dve)
                    Vt.did(dve.tensor_tensor(kv, kv, E[0][:], ALU.add))
                    Vt.own(dve)
                    pe_ = pin[:, TP + TS - 1:NT:TS].unsqueeze(2).to_broadcast([P, NB, P])
                    Vt.own(dve)
                    Vt.did(dve.tensor_tensor(Kb[:, 0:NB, :], Kb[:, 0:NB, :], pe_, ALU.mult), "snew")
                    Qt.wait(dve, "mean", p)
                    Vt.own(dve)
                    Vt.did(dve.scalar_tensor_tensor(two(yt[:]), D[0][:, :, 0:NH], -1.0 / W, two(yt[:]), ALU.mult, ALU.add), "centred")
                    At.wait(dve, "ydev", p)
                    Vt.own(dve)
                    Vt.did(dve.reciprocal(pin[:], pin[:]))
                    Vt.own(dve)
                    Vt.did(dve.tensor_tensor(yt[:], yt[:], pin[:], ALU.mult))
                    Vt.own(dve)
                    Vt.did(dve.tensor_scalar(yt[:], yt[:], v0("lnx_w"), v0("lnx_b"), ALU.mult, ALU.add))
                    Vt.own(dve)
                    Vt.did(dve.tensor_tensor(yt[:], yt[:], bonus[:], ALU.add))
                    Vt.own(dve)
                    At.wait(dve, "finals", p)
                    Vt.did(dve.tensor_tensor(y[:, ds(p + 4, 1), :].rearrange("p a t -> p (a t)"), yt[:], gg[:], ALU.mult), "out")
                Vt.end(CB)

            @block.gpsimd
            def _(pool):
                self.credits(pool, (At, Vt, Qt, Gt))
                pool.memset(self.junk[:, 14:15], 0.0).then_inc(store, 64)
                for t in (AR, Bb, Kb, Vb, wa):
                    G.own(pool)
                    G.did(pool.memset(t[:], 0.0), "zero" if t is wa else None)
                G.own(pool)
                pool.wait_ge(tables, 64)
                V.wait(pool, "omka")
                for p in range(CB):
                    Gt.loop(p)
                    v0 = lambda n: self.vec[:, ds(p + VEC[n][0], 1)]
                    zr = lambda i, r=slice(0, P): z[r, ds(p + i * CB, 1), :].rearrange("p a t -> p (a t)")
                    Vt.wait(pool, "out", p - 1)
                    for hf in range(2):
                        r = slice(64 * hf, 64 * hf + 64)
                        Gt.own(pool)
                        Gt.did(pool.tensor_copy(Vb[r, :, r], zr(2, r).rearrange("p (w s) -> p w s", w=NW)))
                    Gt.own(pool)
                    Gt.did(pool.memset(S[0][:], 0.0), "s0")
                    At.wait(pool, "a", p)
                    Gt.own(pool)
                    Gt.did(pool.tensor_scalar(kp[:], a[:], v0("k_a"), omka[:, ds(p, 1)], ALU.mult, ALU.add))
                    Gt.own(pool)
                    Gt.did(pool.tensor_tensor(kp[:], kp[:], zr(1), ALU.mult), "kp")
                    Gt.own(pool)
                    Gt.did(pool.tensor_tensor(tmp[:], kp[:], zr(0), ALU.mult))
                    Gt.own(pool)
                    Gt.did(pool.tensor_scalar(tmp[:], tmp[:], v0("r_k"), None, ALU.mult), "rkr")
                    At.wait(pool, "pinv", p)
                    Gt.own(pool)
                    Gt.did(pool.tensor_tensor(AR[:, :, P:], zr(0).rearrange("p (w s) -> p w s", w=NW), win(pin[:]), ALU.mult), "r")
                    Vt.wait(pool, "operands", p)
                    Qt.wait(pool, "bonus", p)
                    for g in range(NG):
                        Vt.wait(pool, f"gm{g * GW + GW - 1}", p)
                        LT = GM[:, grp(g), 0, 0:P]
                        m = lambda j: lev[:, j:j + 1, :].to_broadcast([P, GW, P])
                        Gt.own(pool)
                        Gt.did(pool.tensor_tensor(TT[:, grp(g), :], LT, m(0), ALU.mult))
                        Gt.own(pool)
                        Gt.did(pool.tensor_tensor(TT[:, grp(g), :], TT[:, grp(g), :],
                                                  self.ident[:].unsqueeze(1).to_broadcast([P, GW, P]), ALU.add), f"tt0_{g}")
                        Gt.own(pool)
                        Gt.did(pool.tensor_tensor(Lm[:, grp(g), :], LT, m(1), ALU.mult), f"lm1_{g}")
                    for j in range(2, 6):
                        for g in range(NG):
                            LT = GM[:, grp(g), 0, 0:P]
                            m = lev[:, j:j + 1, :].to_broadcast([P, GW, P])
                            Qt.wait(pool, f"w{j - 1}_{g}", p)
                            Gt.own(pool)
                            Gt.did(pool.tensor_tensor(Lm[:, grp(g), :], LT, m, ALU.mult), f"lm{j}_{g}")
                    for w in range(NW - 1):
                        e = w * W + W - 1
                        if w:
                            Vt.wait(pool, f"s{w}", p)
                        else:
                            Gt.own(pool)
                        Gt.did(pool.tensor_scalar(SP[:], S[w % 2][:], pin[:, e:e + 1], None, ALU.mult), f"sp{w}")
                Gt.end(CB)

    def split_branches(self, y, y_hi, y_lo):
        A, V, Q, G = self.stage_steps("splity")
        with self.nc.Block() as block:
            @block.scalar
            def _(act):
                for c in range(12):
                    A.own(act)
                    A.did(act.activation(y_hi[:, c, :], y[:, c, :], ACT.Copy), f"hi{c}")

            @block.vector
            def _(dve):
                for c in range(12):
                    A.wait(dve, f"hi{c}")
                    V.own(dve)
                    V.did(dve.tensor_tensor(y_lo[:, c, :], y[:, c, :], y_hi[:, c, :].bitcast(F32), ALU.subtract), f"lo{c}")

    def merge(self, l, y_hi, y_lo, m_hi, m_lo, tile):
        nc, io, ev = self.nc, self.io, self.evac
        gates = [tile(f"gate{i}", [P, NT]) for i in range(3)]
        part, acc = tile("part", [P, NT]), tile("acc", [P, NT])
        win = io["w_in"].rearrange("l (c p) n -> p (l c) n", p=P)
        wb = [io[f"w_branch_{b}"].rearrange("l (c p) n -> p (l c) n", p=P) for b in "abc"]
        wo = io["w_out"].rearrange("l (c p) n -> p (l c) n", p=P)
        two = lambda t: t.rearrange("p (a t) -> p a t", a=2)
        GP = 3 * KD

        with nc.Block() as block:
            @block.gpsimd
            def _(pool):
                self.credits(pool)

            @block.sync
            def _(sp):
                with sp.Fori(0, KD) as c:
                    for j in range(6):
                        src = win[:, ds(l * KD, KD), ds((c + (COL_G + KD * j)) * P, P)] if j < 3 else \
                            wb[j - 3][:, ds(l * CB, CB), ds(c * P, P)]
                        self.load_w(sp, c * 3 + j // 2, j % 2, src)
                with sp.Fori(0, KD // 2) as c:
                    for s in range(2):
                        self.load_w(sp, c + GP, s, wo[:, ds(l * KD, KD), ds((c * 2 + s) * P, P)])

            @block.tensor
            def _(pe):
                with pe.Fori(0, KD) as c:
                    for j in range(6):
                        k, s = c * 3 + j // 2, j % 2
                        use = (s, c * 3 + (j // 2 + 1))
                        if j < 3:
                            self.products(pe, k, s, self.h_hi, self.h_lo, self.D[s], use)
                        else:
                            r = slice((j - 3) * CB, (j - 2) * CB)
                            self.products(pe, k, s, y_hi[:, r, :], y_lo[:, r, :], self.D[s], use)
                pe.wait_ge(self.part_lo, KD + 1)
                with pe.Fori(0, KD // 2) as c:
                    for s in range(2):
                        self.products(pe, c + GP, s, m_hi, m_lo, self.D[s], (s, c + (GP + 1)))

            @block.scalar
            def _(act):
                def gate(i, j, c):
                    n = i * 2
                    if j < 2:
                        for s in range(2 - j):
                            act.wait_ge(self.mm_done, n + (s + 3))
                            act.activation(two(gates[2 * j + s][:]), self.D[s][:, :, 0:NH], ACT.Sigmoid).then_inc(ev[s], 1)
                    else:
                        act.wait_ge(self.dve_turns, c * 2 + 2)
                        act.activation(m_hi[:, ds(c, 1), :].rearrange("p a t -> p (a t)"), acc[:], ACT.Copy)\
                           .then_inc(self.part_hi, 1)
                self.chase(act, lambda k: self.split_hi(act, k), [(GP, 3, gate), (KD // 2, 1, lambda i, j, c: None)])

            @block.vector
            def _(dve):
                def branch(i, j, c):
                    n = i * 2
                    if j == 1:
                        dve.wait_ge(self.mm_done, n + 4)
                        dve.wait_ge(ev[0], c * 3 + 2)
                        dve.wait_ge(self.part_lo, c + 1)
                        dve.tensor_tensor(two(acc[:]), self.D[1][:, :, 0:NH], two(gates[0][:]), ALU.mult).then_inc(ev[1], 1)
                    if j == 2:
                        dve.wait_ge(self.mm_done, n + 3)
                        dve.wait_ge(ev[1], c * 3 + 3)
                        dve.tensor_tensor(two(part[:]), self.D[0][:, :, 0:NH], two(gates[1][:]), ALU.mult).then_inc(ev[0], 1)
                        dve.wait_ge(ev[0], c * 3 + 4)
                        dve.tensor_tensor(acc[:], acc[:], part[:], ALU.add).then_inc(self.dve_turns, 1)
                        dve.wait_ge(self.mm_done, n + 4)
                        dve.wait_ge(self.dve_turns, c * 2 + 1)
                        dve.tensor_tensor(two(part[:]), self.D[1][:, :, 0:NH], two(gates[2][:]), ALU.mult).then_inc(ev[1], 1)
                        dve.wait_ge(ev[1], c * 3 + 4)
                        dve.tensor_tensor(acc[:], acc[:], part[:], ALU.add).then_inc(self.dve_turns, 1)
                        dve.wait_ge(self.part_hi, c + 1)
                        dve.tensor_tensor(m_lo[:, ds(c, 1), :].rearrange("p a t -> p (a t)"), acc[:],
                                          m_hi[:, ds(c, 1), :].rearrange("p a t -> p (a t)").bitcast(F32),
                                          ALU.subtract).then_inc(self.part_lo, 1)

                def add_out(i, j, c):
                    for s in range(2):
                        dve.wait_ge(self.mm_done, i * 2 + (2 * GP + s + 3))
                        xs = self.x[:, ds(i * 2 + s, 1), :].rearrange("p a (b t) -> p (a b) t", b=2)
                        dve.tensor_tensor(xs, self.D[s][:, :, 0:NH], xs, ALU.add).then_inc(ev[s], 1)
                self.chase(dve, lambda k: self.split_lo(dve, k), [(GP, 3, branch), (KD // 2, 1, add_out)])

    def finish(self):
        nc, io = self.nc, self.io
        tile = self.region("final", self.r0)
        self.norm_tiles(tile)
        A, V, Q, G = self.stage_steps("final")
        out = tile("out", [P, TP // P + 1, D])
        nblk = TP // P + 1
        with nc.Block() as block:
            @block.tensor
            def _(pe):
                self.norm_pe(pe, A, Q)
                V.wait(pe, "y")
                for b in range(nblk):
                    m = P if b < nblk - 1 else NS
                    if b >= 2:
                        (A, V)[b % 2].wait(pe, f"out{b - 2}")
                    for c in range(KD):
                        tr = pe.transpose(self.D[b % 2][0:m, c // 4, c % 4 * P:(c % 4 + 1) * P],
                                          self.x[:, c, b * P:b * P + m], self.ident[:])
                    Q.did(tr, f"turn{b}")

            @block.scalar
            def _(act):
                self.norm_act(act, A, V, Q)
                for b in range(0, nblk, 2):
                    m = P if b < nblk - 1 else NS
                    Q.wait(act, f"turn{b}")
                    A.own(act)
                    A.did(act.activation(out[0:m, b, :].rearrange("p (a n) -> p a n", a=2), self.D[0][0:m], ACT.Copy), f"out{b}")

            @block.vector
            def _(dve):
                A.wait(dve, "root")
                V.own(dve)
                V.did(dve.reciprocal(self.rstd[:], self.rstd[:]))
                V.own(dve)
                for c in range(KD):
                    o = dve.scalar_tensor_tensor(self.x[:, c, :], self.x[:, c, :], self.vec_all[:, L - 1, NVEC + c:NVEC + c + 1],
                                                 self.rstd[:], ALU.mult, ALU.mult)
                V.did(o, "y")
                for b in range(1, nblk, 2):
                    Q.wait(dve, f"turn{b}")
                    V.own(dve)
                    V.did(dve.tensor_copy(out[:, b, :].rearrange("p (a n) -> p a n", a=2), self.D[1][:]), f"out{b}")

            @block.sync
            def _(sp):
                A.wait(sp, f"out{nblk - 1}")
                V.wait(sp, f"out{nblk - 2}")
                sp.dma_start(io["y_prompt"].rearrange("a (b p) d -> p (a b) d", p=P), out[:, 0:nblk - 1, :])\
                  .then_inc(self.stores[0], 16)
                sp.dma_start(io["y_sample"].rearrange("b s d -> (b s) d"), out[0:NS, nblk - 1, :]).then_inc(self.stores[0], 16)
                sp.wait_ge(self.stores[0], 32)

    def build(self):
        nc = self.nc
        KB = 4 * NT
        y = self.place("y", [P, 12, NT], self.r0)
        proj = self.place("proj", [P, 24, NT], self.r0 + 12 * KB)
        z = self.place("z", [P, CZ, NT], self.r0 + 12 * KB)
        m_hi = self.place("m_hi", [P, KD, NT], self.r0, F32R)
        m_lo = self.place("m_lo", [P, KD, NT], self.r0 + KD * KB, F32R)
        y_hi = self.place("y_hi", [P, 12, NT], self.r0 + 16 * KB, F32R)
        y_lo = self.place("y_lo", [P, 12, NT], self.r0 + 28 * KB, F32R)
        self.setup()
        with nc.Fori(0, L) as l:
            self.barrier()
            self.layer_vectors(l)
            self.barrier()
            self.ffn(l, "ffn1")
            self.barrier()
            tile = self.region("proj", self.r0 + 36 * KB)
            self.norm_tiles(tile)
            self.project(l, "proj", [(0, 12), (COL_Q, 12)], proj, True)
            self.barrier()
            tile = self.region("attn", self.r0 + 36 * KB)
            vtok = tile("vtok", [P, TP // P + 1, DB])
            after = tile.at[0]
            self.prompt_attention(l, proj, y, vtok, tile)
            self.barrier()
            self.sample_attention(l, proj, y, vtok, self.region("sample", after))
            self.barrier()
            self.project(l, "z", [(COL_Z, CZ)], z, False)
            self.barrier()
            self.token_shift(l, z)
            self.barrier()
            self.recurrence(l, z, y, self.region("rwkv", self.r0 + (12 + CZ) * KB))
            self.barrier()
            self.split_branches(y, y_hi, y_lo)
            self.barrier()
            self.merge(l, y_hi, y_lo, m_hi, m_lo, self.region("merge", self.r0 + 40 * KB))
            self.barrier()
            self.ffn(l, "ffn2")
        self.barrier()
        self.finish()


def program(make_nc, io_of):
    book = {}
    for _ in range(2):
        nc = make_nc()
        io = io_of(nc)
        with ExitStack() as ctx:
            core = Core(nc, ctx, io, book)
            core.build()
            assert _ == 0 or core.new == book
        book = core.new
    return nc


_INS = ['x_prompt', 'x_sample', 'cache_k', 'cache_v', 'state_wkv', 'state_shift', 'state_conv', 'page_table',
        'ffn1_norm', 'ffn1_w_gate', 'ffn1_w_up', 'ffn1_w_down', 'mix_norm', 'w_in', 'conv_w', 'tm_mu',
        'w_up_w', 'w0', 'a_up_w', 'a0', 'g_up_w', 'k_k', 'k_a', 'r_k', 'lnx_w', 'lnx_b',
        'lam_q1', 'lam_k1', 'lam_q2', 'lam_k2', 'subln_w', 'w_branch_a', 'w_branch_b', 'w_branch_c', 'w_out',
        'ffn2_norm', 'ffn2_w_gate', 'ffn2_w_up', 'ffn2_w_down', 'final_norm']
_OUTS = [('y_prompt', (1, TP, D)), ('y_sample', (NB, TS, D)),
         ('k_prompt', (L, 1, TP, MAPS, 64)), ('v_prompt', (L, 1, TP, HC, P)),
         ('k_sample', (L, NB, TS, MAPS, 64)), ('v_sample', (L, NB, TS, HC, P)),
         ('wkv_prompt', (L, 1, 8, 64, 64)), ('wkv_sample', (L, NB, 8, 64, 64)),
         ('shift_prompt', (L, 1, NSHIFT)), ('shift_sample', (L, NB, NSHIFT)),
         ('conv_prompt', (L, 1, 2, DB)), ('conv_sample', (L, NB, 2, DB))]


def kernel(**inputs):
    import concourse.bacc as _bacc
    from concourse.bass_utils import run_bass_kernel_spmd as _run

    arrays = {n: np.ascontiguousarray(inputs[n]) for n in _INS}
    arrays.update(shape_constants())

    def io_of(nc):
        io = {n: nc.dram_tensor(f"in_{n}_dram", a.shape, mybir.dt.from_np(a.dtype), kind="ExternalInput").ap()
              for n, a in arrays.items()}
        io.update({n: nc.dram_tensor(f"out_{n}_dram", shape, F32, kind="ExternalOutput").ap() for n, shape in _OUTS})
        return io
    nc = program(lambda: _bacc.Bacc("TRN2", target_bir_lowering=False, num_devices=1), io_of)
    r = _run(nc, [{f"in_{n}_dram": a for n, a in arrays.items()}], core_ids=[0])
    return tuple(r.results[0][f"out_{n}_dram"] for n, _ in _OUTS)
```

```python
import math
from contextlib import ExitStack

import numpy as np
import concourse.bass as bass
from concourse import mybir

F32 = mybir.dt.float32
F32R = mybir.dt.float32r
I32 = mybir.dt.int32
ALU = mybir.AluOpType
ACT = mybir.ActivationFunctionType
AX = mybir.AxisListType
ds = bass.ds

P = 128
L = 2
D = 1024
KD = D // P
FF = 2816
KF = FF // P
HF = KF // 2
TP, NB, TS = 512, 8, 8
NS = NB * TS
NT = TP + NS
NH = NT // 2
DB = 512
CB = DB // P
NSHIFT = 3 * DB + 256
CZ = NSHIFT // P
N_IN = 3 * DB + NSHIFT + 3 * DB + 3 * D
COL_Z = 3 * DB // P
COL_Q = COL_Z + CZ
COL_G = COL_Q + 3 * CB
PAST, PAGE = 1024, 128
NPG = PAST // PAGE
HC, MAPS = 4, 8
W = 64
NW = NT // W
NEG = -1.0e30
BASE, LIMIT = 16512, 229344
VEC = {}
_at = 0
for _n, _c in (("ffn1_norm", KD), ("mix_norm", KD), ("ffn2_norm", KD), ("tm_mu", CZ), ("w0", CB), ("a0", CB),
               ("k_k", CB), ("k_a", CB), ("r_k", CB), ("lnx_w", CB), ("lnx_b", CB), ("conv_w", 3 * CB), ("subln_w", 1)):
    VEC[_n] = (_at, _c)
    _at += _c
NVEC = _at


def shape_constants():
    p = np.arange(P)
    half = p // W
    s64 = p % W
    same = (half[:, None] == half[None, :])
    c = {}
    c["ident"] = np.eye(P)
    c["halves"] = same
    slopes = np.array([2.0 ** (-8.0 * (h + 1) / HC) for h in range(HC)])
    t = np.arange(TP)
    dist = p[:, None] - (t[None, :] - (TP - P))
    c["alibi_prompt"] = np.stack([np.where(dist >= 0, -s * dist, NEG) for s in slopes], 1).reshape(P, -1)
    row = np.arange(P)
    m, q = (row % 64) // TS, row % TS
    sl = slopes[m // 2]
    c["alibi_past"] = -sl[:, None] * (PAST + q[:, None] - np.arange(PAST)[None, :])
    kb, ks = np.arange(NS) // TS, np.arange(NS) % TS
    new = np.full((P, NB, NS), NEG)
    for b in range(NB):
        ok = (kb[None, :] == b) & (ks[None, :] <= q[:, None])
        new[:, b] = np.where(ok, -sl[:, None] * (q[:, None] - ks[None, :]), NEG)
    c["alibi_new"] = new.reshape(P, -1)
    s_, t_ = s64[:, None], s64[None, :]
    strict = same & (s_ < t_)
    incl = s_ <= np.arange(W)[None, :]
    sb = (s_ // TS == t_ // TS)
    sbi = (s_ // TS == np.arange(W)[None, :] // TS)
    c["gram_mask"] = np.stack([np.concatenate([strict, incl], 1), np.concatenate([strict & sb, incl & sbi], 1)], 1).reshape(P, -1)
    lev = []
    for j in range(6):
        z = 1 << j
        lev.append(same & (s_ // (2 * z) == t_ // (2 * z)) & (s_ // z % 2 == 0) & (t_ // z % 2 == 1))
    c["level_mask"] = np.stack(lev, 1).reshape(P, -1)
    tt = np.arange(NT)
    first = np.where(tt < TP, tt % W == 0, tt % TS == 0)
    c["carry"] = np.broadcast_to(1.0 - first, (P, NT))
    c["batch_mask"] = (s64[:, None] // TS == np.arange(NB)[None, :])
    e = np.zeros((P, 2, HC * TS))
    for r in range(64):
        mm, qq = r // TS, r % TS
        e[r, mm % 2, (mm // 2) * TS + qq] = 1.0
    c["combine"] = e.reshape(P, -1)
    li = np.array([0.8 - 0.6 * math.exp(-0.3 * l) for l in range(L)])
    c["lam_init"] = np.broadcast_to(np.concatenate([li, 1.0 - li])[None, :], (P, 2 * L))
    return {k: np.ascontiguousarray(v, dtype=np.float32) for k, v in c.items()}


class Steps:

    def __init__(self, sem, stage, book, new):
        self.sem, self.stage, self.book, self.new = sem, stage, book, new
        self.n, self.per, self.it, self.start = 0, 0, None, 0
        self.credit = book.get((stage, "per"), 0)

    def loop(self, it):
        if self.it is None:
            self.start = self.n
        self.it, self.n = it, self.start
        self.per = self.book.get((self.stage, "per"), 0)

    def end(self, turns):
        per = self.n - self.start
        self.new[(self.stage, "per")] = per
        self.it, self.n = None, self.start + turns * per

    def did(self, ins, name=None):
        ins.then_inc(self.sem, 1)
        self.n += 1
        if name is not None:
            assert self.new.get((self.stage, name), self.n) == self.n, (self.stage, name)
            self.new[(self.stage, name)] = self.n

    def own(self, eng):
        v = self.credit + self.n
        if self.it is not None:
            v = self.it * self.per + v
        elif v == 0:
            return
        eng.wait_ge(self.sem, v)

    def wait(self, eng, name, it=0):
        v = self.credit + self.book.get((self.stage, name), 1)
        per = self.book.get((self.stage, "per"), 0)
        if not isinstance(it, int) or it:
            v = it * per + v
        eng.wait_ge(self.sem, v)


class Core:

    def __init__(self, nc, ctx, io, book):
        self.nc, self.io, self.book, self.new = nc, io, book, {}

        def sem(name):
            return ctx.enter_context(nc.semaphore(name))

        self.w_loaded = [sem("w_loaded0"), sem("w_loaded1")]
        self.w_hi = sem("w_hi")
        self.w_split = sem("w_split")
        self.mm_done = sem("mm_done")
        self.evac = [sem("evac0"), sem("evac1")]
        self.part_hi = sem("part_hi")
        self.part_lo = sem("part_lo")
        self.pe_steps, self.act_steps = sem("pe_steps"), sem("act_steps")
        self.dve_steps, self.pool_steps = sem("dve_steps"), sem("pool_steps")
        self.pe_turns, self.act_turns = sem("pe_turns"), sem("act_turns")
        self.dve_turns, self.pool_turns = sem("dve_turns"), sem("pool_turns")
        self.loads = [sem(f"loads{i}") for i in range(5)]
        self.stores = [sem(f"stores{i}") for i in range(2)]
        every = [self.w_hi, self.w_split, self.mm_done, self.part_hi, self.part_lo, self.pe_steps, self.act_steps,
                 self.dve_steps, self.pool_steps, self.pe_turns, self.act_turns, self.dve_turns, self.pool_turns,
                 *self.w_loaded, *self.evac, *self.loads, *self.stores]
        nums = sorted(s.num for s in every)
        assert nums == list(range(nums[0], nums[0] + len(nums)))
        self.all_sems = range(nums[0], nums[-1] + 1)

        at = BASE

        def fixed(name, shape, dt=F32):
            nonlocal at
            t = self.place(name, shape, at, dt)
            at += (4 * int(np.prod(shape[1:])) + 31) // 32 * 32
            return t

        self.ident = fixed("ident", [P, P])
        self.ones = fixed("ones", [P, P])
        self.halves = fixed("halves", [P, P])
        self.vec_all = fixed("vec_all", [P, L, NVEC + KD])
        self.vec = fixed("vec", [P, NVEC])
        self.neg_lam = fixed("neg_lam", [P, L])
        self.lam_init = fixed("lam_init", [P, 2 * L])
        self.nlam = fixed("nlam", [P, 1])
        self.one_li = fixed("one_li", [P, 1])
        self.eps = fixed("eps", [P, 4])
        self.pages = fixed("pages", [1, NB * NPG], I32)
        self.junk = fixed("junk", [P, 16])
        assert at <= BASE + 5120
        at = BASE + 5120
        self.x = fixed("x", [P, KD, NT])
        self.h_hi = fixed("h_hi", [P, KD, NT], F32R)
        self.h_lo = fixed("h_lo", [P, KD, NT], F32R)
        self.ring = at
        self.raw = [fixed(f"raw{s}", [P, KD, P]) for s in range(2)]
        self.whi = [fixed(f"whi{s}", [P, KD, P], F32R) for s in range(2)]
        self.wlo = [fixed(f"wlo{s}", [P, KD, P], F32R) for s in range(2)]
        self.r0 = at
        self.D = [ctx.enter_context(nc.psum_tensor(f"dense{s}", [P, 2, 512], F32)) for s in range(2)]
        self.E = [ctx.enter_context(nc.psum_tensor(f"extra{s}", [P, 2, 512], F32)) for s in range(2)]

    def place(self, name, shape, offset, dt=F32):
        return self.nc.alloc_sbuf_tensor_at(name, shape, dt, offset=offset)

    def region(self, prefix, at):
        here = [at]

        def tile(name, shape, dt=F32):
            t = self.place(f"{prefix}_{name}", shape, here[0], dt)
            here[0] += (4 * int(np.prod(shape[1:])) + 31) // 32 * 32
            assert here[0] <= LIMIT, (prefix, name, here[0])
            return t
        tile.at = here
        return tile

    def steps(self, sem, stage):
        return Steps(sem, stage, self.book, self.new)

    def barrier(self):
        self.nc.all_engine_barrier(sems_to_clear=self.all_sems)

    def credits(self, pool, steps=()):
        give = [(self.part_lo, 1), (self.w_split, 2), (self.mm_done, 2), (self.evac[0], 1), (self.evac[1], 1)]
        give += [(s.sem, s.credit) for s in steps if s.credit]
        for i, (s, n) in enumerate(give):
            pool.memset(self.junk[:, i:i + 1], 0.0).then_inc(s, n)

    def load_w(self, sp, k, s, src):
        sp.wait_ge(self.w_split, 2 * k + s + 1)
        sp.dma_start(self.raw[s][:, 0:src.shape[1], :], src).then_inc(self.w_loaded[s], 16)

    def split_hi(self, act, k, s):
        act.wait_ge(self.w_loaded[s], 16 * k + 16)
        act.wait_ge(self.mm_done, 2 * k + s + 1)
        act.activation(self.whi[s][:], self.raw[s][:], ACT.Copy).then_inc(self.w_hi, 1)

    def split_lo(self, dve, k, s):
        dve.wait_ge(self.w_hi, 2 * k + s + 1)
        dve.tensor_tensor(self.wlo[s][:], self.raw[s][:], self.whi[s][:].bitcast(F32), ALU.subtract)\
           .then_inc(self.w_split, 1)

    def products(self, pe, k, s, hi, lo, out, bank_use=None, first=True, last=True):
        pe.wait_ge(self.w_split, 2 * k + s + 3)
        if bank_use is not None:
            pe.wait_ge(self.evac[bank_use[0]], bank_use[1])
        chunks = hi.shape[1]
        for half in range(2):
            t = slice(half * NH, (half + 1) * NH)
            o = out[:, half, 0:NH]
            for c in range(chunks):
                w_hi, w_lo = self.whi[s][:, c, :], self.wlo[s][:, c, :]
                pe.matmul(o, w_hi, hi[:, c, t], start=(first and c == 0), stop=False)
                pe.matmul(o, w_hi, lo[:, c, t], start=False, stop=False)
                mm = pe.matmul(o, w_lo, hi[:, c, t], start=False, stop=(last and c == chunks - 1))
        mm.then_inc(self.mm_done, 1)

    @staticmethod
    def chase(eng, split, segments):
        for s in range(2):
            split(0, s)
        k0 = 0
        for n, (pairs, unroll, finish) in enumerate(segments):
            last = n == len(segments) - 1
            turns = pairs // unroll - last

            def turn(i, final=False):
                for j in range(unroll):
                    for s in range(2):
                        if not (final and j == unroll - 1):
                            split(i * unroll + (k0 + j + 1), s)
                        finish(i * unroll + j, j, i, s)
            if turns:
                with eng.Fori(0, turns) as i:
                    turn(i)
            if last:
                turn(pairs // unroll - 1, True)
            k0 += pairs

    def norm_tiles(self, tile):
        self.sq = [tile(f"sq{i}", [P, NT]) for i in range(2)]
        self.rstd = tile("rstd", [P, NT])
        self.hf = [tile(f"hf{i}", [P, NT]) for i in range(2)]

    def norm_act(self, act, A, V, Q):
        for c in range(KD):
            if c >= 2:
                Q.wait(act, f"sum{c - 2}")
            A.did(act.activation(self.sq[c % 2][:], self.x[:, c, :], ACT.Square), f"sq{c}")
        Q.wait(act, f"sum{KD - 1}")
        A.own(act)
        A.did(act.activation(self.rstd[:].rearrange("p (a t) -> p a t", a=2), self.E[0][:, :, 0:NH], ACT.Sqrt,
                             bias=self.eps[:, 0:1], scale=1.0 / D), "root")

    def norm_pe(self, pe, A, Q):
        for c in range(KD):
            A.wait(pe, f"sq{c}")
            for half in range(2):
                mm = pe.matmul(self.E[0][:, half, 0:NH], self.ones[:], self.sq[c % 2][:, half * NH:(half + 1) * NH],
                               start=(c == 0), stop=(c == KD - 1))
            Q.did(mm, f"sum{c}")

    def h_act(self, act, A, V):
        for c in range(KD):
            V.wait(act, f"h{c}")
            A.did(act.activation(self.h_hi[:, c, :], self.hf[c % 2][:], ACT.Copy), f"hhi{c}")

    def h_dve(self, dve, A, V, vec):
        A.wait(dve, "root")
        V.did(dve.reciprocal(self.rstd[:], self.rstd[:]), "rstd")
        V.own(dve)

        def low(c):
            A.wait(dve, f"hhi{c}")
            V.did(dve.tensor_tensor(self.h_lo[:, c, :], self.hf[c % 2][:], self.h_hi[:, c, :].bitcast(F32),
                                    ALU.subtract), f"hlo{c}")
        for c in range(KD):
            if c >= 2:
                V.own(dve)
            V.did(dve.scalar_tensor_tensor(self.hf[c % 2][:], self.x[:, c, :], vec[:, c:c + 1], self.rstd[:],
                                           ALU.mult, ALU.mult), f"h{c}")
            if c >= 1:
                low(c - 1)
        low(KD - 1)

    def ffn(self, l, which):
        nc, io, ev = self.nc, self.io, self.evac
        tile = self.region(which, self.r0)
        self.norm_tiles(tile)
        a_hi, a_lo = tile("a_hi", [P, HF, NT], F32R), tile("a_lo", [P, HF, NT], F32R)
        gate, prod = tile("gate", [P, NT]), tile("prod", [P, NT])
        wg = io[which + "_w_gate"].rearrange("l (c p) n -> p (l c) n", p=P)
        wu = io[which + "_w_up"].rearrange("l (c p) n -> p (l c) n", p=P)
        wd = io[which + "_w_down"].rearrange("l (c p) n -> p (l c) n", p=P)
        v0 = VEC[which + "_norm"][0]
        vec = self.vec[:, v0:v0 + KD]
        A, V, Q = (self.steps(s, which + n) for s, n in
                   ((self.act_steps, "A"), (self.dve_steps, "V"), (self.pe_steps, "Q")))
        KS = (HF + 1) // 2
        PAIRS = HF + KD
        pair = [h * PAIRS for h in range(2)]
        used = [h * (HF + KD // 2) for h in range(2)]

        with nc.Block() as block:
            @block.gpsimd
            def _(pool):
                self.credits(pool)

            @block.sync
            def _(sp):
                for h in range(2):
                    with sp.Fori(0, HF) as f:
                        for s, w in enumerate((wg, wu)):
                            self.load_w(sp, f + pair[h], s, w[:, ds(l * KD, KD), ds((f + h * HF) * P, P)])
                    with sp.Fori(0, KD) as c:
                        for s, (a, n) in enumerate(((0, KS), (KS, HF - KS))):
                            self.load_w(sp, c + (pair[h] + HF), s, wd[:, ds(l * KF + (h * HF + a), n), ds(c * P, P)])

            @block.tensor
            def _(pe):
                self.norm_pe(pe, A, Q)
                V.wait(pe, f"hlo{KD - 1}")
                for h in range(2):
                    with pe.Fori(0, HF) as f:
                        for s in range(2):
                            self.products(pe, f + pair[h], s, self.h_hi, self.h_lo, self.D[s], (s, f + (used[h] + 1)))
                    pe.wait_ge(self.part_lo, (h + 1) * HF + 1)
                    with pe.Fori(0, KD // 2) as c:
                        for u in range(2):
                            k = c * 2 + (pair[h] + HF + u)
                            out, use = self.D[u], (u, c + (used[h] + HF + 1))
                            self.products(pe, k, 0, a_hi[:, 0:KS], a_lo[:, 0:KS], out, use, last=False)
                            self.products(pe, k, 1, a_hi[:, KS:HF], a_lo[:, KS:HF], out, first=False)

            @block.scalar
            def _(act):
                self.norm_act(act, A, V, Q)
                self.h_act(act, A, V)

                def silu_and_high(h):
                    def finish(f, j, _, s):
                        if s == 0:
                            act.wait_ge(self.mm_done, f * 2 + (2 * pair[h] + 3))
                            act.wait_ge(ev[1], f + (used[h] + 1))
                            act.activation(gate[:].rearrange("p (a t) -> p a t", a=2), self.D[0][:, :, 0:NH], ACT.Silu)\
                               .then_inc(ev[0], 1)
                            return
                        act.wait_ge(ev[1], f + (used[h] + 2))
                        act.activation(a_hi[:, ds(f, 1), :].rearrange("p a t -> p (a t)"), prod[:], ACT.Copy)\
                           .then_inc(self.part_hi, 1)
                    return finish
                none = lambda i, j, c, s: None
                self.chase(act, lambda k, s: self.split_hi(act, k, s),
                           [(HF, 1, silu_and_high(0)), (KD, 2, none), (HF, 1, silu_and_high(1)), (KD, 2, none)])

            @block.vector
            def _(dve):
                self.h_dve(dve, A, V, vec)

                def times_up(h):
                    def finish(f, j, _, s):
                        if s == 0:
                            return
                        dve.wait_ge(self.mm_done, f * 2 + (2 * pair[h] + 4))
                        dve.wait_ge(ev[0], f + (used[h] + 2))
                        dve.wait_ge(self.part_lo, f + (h * HF + 1))
                        dve.tensor_tensor(prod[:].rearrange("p (a t) -> p a t", a=2), self.D[1][:, :, 0:NH],
                                          gate[:].rearrange("p (a t) -> p a t", a=2), ALU.mult).then_inc(ev[1], 1)
                        dve.wait_ge(self.part_hi, f + (h * HF + 1))
                        dve.tensor_tensor(a_lo[:, ds(f, 1), :].rearrange("p a t -> p (a t)"), prod[:],
                                          a_hi[:, ds(f, 1), :].rearrange("p a t -> p (a t)").bitcast(F32),
                                          ALU.subtract).then_inc(self.part_lo, 1)
                    return finish

                def add_down(h):
                    def finish(c, u, _, s):
                        if s == 0:
                            return
                        dve.wait_ge(self.mm_done, c * 2 + (2 * (pair[h] + HF) + 4))
                        xs = self.x[:, ds(c, 1), :].rearrange("p a (b t) -> p (a b) t", b=2)
                        dve.scalar_tensor_tensor(xs, self.D[u][:, :, 0:NH], 0.5, xs, ALU.mult, ALU.add)\
                           .then_inc(ev[u], 1)
                    return finish
                self.chase(dve, lambda k, s: self.split_lo(dve, k, s),
                           [(HF, 1, times_up(0)), (KD, 2, add_down(0)), (HF, 1, times_up(1)), (KD, 2, add_down(1))])

    def setup(self):
        nc, io, ev = self.nc, self.io, self.evac
        tile = self.region("setup", self.r0)
        rows = [tile(f"rows{l}", [P, P]) for l in range(L)]
        xt = tile("xt", [P, TP // P + 1, D])
        lam = tile("lam", [1, 4, L * 64])
        lprod = tile("lprod", [1, 2, L * 64])
        lsum, lexp, lrow = tile("lsum", [1, 2 * L]), tile("lexp", [1, 2 * L]), tile("lrow", [1, L])
        A, V, Q, G = self.stage_steps("setup")
        consts, vectors, tokens, lams = self.loads[0:4]
        views = {n: io[n].rearrange({"conv_w": "l j (c p) -> (l j c) p", "r_k": "l (c h) k -> (l c) (h k)"}
                                    .get(n, "l (c p) -> (l c) p"), **({"h": 2} if n == "r_k" else {"p": P})) for n in VEC}

        with nc.Block() as block:
            @block.gpsimd
            def _(pool):
                pool.memset(self.ones[:], 1.0)
                pool.memset(self.eps[:, 0:1], 1e-6)
                pool.memset(self.eps[:, 1:2], 1e-5)
                G.own(pool)
                G.did(pool.memset(self.eps[:, 2:3], 64e-5), "ones")

            @block.sync
            def _(sp):
                for n, t in (("ident", self.ident), ("halves", self.halves), ("lam_init", self.lam_init)):
                    sp.dma_start(t[:], io[n]).then_inc(consts, 16)
                for l in range(L):
                    for n, (r, c) in VEC.items():
                        sp.dma_start(rows[l][r:r + c, :], views[n][l * c:(l + 1) * c, :]).then_inc(vectors, 16)
                sp.dma_start(rows[L - 1][NVEC:NVEC + KD, :], io["final_norm"].rearrange("(c p) -> c p", p=P))\
                  .then_inc(vectors, 16)
                sp.dma_start(xt[:, 0:TP // P, :], io["x_prompt"].rearrange("a (b p) d -> p (a b) d", p=P))\
                  .then_inc(tokens, 16)
                sp.dma_start(xt[0:NS, TP // P, :], io["x_sample"].rearrange("b s d -> (b s) d")).then_inc(tokens, 16)
                for i, n in enumerate(("lam_q1", "lam_k1", "lam_q2", "lam_k2")):
                    sp.dma_start(lam[0:1, i, :], io[n].rearrange("(a l) d -> a (l d)", a=1)).then_inc(lams, 16)
                sp.dma_start(self.pages[:], io["page_table"].rearrange("(a b) n -> a (b n)", a=1)).then_inc(lams, 16)

            @block.tensor
            def _(pe):
                pe.wait_ge(consts, 16 * 3)
                pe.wait_ge(vectors, 16 * (L * len(VEC) + 1))
                for l in range(L):
                    n = NVEC + (KD if l == L - 1 else 0)
                    Q.did(pe.transpose(self.E[l][:, 0, 0:n], rows[l][0:n, :], self.ident[0:n, 0:n]), f"vec{l}")
                G.wait(pe, "ones")
                V.wait(pe, "lam")
                Q.did(pe.matmul(self.E[0][:, 1, 0:L], self.ones[0:1, :], lrow[:], start=True, stop=True), "lam")
                pe.wait_ge(tokens, 32)
                for c in range(KD):
                    if c >= 2:
                        V.wait(pe, f"x{c - 2}")
                    for b in range(TP // P):
                        pe.transpose(self.D[c % 2][:, 0, b * P:(b + 1) * P], xt[:, b, c * P:(c + 1) * P], self.ident[:])
                    Q.did(pe.transpose(self.D[c % 2][:, 1, 0:NS], xt[0:NS, TP // P, c * P:(c + 1) * P],
                                       self.ident[0:NS, 0:NS]), f"x{c}")

            @block.scalar
            def _(act):
                V.wait(act, "dots")
                A.own(act)
                A.did(act.activation(lexp[:], lsum[:], ACT.Exp), "exp")
                for l in range(L):
                    n = NVEC + (KD if l == L - 1 else 0)
                    Q.wait(act, f"vec{l}")
                    A.own(act)
                    A.did(act.activation(self.vec_all[:, l, 0:n], self.E[l][:, 0, 0:n], ACT.Copy), f"vec{l}")

            @block.vector
            def _(dve):
                dve.wait_ge(lams, 16 * 5)
                lv = lam[:].rearrange("a (i j) n -> a i j n", j=2)
                V.own(dve)
                V.did(dve.tensor_tensor(lprod[:], lv[:, :, 0, :], lv[:, :, 1, :], ALU.mult), "prods")
                V.own(dve)
                V.did(dve.tensor_reduce(lsum[:], lprod[:].rearrange("a i (l d) -> a (i l) d", l=L), AX.X, ALU.add), "dots")
                A.wait(dve, "exp")
                dve.wait_ge(consts, 16 * 3)
                V.own(dve)
                V.did(dve.tensor_tensor(lrow[:], lexp[:, L:2 * L], lexp[:, 0:L], ALU.subtract), "diff")
                V.own(dve)
                V.did(dve.tensor_tensor(lrow[:], lrow[:], self.lam_init[0:1, 0:L], ALU.subtract), "lam")
                Q.wait(dve, "lam")
                A.wait(dve, "vec0")
                V.own(dve)
                V.did(dve.tensor_copy(self.neg_lam[:], self.E[0][:, 1, 0:L]), "neg_lam")
                for c in range(KD):
                    Q.wait(dve, f"x{c}")
                    dve.tensor_copy(self.x[:, c, 0:TP], self.D[c % 2][:, 0, :])
                    V.own(dve)
                    V.did(dve.tensor_copy(self.x[:, c, TP:NT], self.D[c % 2][:, 1, 0:NS]), f"x{c}")

    def stage_steps(self, stage, turns=False):
        kinds = (self.act_turns, self.dve_turns, self.pe_turns, self.pool_turns) if turns else \
                (self.act_steps, self.dve_steps, self.pe_steps, self.pool_steps)
        return [self.steps(s, stage + n + "t" * turns) for s, n in zip(kinds, "AVQG")]

    def layer_vectors(self, l):
        A, V, Q, G = self.stage_steps("vectors")
        with self.nc.Block() as block:
            @block.vector
            def _(dve):
                dve.tensor_copy(self.vec[:], self.vec_all[:, ds(l, 1), 0:NVEC].rearrange("p a n -> p (a n)"))
                dve.tensor_copy(self.nlam[:], self.neg_lam[:, ds(l, 1)])
                V.own(dve)
                V.did(dve.tensor_copy(self.one_li[:], self.lam_init[:, ds(l + L, 1)]), "all")

    def project(self, l, name, runs, dest, norm):
        nc, io, ev = self.nc, self.io, self.evac
        A, V, Q, G = self.stage_steps(name)
        win = io["w_in"].rearrange("l (c p) n -> p (l c) n", p=P)
        pairs = sum(n for _, n in runs) // 2
        v0 = VEC["mix_norm"][0]

        with nc.Block() as block:
            @block.gpsimd
            def _(pool):
                self.credits(pool)

            @block.sync
            def _(sp):
                k0 = 0
                for first, count in runs:
                    with sp.Fori(0, count // 2) as k:
                        for s in range(2):
                            self.load_w(sp, k + k0, s, win[:, ds(l * KD, KD), ds((k * 2 + (first + s)) * P, P)])
                    k0 += count // 2

            @block.tensor
            def _(pe):
                if norm:
                    self.norm_pe(pe, A, Q)
                    V.wait(pe, f"hlo{KD - 1}")
                with pe.Fori(0, pairs) as k:
                    for s in range(2):
                        self.products(pe, k, s, self.h_hi, self.h_lo, self.D[s], (s, k + 1))

            @block.scalar
            def _(act):
                if norm:
                    self.norm_act(act, A, V, Q)
                    self.h_act(act, A, V)

                def copy_even(k, j, _, s):
                    if s == 1:
                        return
                    act.wait_ge(self.mm_done, k * 2 + 3)
                    act.activation(dest[:, ds(k * 2, 1), :].rearrange("p a (b t) -> p (a b) t", b=2),
                                   self.D[0][:, :, 0:NH], ACT.Copy).then_inc(ev[0], 1)
                self.chase(act, lambda k, s: self.split_hi(act, k, s), [(pairs, 1, copy_even)])

            @block.vector
            def _(dve):
                if norm:
                    self.h_dve(dve, A, V, self.vec[:, v0:v0 + KD])

                def copy_odd(k, j, _, s):
                    if s == 0:
                        return
                    dve.wait_ge(self.mm_done, k * 2 + 4)
                    dve.tensor_copy(dest[:, ds(k * 2 + 1, 1), :].rearrange("p a (b t) -> p (a b) t", b=2),
                                    self.D[1][:, :, 0:NH]).then_inc(ev[1], 1)
                self.chase(dve, lambda k, s: self.split_lo(dve, k, s), [(pairs, 1, copy_odd)])

    def prompt_attention(self, l, proj, y, vtok, tile):
        nc, io = self.nc, self.io
        A, V, Q, G = self.stage_steps("prompt")
        At, Vt, Qt, Gt = self.stage_steps("prompt", True)
        alibi = tile("alibi", [P, HC, TP])
        ring = self.region("prompt_ring", self.ring)
        ktok = ring("ktok", [P, TP // P + 1, DB])
        S = [tile(f"S{i}", [P, 2, TP]) for i in range(2)]
        qm = [tile(f"qm{i}", [P, 2, TP]) for i in range(2)]
        vh = [tile(f"vh{i}", [P, TP // P, P]) for i in range(2)]
        attn_t = [tile(f"attn_t{i}", [P, TP]) for i in range(2)]
        mx, ex, ri = ([tile(f"{n}{i}", [P, w]) for i in range(2)] for n, w in (("mx", 4), ("ex", 2), ("ri", 2)))
        rows_in = ring("rows_in", [NB * 2, DB])
        state = ring("state", [P, CB, NB * 2])
        ext = ring("ext", [P, 2 + TP])
        ext_s = ring("ext_s", [P, NB, 2 + TS])
        tmp, tmp2 = ring("tmp", [P, NT]), ring("tmp2", [P, NT])
        last = ring("last", [P, CB, 2 + NB * 2])
        rows_out = ring("rows_out", [2 + NB * 2, DB])
        tables, states = self.loads[0:2]
        kv_out, conv_out = self.stores
        nblk = TP // P + 1
        cw = VEC["conv_w"][0]
        NU = 2 * (TP // P)
        keys = lambda u: (u % (TP // P) + 1) * P
        bank = lambda pair, u, n: pair[:, u % 2, 0:n]
        kv = [(b, w) for b in range(nblk) for w in range(2)]
        slot = lambda n: self.E[n % 4 // 2][:, n % 2, :]

        def evac_kv(eng, w):
            for n, (b, w_) in enumerate(kv):
                if w_ != w:
                    continue
                m = P if b < nblk - 1 else NS
                Q.wait(eng, f"kv{n}")
                dst = (ktok, vtok)[w][0:m, b, :]
                if w == 0:
                    A.own(eng)
                    A.did(eng.activation(dst, slot(n)[0:m, :], ACT.Copy), f"kv{n}")
                else:
                    V.own(eng)
                    V.did(eng.tensor_copy(dst, slot(n)[0:m, :]), f"kv{n}")

        with nc.Block() as block:
            @block.sync
            def _(sp):
                sp.dma_start(rows_in[:], io["state_conv"].rearrange("l b j n -> (l b j) n")[ds(l * (2 * NB), 2 * NB), :])\
                  .then_inc(states, 16)
                sp.dma_start(alibi[:].rearrange("p h t -> p (h t)"), io["alibi_prompt"]).then_inc(tables, 16)
                for eng, led, t, out in ((None, A, ktok, "k"), (None, V, vtok, "v")):
                    w = 0 if t is ktok else 1
                    led.wait(sp, f"kv{2 * (nblk - 1) + w}")
                    sp.dma_start(io[f"{out}_prompt"].rearrange("l a (b p) h d -> p (l a b) (h d)", p=P)
                                 [:, ds(l * (nblk - 1), nblk - 1), :], t[:, 0:nblk - 1, :]).then_inc(kv_out, 16)
                    sp.dma_start(io[f"{out}_sample"].rearrange("l b s h d -> (l b s) (h d)")[ds(l * NS, NS), :],
                                 t[0:NS, nblk - 1, :]).then_inc(kv_out, 16)
                A.wait(sp, "conv_rows")
                sp.dma_start(io["conv_prompt"].rearrange("l a j n -> (l a j) n")[ds(l * 2, 2), :], rows_out[0:2, :])\
                  .then_inc(conv_out, 16)
                sp.dma_start(io["conv_sample"].rearrange("l b j n -> (l b j) n")[ds(l * (2 * NB), 2 * NB), :],
                             rows_out[2:2 + 2 * NB, :]).then_inc(conv_out, 16)
                sp.wait_ge(kv_out, 64)
                sp.wait_ge(conv_out, 32)

            @block.tensor
            def _(pe):
                for n, (b, w) in enumerate(kv):
                    m = P if b < nblk - 1 else NS
                    if n >= 4:
                        (A, V)[w].wait(pe, f"kv{n - 4}")
                    for c in range(CB):
                        tr = pe.transpose(slot(n)[0:m, c * P:(c + 1) * P],
                                          proj[:, 16 + 4 * w + c, b * P:b * P + m], self.ident[:])
                    Q.did(tr, f"kv{n}")
                pe.wait_ge(states, 16)
                for c in range(CB):
                    tr = pe.transpose(self.D[0][:, 0, c * 16:(c + 1) * 16], rows_in[:, c * P:(c + 1) * P],
                                      self.ident[0:16, 0:16])
                Q.did(tr, "state")
                V.wait(pe, f"kv{len(kv) - 1}")
                A.wait(pe, "state")
                with pe.Fori(0, HC // 2) as t:
                    Qt.loop(t)

                    def scores(u):
                        g, i = divmod(u, TP // P)
                        if i == 0:
                            Gt.wait(pe, f"staged{g}", t)
                        for m in range(2):
                            k_h = proj[:, ds(t * 2 + (16 + g), 1), 0:keys(u)].rearrange("p a k -> p (a k)")
                            mm = pe.matmul(self.E[u % 2][:, m, 0:keys(u)], qm[g][:, m, i * P:(i + 1) * P], k_h,
                                           start=True, stop=True)
                        Qt.did(mm, f"scores{u}")
                    scores(0)
                    scores(1)
                    for u in range(NU):
                        g, i = divmod(u, TP // P)
                        Vt.wait(pe, f"attn{u}", t)
                        for b in range(i + 1):
                            tr = pe.transpose(bank(self.D[0], u, TP)[:, b * P:(b + 1) * P], S[u % 2][:, 0, b * P:(b + 1) * P],
                                              self.ident[:])
                        Qt.did(tr, f"turn{u}")
                        if u + 2 < NU:
                            scores(u + 2)
                        if u >= 2:
                            At.wait(pe, f"out{u - 2}", t)
                        else:
                            At.wait(pe, f"out{u + NU - 2}", t - 1)
                        At.wait(pe, f"turned{u}", t)
                        for b in range(i + 1):
                            mm = pe.matmul(bank(self.D[1], u, P), vh[g][:, b, :], attn_t[u % 2][:, b * P:(b + 1) * P],
                                           start=(b == 0), stop=(b == i))
                        Qt.did(mm, f"pv{u}")
                Qt.end(HC // 2)
                Gt.wait(pe, "conv1", HC // 2 - 1)
                A.wait(pe, "outs")
                for c in range(CB):
                    tr = pe.transpose(self.D[0][0:18, 1, c * P:(c + 1) * P], last[:, c, :], self.ident[:])
                Q.did(tr, "conv_rows")

            @block.scalar
            def _(act):
                evac_kv(act, 0)
                Q.wait(act, "state")
                A.own(act)
                A.did(act.activation(state[:].rearrange("p c n -> p (c n)"), self.D[0][:, 0, 0:CB * 16], ACT.Copy), "state")
                with act.Fori(0, HC // 2) as t:
                    At.loop(t)

                    def exp(u):
                        Vt.wait(act, f"negmax{u}", t)
                        At.own(act)
                        for m in range(2):
                            e = act.activation(S[u % 2][:, m, 0:keys(u)], S[u % 2][:, m, 0:keys(u)], ACT.Exp,
                                               bias=mx[u % 2][:, 2 + m:3 + m], scale=1.0, accum_out=ex[u % 2][:, m:m + 1])
                        At.did(e, f"exp{u}")

                    def out(u):
                        g, i = divmod(u, TP // P)
                        Qt.wait(act, f"pv{u}", t)
                        At.own(act)
                        At.did(act.activation(y[:, ds(t * 2 + (8 + g), 1), i * P:(i + 1) * P].rearrange("p a t -> p (a t)"),
                                              bank(self.D[1], u, P), ACT.Copy), f"out{u}")
                    exp(0)
                    for u in range(NU):
                        if u + 1 < NU:
                            exp(u + 1)
                        Qt.wait(act, f"turn{u}", t)
                        At.own(act)
                        At.did(act.activation(attn_t[u % 2][:, 0:keys(u)], bank(self.D[0], u, keys(u)), ACT.Copy), f"turned{u}")
                        if u:
                            out(u - 1)
                    out(NU - 1)
                At.end(HC // 2)
                At.wait(act, f"out{NU - 1}", HC // 2 - 1)
                A.did(act.activation(self.junk[:, 14:15], self.eps[:, 0:1], ACT.Copy), "outs")
                Q.wait(act, "conv_rows")
                A.own(act)
                A.did(act.activation(rows_out[:], self.D[0][0:18, 1, :], ACT.Copy), "conv_rows")

            @block.vector
            def _(dve):
                evac_kv(dve, 1)
                dve.wait_ge(self.loads[0], 16)
                with dve.Fori(0, HC // 2) as t:
                    Vt.loop(t)

                    def maxima(u):
                        g, n, s = u // (TP // P), keys(u), S[u % 2]
                        Qt.wait(dve, f"scores{u}", t)
                        if u >= 2:
                            Qt.wait(dve, f"turn{u - 2}", t)
                        else:
                            Qt.wait(dve, f"turn{u + NU - 2}", t - 1)
                        bias = alibi[:, ds(t * 2 + g, 1), TP - n:TP].to_broadcast([P, 2, n])
                        Vt.own(dve)
                        Vt.did(dve.scalar_tensor_tensor(s[:, :, 0:n], self.E[u % 2][:, :, 0:n], 0.125, bias,
                                                        ALU.mult, ALU.add), f"scaled{u}")
                        Vt.own(dve)
                        Vt.did(dve.tensor_reduce(mx[u % 2][:, 0:2], s[:, :, 0:n], AX.X, ALU.max))
                        Vt.own(dve)
                        Vt.did(dve.tensor_scalar(mx[u % 2][:, 2:4], mx[u % 2][:, 0:2], -1.0, None, ALU.mult), f"negmax{u}")
                    maxima(0)
                    for u in range(NU):
                        if u + 1 < NU:
                            maxima(u + 1)
                        n, s, r = keys(u), S[u % 2], ri[u % 2]
                        At.wait(dve, f"exp{u}", t)
                        Vt.own(dve)
                        Vt.did(dve.reciprocal(r[:], ex[u % 2][:]))
                        Vt.own(dve)
                        Vt.did(dve.tensor_scalar(r[:, 1:2], r[:, 1:2], self.nlam[:], None, ALU.mult))
                        Vt.own(dve)
                        Vt.did(dve.tensor_scalar(s[:, 0, 0:n], s[:, 0, 0:n], r[:, 0:1], None, ALU.mult))
                        Vt.own(dve)
                        Vt.did(dve.scalar_tensor_tensor(s[:, 0, 0:n], s[:, 1, 0:n], r[:, 1:2], s[:, 0, 0:n],
                                                        ALU.mult, ALU.add), f"attn{u}")
                Vt.end(HC // 2)

            @block.gpsimd
            def _(pool):
                self.credits(pool, (At, Vt, Qt, Gt))
                G.own(pool)
                G.did(pool.memset(qm[0][:], 0.0))
                G.own(pool)
                G.did(pool.memset(qm[1][:], 0.0))
                G.own(pool)
                G.did(pool.memset(ext[:, 0:2], 0.0), "zero")
                G.own(pool)
                A.wait(pool, "state")
                V.wait(pool, f"kv{len(kv) - 1}")
                for h in range(HC):
                    t, g = divmod(h, 2)
                    flat = lambda j, t=slice(0, TP), r=slice(0, P): proj[r, ds(h + j, 1), t].rearrange("p a t -> p (a t)")
                    if g == 0:
                        Gt.loop(t)
                        for n in range(2):
                            hn = h + n
                            Qt.wait(pool, f"pv{(n + 1) * (TP // P) - 1}", t - 1)
                            Gt.own(pool)
                            Gt.did(pool.tensor_copy(qm[n][0:64, 0, :], proj[0:64, 12 + hn, 0:TP]))
                            Gt.own(pool)
                            Gt.did(pool.tensor_copy(qm[n][64:128, 1, :], proj[64:128, 12 + hn, 0:TP]))
                            Gt.own(pool)
                            Gt.did(pool.tensor_copy(vh[n][:], vtok[:, 0:TP // P, hn * P:(hn + 1) * P]), f"staged{n}")
                    xs = lambda j: flat(j, slice(TP, NT)).rearrange("p (b s) -> p b s", b=NB)
                    Gt.own(pool)
                    Gt.did(pool.tensor_copy(ext_s[:, :, 0:2], state[:, ds(h, 1), :].rearrange("p a (b j) -> p (a b) j", b=NB)))
                    Gt.own(pool)
                    Gt.did(pool.tensor_tensor(ext[:, 2:], flat(8), flat(0), ALU.mult))
                    Gt.own(pool)
                    Gt.did(pool.tensor_tensor(ext_s[:, :, 2:], xs(8), xs(0), ALU.mult))
                    Gt.own(pool)
                    ty, tys = tmp[:, 0:TP], tmp[:, TP:NT].rearrange("p (b s) -> p b s", b=NB)
                    for j in range(3):
                        wj = self.vec[:, ds(h + (cw + CB * j), 1)]
                        o, os = (ty, tys) if j == 0 else (tmp2[:, 0:TP], tmp2[:, TP:NT].rearrange("p (b s) -> p b s", b=NB))
                        Gt.own(pool)
                        Gt.did(pool.tensor_scalar(o, ext[:, j:j + TP], wj, None, ALU.mult))
                        Gt.own(pool)
                        Gt.did(pool.tensor_scalar(os, ext_s[:, :, j:j + TS], wj, None, ALU.mult))
                        Gt.own(pool)
                        if j:
                            Gt.own(pool)
                            Gt.did(pool.tensor_tensor(tmp[:], tmp[:], tmp2[:], ALU.add))
                            Gt.own(pool)
                    Gt.own(pool)
                    Gt.did(pool.tensor_tensor(y[:, ds(h, 1), :].rearrange("p a t -> p (a t)"), tmp[:], flat(4, slice(0, NT)), ALU.mult))
                    Gt.own(pool)
                    Gt.did(pool.tensor_copy(last[:, ds(h, 1), 0:2].rearrange("p a j -> p (a j)"), ext[:, TP:TP + 2]))
                    Gt.own(pool)
                    Gt.did(pool.tensor_copy(last[:, ds(h, 1), 2:18].rearrange("p a (b j) -> p (a b) j", b=NB),
                                            ext_s[:, :, TS:TS + 2]), f"conv{g}")
                    Gt.own(pool)
                    Gt.did(pool.memset(self.junk[:, 15:16], 0.0))
                Gt.end(HC // 2)

    def sample_attention(self, l, proj, y, vtok, tile):
        nc, io = self.nc, self.io
        A, V, Q, G = self.stage_steps("sample")
        At, Vt, Qt, Gt = self.stage_steps("sample", True)
        KB, n_at, NU = 4 * NT, HC * TS, 4
        kt_at = tile.at[0]
        kt = tile("kt", [P, CB, PAST])
        past, new = tile("past", [64, PAST]), tile("new", [64, NB, NS])
        S = tile("S", [64, PAST + NS])
        qs = tile("qs", [P, 80 * CB])
        comb = tile("comb", [64, 2, HC * TS])
        e0, e1 = tile("e0", [64, HC * TS]), tile("e1", [64, HC * TS])
        mx, ex = tile("mx", [64, 2]), tile("ex", [64, 2])
        at = tile("at", [P, (NPG + 1) * HC * TS])
        norm = self.region("subnorm", kt_at)
        sq, rstd = ([norm(f"{n}{i}", [P, NT]) for i in range(2)] for n in ("sq", "rstd"))
        places = []
        for a, b in ((self.r0 + 12 * KB, self.r0 + 24 * KB), (self.r0 + 32 * KB, self.r0 + 36 * KB),
                     (self.r0 + 4 * KB, self.r0 + 8 * KB), (self.ring, self.r0), (tile.at[0], LIMIT)):
            places += range(a, b - 4 * DB + 1, 4 * DB)
        page = [self.place(f"page{i}", [P, DB], a) for i, a in enumerate(places[:4 * NPG])]
        kp, vp = ([page[(2 * w + s) * NPG:(2 * w + s + 1) * NPG] for s in range(2)] for w in range(2))
        tables, kload, vload = self.loads[0], self.loads[1:3], self.loads[3:5]
        who = lambda n: (At, Vt)[n in (5, 7)]

        with nc.Block() as block:
            @block.sync
            def _(sp):
                ck = io["cache_k"].rearrange("l g t m d -> t (l g) (m d)")
                cv = io["cache_v"].rearrange("l g t m d -> t (l g) (m d)")
                pool_n = io["cache_k"].shape[1]
                sp.dma_start(past[:], io["alibi_past"][0:64, :]).then_inc(tables, 16)
                sp.dma_start(new[:].rearrange("p b k -> p (b k)"), io["alibi_new"][0:64, :]).then_inc(tables, 16)
                sp.dma_start(comb[:].rearrange("p b k -> p (b k)"), io["combine"][0:64, :]).then_inc(tables, 16)
                with sp.Fori(0, NB // NU) as t:
                    for u in range(NU):
                        turn, v, s = (t, u - 2, u % 2) if u >= 2 else (t - 1, u + NU - 2, u % 2)
                        pg = [sp.value_load(self.pages[0:1, ds(t * (NU * NPG) + (u * NPG + j), 1)], min_val=0, max_val=pool_n - 1)
                              for j in range(NPG)]
                        for j in range(NPG):
                            if j == 0:
                                Qt.wait(sp, f"kturn{v}_7", turn)
                            sp.dma_start(kp[s][j][:], ck[:, ds(l * pool_n + pg[j], 1), :].rearrange("t a n -> t (a n)"))\
                              .then_inc(kload[s], 16)
                        for j in range(NPG):
                            if j == 0:
                                Qt.wait(sp, f"pv{v}", turn)
                            sp.dma_start(vp[s][j][:], cv[:, ds(l * pool_n + pg[j], 1), :].rearrange("t a n -> t (a n)"))\
                              .then_inc(vload[s], 16)

            @block.gpsimd
            def _(pool):
                self.credits(pool, (At, Vt, Qt, Gt))
                G.own(pool)
                G.did(pool.memset(qs[:], 0.0), "zero")
                G.own(pool)
                qv = qs[:].rearrange("p (c x) -> p c x", c=CB)
                with pool.Fori(0, NB // NU) as t:
                    Gt.loop(t)
                    for u in range(NU):
                        if u:
                            Qt.wait(pool, f"scores{u - 1}", t)
                        else:
                            Qt.wait(pool, f"scores{NU - 1}", t - 1)
                        for hf in range(2):
                            r = slice(64 * hf, 64 * hf + 64)
                            Gt.own(pool)
                            Gt.did(pool.tensor_copy(qv[r, :, hf * TS:hf * TS + TS],
                                                    proj[r, 12:16, ds(t * (NU * TS) + (u * TS + TP), TS)]),
                                   f"q{u}" if hf else None)
                Gt.end(NB // NU)

            @block.tensor
            def _(pe):
                with pe.Fori(0, NB // NU) as t:
                    Qt.loop(t)

                    def turn_keys(u):
                        s = u % 2
                        for n in range(2 * CB):
                            hf, c = divmod(n, CB)
                            if n == 0:
                                pe.wait_ge(kload[s], t * (16 * NPG * NU // 2) + 16 * NPG * (u // 2 + 1))
                            if n >= 2:
                                who(n - 2).wait(pe, f"kt{u}_{n - 2}", t)
                            elif u:
                                who(n + 6).wait(pe, f"kt{u - 1}_{n + 6}", t)
                            else:
                                who(n + 6).wait(pe, f"kt{NU - 1}_{n + 6}", t - 1)
                            for j in range(4):
                                tr = pe.transpose(self.E[n % 2][:, 0, j * P:(j + 1) * P],
                                                  kp[s][hf * 4 + j][:, c * P:(c + 1) * P], self.ident[:])
                            Qt.did(tr, f"kturn{u}_{n}")

                    def scores(u):
                        Gt.wait(pe, f"q{u}", t)
                        At.wait(pe, f"kt{u}_6", t)
                        Vt.wait(pe, f"kt{u}_7", t)
                        for hf in range(2):
                            for c in range(CB):
                                pe.matmul(self.D[0][0:64, hf, :], qs[:, c * 64:(c + 1) * 64], kt[:, c, hf * 512:(hf + 1) * 512],
                                          start=(c == 0), stop=(c == CB - 1))
                        for c in range(CB):
                            mm = pe.matmul(self.D[1][0:64, 0, 0:NS], qs[:, c * 64:(c + 1) * 64], proj[:, 16 + c, TP:NT],
                                           start=(c == 0), stop=(c == CB - 1))
                        Qt.did(mm, f"scores{u}")
                    turn_keys(0)
                    scores(0)
                    for u in range(NU):
                        if u + 1 < NU:
                            turn_keys(u + 1)
                        Vt.wait(pe, f"weights{u}", t)
                        for j in range(NPG + 1):
                            m = P if j < NPG else NS
                            mm = pe.matmul(self.E[0][0:m, 1, j * n_at:(j + 1) * n_at], S[:, j * P:j * P + m], e1[:],
                                           start=True, stop=True)
                        Qt.did(mm, f"turn{u}")
                        pe.wait_ge(vload[u % 2], t * (16 * NPG * NU // 2) + 16 * NPG * (u // 2 + 1))
                        At.wait(pe, f"turned{u}", t)
                        if u:
                            At.wait(pe, f"out{u - 1}", t)
                        else:
                            At.wait(pe, f"out{NU - 1}", t - 1)
                        for h in range(HC):
                            for j in range(NPG + 1):
                                m = P if j < NPG else NS
                                v = vp[u % 2][j][:, h * P:(h + 1) * P] if j < NPG else vtok[0:NS, TP // P, h * P:(h + 1) * P]
                                mm = pe.matmul(self.E[1][:, 1, h * TS:(h + 1) * TS], v,
                                               at[0:m, j * n_at + h * TS:j * n_at + (h + 1) * TS],
                                               start=(j == 0), stop=(j == NPG))
                        Qt.did(mm, f"pv{u}")
                        if u + 1 < NU:
                            scores(u + 1)
                Qt.end(NB // NU)
                for h in range(HC):
                    A.wait(pe, f"sq{h}")
                    for half in range(2):
                        mm = pe.matmul(self.D[h % 2][:, half, 0:NH], self.ones[:], sq[h % 2][:, half * NH:(half + 1) * NH],
                                       start=True, stop=True)
                    Q.did(mm, f"sum{h}")

            @block.scalar
            def _(act):
                with act.Fori(0, NB // NU) as t:
                    At.loop(t)

                    def keys(u, ns):
                        for n in ns:
                            hf, c = divmod(n, CB)
                            Qt.wait(act, f"kturn{u}_{n}", t)
                            if n == 0:
                                if u:
                                    Qt.wait(act, f"scores{u - 1}", t)
                                else:
                                    Qt.wait(act, f"scores{NU - 1}", t - 1)
                            At.own(act)
                            At.did(act.activation(kt[:, c, hf * 512:(hf + 1) * 512], self.E[n % 2][:, 0, :], ACT.Copy),
                                   f"kt{u}_{n}")
                    keys(0, (0, 1, 2, 3, 4, 6))
                    for u in range(NU):
                        if u + 1 < NU:
                            keys(u + 1, (0, 1, 2, 3))
                        Vt.wait(act, f"negmax{u}", t)
                        At.own(act)
                        At.did(act.activation(S[:], S[:], ACT.Exp, bias=mx[:, 1:2], scale=1.0, accum_out=ex[:, 0:1]), f"exp{u}")
                        if u + 1 < NU:
                            keys(u + 1, (4, 6))
                        Qt.wait(act, f"turn{u}", t)
                        act.activation(at[:, 0:NPG * n_at], self.E[0][:, 1, 0:NPG * n_at], ACT.Copy)
                        At.own(act)
                        At.did(act.activation(at[0:NS, NPG * n_at:], self.E[0][0:NS, 1, NPG * n_at:(NPG + 1) * n_at], ACT.Copy),
                               f"turned{u}")
                        Qt.wait(act, f"pv{u}", t)
                        At.own(act)
                        At.did(act.activation(y[:, 8:12, ds(t * (NU * TS) + (u * TS + TP), TS)],
                                              self.E[1][:, 1, 0:HC * TS].rearrange("p (h s) -> p h s", h=HC), ACT.Copy),
                               f"out{u}")
                At.end(NB // NU)
                At.own(act)

                def square(h):
                    if h >= 2:
                        Q.wait(act, f"sum{h - 2}")
                    A.did(act.activation(sq[h % 2][:], y[:, 8 + h, :], ACT.Square), f"sq{h}")
                square(0)
                for h in range(HC):
                    if h + 1 < HC:
                        square(h + 1)
                    Q.wait(act, f"sum{h}")
                    if h >= 2:
                        V.wait(act, f"y{h - 2}")
                    A.did(act.activation(rstd[h % 2][:].rearrange("p (a t) -> p a t", a=2), self.D[h % 2][:, :, 0:NH], ACT.Sqrt,
                                         bias=self.eps[:, 1:2], scale=1.0 / P), f"root{h}")

            @block.vector
            def _(dve):
                dve.wait_ge(tables, 48)
                V.own(dve)
                V.did(dve.scalar_tensor_tensor(e0[:], comb[:, 1, :], self.nlam[0:64, :], comb[:, 0, :], ALU.mult, ALU.add))
                with dve.Fori(0, NB // NU) as t:
                    Vt.loop(t)

                    def keys(u):
                        for n in (5, 7):
                            hf, c = divmod(n, CB)
                            Qt.wait(dve, f"kturn{u}_{n}", t)
                            Vt.own(dve)
                            Vt.did(dve.tensor_copy(kt[:, c, hf * 512:(hf + 1) * 512], self.E[1][:, 0, :]), f"kt{u}_{n}")
                    keys(0)
                    for u in range(NU):
                        Qt.wait(dve, f"scores{u}", t)
                        dve.scalar_tensor_tensor(S[:, 0:PAST].rearrange("p (a k) -> p a k", a=2), self.D[0][0:64, :, :], 0.125,
                                                 past[:].rearrange("p (a k) -> p a k", a=2), ALU.mult, ALU.add)
                        Vt.own(dve)
                        Vt.did(dve.scalar_tensor_tensor(S[:, PAST:], self.D[1][0:64, 0, 0:NS], 0.125,
                                                        new[:, ds(t * NU + u, 1), :].rearrange("p a k -> p (a k)"),
                                                        ALU.mult, ALU.add), f"scaled{u}")
                        Vt.own(dve)
                        Vt.did(dve.tensor_reduce(mx[:, 0:1], S[:], AX.X, ALU.max))
                        Vt.own(dve)
                        Vt.did(dve.tensor_scalar(mx[:, 1:2], mx[:, 0:1], -1.0, None, ALU.mult), f"negmax{u}")
                        if u + 1 < NU:
                            keys(u + 1)
                        At.wait(dve, f"exp{u}", t)
                        Vt.own(dve)
                        Vt.did(dve.reciprocal(ex[:, 1:2], ex[:, 0:1]))
                        Vt.own(dve)
                        Vt.did(dve.tensor_scalar(e1[:], e0[:], ex[:, 1:2], None, ALU.mult), f"weights{u}")
                Vt.end(NB // NU)
                sw = VEC["subln_w"][0]
                for h in range(HC):
                    yh, r = y[:, 8 + h, :], rstd[h % 2][:]
                    A.wait(dve, f"root{h}")
                    V.own(dve)
                    V.did(dve.reciprocal(r, r))
                    V.own(dve)
                    V.did(dve.tensor_tensor(r, r, yh, ALU.mult))
                    V.own(dve)
                    V.did(dve.tensor_scalar(yh, r, self.vec[:, sw:sw + 1], self.one_li[:], ALU.mult, ALU.mult), f"y{h}")

    def token_shift(self, l, z):
        nc, io = self.nc, self.io
        A, V, Q, G = self.stage_steps("shift")
        At, Vt, Qt, Gt = self.stage_steps("shift", True)
        ring = self.region("shift", self.ring)
        rows_in, state = ring("rows_in", [NB, NSHIFT]), ring("state", [P, CZ, NB])
        last, rows_out = ring("last", [P, CZ, 1 + NB]), ring("rows_out", [1 + NB, NSHIFT])
        diff = ring("diff", [P, NT])
        mu0 = VEC["tm_mu"][0]
        banks = [self.E[1][:, 0, :], self.E[1][:, 1, :], self.D[0][:, 0, :], self.D[0][:, 1, :]]

        with nc.Block() as block:
            @block.sync
            def _(sp):
                sp.dma_start(rows_in[:], io["state_shift"].rearrange("l b n -> (l b) n")[ds(l * NB, NB), :])\
                  .then_inc(self.loads[0], 16)
                A.wait(sp, "rows")
                sp.dma_start(io["shift_prompt"].rearrange("l b n -> (l b) n")[ds(l, 1), :], rows_out[0:1, :])\
                  .then_inc(self.stores[0], 16)
                sp.dma_start(io["shift_sample"].rearrange("l b n -> (l b) n")[ds(l * NB, NB), :], rows_out[1:1 + NB, :])\
                  .then_inc(self.stores[0], 16)
                sp.wait_ge(self.stores[0], 32)

            @block.gpsimd
            def _(pool):
                self.credits(pool, (Vt,))
                G.own(pool)
                G.did(pool.tensor_copy(last[:, :, 0:1], z[:, :, TP - 1:TP]))
                G.own(pool)
                G.did(pool.tensor_copy(last[:, :, 1:], z[:, :, TP + TS - 1:NT:TS]), "last")

            @block.tensor
            def _(pe):
                pe.wait_ge(self.loads[0], 16)
                for c in range(CZ):
                    tr = pe.transpose(self.E[0][:, 0, c * NB:(c + 1) * NB], rows_in[:, c * P:(c + 1) * P],
                                      self.ident[0:NB, 0:NB])
                Q.did(tr, "state")
                G.wait(pe, "last")
                for c in range(CZ):
                    tr = pe.transpose(banks[c // 4][0:1 + NB, c % 4 * P:(c % 4 + 1) * P], last[:, c, :], self.ident[:])
                Q.did(tr, "rows")

            @block.scalar
            def _(act):
                Q.wait(act, "state")
                A.own(act)
                A.did(act.activation(state[:].rearrange("p c b -> p (c b)"), self.E[0][:, 0, 0:CZ * NB], ACT.Copy), "state")
                Q.wait(act, "rows")
                for i, bank in enumerate(banks):
                    n = min(512, NSHIFT - i * 512)
                    a = act.activation(rows_out[:, i * 512:i * 512 + n], bank[0:1 + NB, 0:n], ACT.Copy)
                A.did(a, "rows")
                Vt.wait(act, "mixed", CZ - 1)
                act.activation(z[0:64, 3 * CB, :], z[0:64, 3 * CB, :], ACT.Tanh)
                A.own(act)
                A.did(act.activation(z[:, 3 * CB + 1, :], z[:, 3 * CB + 1, :], ACT.Sigmoid), "low")

            @block.vector
            def _(dve):
                A.wait(dve, "state")
                G.wait(dve, "last")
                with dve.Fori(0, CZ) as c:
                    Vt.loop(c)
                    zc = z[:, ds(c, 1), :].rearrange("p a t -> p (a t)")
                    zs, dsm = (t[:, TP:NT].rearrange("p (b s) -> p b s", b=NB) for t in (zc, diff))
                    Vt.own(dve)
                    dve.tensor_tensor(diff[:, 1:TP], zc[:, 0:TP - 1], zc[:, 1:TP], ALU.subtract)
                    dve.tensor_scalar(diff[:, 0:1], zc[:, 0:1], -1.0, None, ALU.mult)
                    dve.tensor_tensor(dsm[:, :, 1:TS], zs[:, :, 0:TS - 1], zs[:, :, 1:TS], ALU.subtract)
                    Vt.own(dve)
                    Vt.did(dve.tensor_tensor(dsm[:, :, 0:1], state[:, ds(c, 1), :].rearrange("p a (b o) -> p (a b) o", o=1),
                                             zs[:, :, 0:1], ALU.subtract))
                    Vt.own(dve)
                    Vt.did(dve.scalar_tensor_tensor(zc, diff[:], self.vec[:, ds(c + mu0, 1)], zc, ALU.mult, ALU.add), "mixed")
                Vt.end(CZ)

    def recurrence(self, l, z, y, tile):
        nc, io = self.nc, self.io
        A, V, Q, G = self.stage_steps("rwkv")
        At, Vt, Qt, Gt = self.stage_steps("rwkv", True)
        E, D = self.E, self.D
        ring = self.region("rwkv_ring", self.ring)
        NG, GW = 3, 3
        temps = tile.at[0]
        kk, kp, a, lw, cum, pinv, pprev, tmp = (tile(n, [P, NT]) for n in
                                                ("kk", "kp", "a", "lw", "cum", "pinv", "pprev", "tmp"))
        over = self.region("rwkv_over", temps)
        T, TT, W1, Lm = (over(n, [P, NW, P]) for n in ("T", "TT", "W1", "Lm"))
        assert over.at[0] <= tile.at[0]
        AR = tile("AR", [P, NW, P + W])
        Bb, Kb, Vb = (tile(n, [P, NW, P]) for n in ("Bb", "Kb", "Vb"))
        GM = tile("GM", [P, NW, 2, P + W])
        TM = ring("TM", [P, NW, 3, P])
        gg, bonus = tile("gg", [P, NT]), tile("bonus", [P, NT])
        pin, yt = tile("pin", [P, NT]), tile("yt", [P, NT])
        sq = ring("sq", [P, NT])
        carry = ring("carry", [P, NT])
        lev = ring("lev", [P, 6, P])
        gmask = ring("gmask", [P, 2, P + W])
        bmask = ring("bmask", [P, NB])
        wa, gup = tile("wa", [P, 2, P]), tile("gup", [P, P])
        S = [tile(f"S{i}", [P, P]) for i in range(2)]
        SP, Xs, Us, so = (tile(n, [P, P]) for n in ("SP", "Xs", "Us", "so"))
        omka = tile("omka", [P, CB])
        low, glow = z[:, 3 * CB, :], z[:, 3 * CB + 1, :]
        tables, wload, sload = self.loads[0:3]
        store = self.stores[0]
        two = lambda t: t.rearrange("p (a t) -> p a t", a=2)
        win = lambda t, r=slice(0, P): t[r, :].rearrange("p (w s) -> p w s", w=NW)
        cmul = -math.exp(-0.5)
        tok_bank = lambda w: D[w % 2][:, 0, 0:3 * P]
        gram_bank = lambda w: E[w % 2][:, 0, 0:2 * (P + W)]
        grp = lambda g: slice(g * GW, (g + 1) * GW)
        inv_bank = lambda g: (E[0][:, 1, 0:GW * P], E[1][:, 1, 0:GW * P], D[0][:, 1, 0:GW * P])[g]
        blocks = lambda t: t.rearrange("p (i n) -> p i n", n=P)

        with nc.Block() as block:
            @block.sync
            def _(sp):
                for n, t in (("carry", carry[:]), ("batch_mask", bmask[:]), ("level_mask", lev[:].rearrange("p j n -> p (j n)")),
                             ("gram_mask", gmask[:].rearrange("p j n -> p (j n)"))):
                    sp.dma_start(t, io[n]).then_inc(tables, 16)
                G.wait(sp, "zero")
                with sp.Fori(0, CB) as p:
                    Vt.wait(sp, "out", p - 1)
                    sp.dma_start(wa[0:64, 0, :], io["w_up_w"].rearrange("l r n -> r l n")[:, ds(l, 1), ds(p * P, P)]
                                 .rearrange("r a n -> r (a n)")).then_inc(wload, 16)
                    sp.dma_start(wa[64:128, 1, :], io["a_up_w"].rearrange("l r n -> r l n")[:, ds(l, 1), ds(p * P, P)]
                                 .rearrange("r a n -> r (a n)")).then_inc(wload, 16)
                    sp.dma_start(gup[:], io["g_up_w"].rearrange("l r n -> r l n")[:, ds(l, 1), ds(p * P, P)]
                                 .rearrange("r a n -> r (a n)")).then_inc(wload, 16)
                    Vt.wait(sp, f"gm{NW - 1}", p)
                    At.wait(sp, f"tm{NW - 1}", p)
                    st = io["state_wkv"].rearrange("l b h v k -> h v (l b) k")
                    so_d = io["wkv_sample"].rearrange("l b h v k -> h v (l b) k")
                    po_d = io["wkv_prompt"].rearrange("l a h v k -> (l a h) v k")
                    for hf in range(2):
                        r = slice(64 * hf, 64 * hf + 64)
                        sp.dma_start(Bb[r, 0:NB, r], st[ds(p * 2 + hf, 1), :, ds(l * NB, NB), :]
                                     .rearrange("a v b k -> (a v) b k")).then_inc(sload, 16)
                    At.wait(sp, "final", p)
                    for hf in range(2):
                        r = slice(64 * hf, 64 * hf + 64)
                        sp.dma_start(po_d[ds(l * (2 * CB) + p * 2 + hf, 1), :, :].rearrange("a v k -> (a v) k"), so[r, r])\
                          .then_inc(store, 16)
                    At.wait(sp, "finals", p)
                    for hf in range(2):
                        r = slice(64 * hf, 64 * hf + 64)
                        sp.dma_start(so_d[ds(p * 2 + hf, 1), :, ds(l * NB, NB), :].rearrange("a v b k -> (a v) b k"),
                                     Bb[r, 0:NB, r]).then_inc(store, 16)
                sp.wait_ge(store, 64 * CB + 64)

            @block.tensor
            def _(pe):
                pe.wait_ge(tables, 64)
                G.wait(pe, "zero")
                with pe.Fori(0, CB) as p:
                    Qt.loop(p)
                    Vt.wait(pe, "out", p - 1)

                    def spread(out, lhs, rhs, name):
                        for half in range(2):
                            mm = pe.matmul(out[:, half, 0:NH], lhs, rhs[:, half * NH:(half + 1) * NH], start=True, stop=True)
                        Qt.did(mm, name)
                    pe.wait_ge(wload, p * 48 + 48)
                    spread(D[0], wa[:, 0, :], low, "w")
                    spread(D[1], wa[:, 1, :], low, "a")
                    spread(E[1], gup[:], glow, "g")
                    At.wait(pe, "kksq", p)
                    spread(E[0], self.halves[:], sq[:], "ss")
                    Gt.wait(pe, "rkr", p)
                    At.wait(pe, "decay", p)
                    spread(D[0], self.halves[:], tmp, "bonus")
                    Gt.wait(pe, "r", p)
                    Vt.wait(pe, "operands", p)
                    Vt.wait(pe, "bonus", p)
                    At.wait(pe, "gg", p)
                    for w in range(NW):
                        if w >= 2:
                            Vt.wait(pe, f"gm{w - 2}", p)
                        for i, b in enumerate((Bb, Kb)):
                            mm = pe.matmul(gram_bank(w)[:, i * (P + W):(i + 1) * (P + W)], b[:, w, :], AR[:, w, :],
                                           start=True, stop=True)
                        Qt.did(mm, f"gram{w}")
                        if w >= 2:
                            At.wait(pe, f"tm{w - 2}", p)
                        for i, b in enumerate((Bb, Kb, Vb)):
                            tr = pe.transpose(tok_bank(w)[:, i * P:(i + 1) * P], b[:, w, :], self.ident[:])
                        Qt.did(tr, f"tok{w}")

                    def turn(j, g):
                        for i in range(GW):
                            tr = pe.transpose(inv_bank(g)[:, i * P:(i + 1) * P], TT[:, g * GW + i, :], self.ident[:])
                        Qt.did(tr, f"tr{j}_{g}")
                    for g in range(NG):
                        Gt.wait(pe, f"tt0_{g}", p)
                        turn(0, g)
                    for j in range(1, 6):
                        for g in range(NG):
                            At.wait(pe, f"t{j - 1}_{g}", p)
                            Gt.wait(pe, f"lm{j}_{g}", p)
                            for i in range(GW):
                                mm = pe.matmul(inv_bank(g)[:, i * P:(i + 1) * P], Lm[:, g * GW + i, :], T[:, g * GW + i, :],
                                               start=True, stop=True)
                            Qt.did(mm, f"w{j}_{g}")
                        for g in range(NG):
                            Vt.wait(pe, f"w{j}_{g}", p)
                            for i in range(GW):
                                mm = pe.matmul(inv_bank(g)[:, i * P:(i + 1) * P], W1[:, g * GW + i, :], TT[:, g * GW + i, :],
                                               start=True, stop=True)
                            Qt.did(mm, f"dt{j}_{g}")
                        for g in range(NG):
                            Vt.wait(pe, f"tt{j}_{g}", p)
                            if j < 5:
                                turn(j, g)
                    At.wait(pe, f"tm{NW - 1}", p)
                    for w in range(NW - 1):
                        s = S[w % 2]
                        if w:
                            Vt.wait(pe, f"s{w}", p)
                        else:
                            Gt.wait(pe, "s0", p)
                        pe.matmul(D[0][:, 0, 0:P], AR[:, w, 0:P], s[:], start=True, stop=False)
                        Qt.did(pe.matmul(D[0][:, 0, 0:P], GM[:, w, 1, 0:P], TM[:, w, 2, :], start=False, stop=True), f"x{w}")
                        At.wait(pe, f"xs{w}", p)
                        Qt.did(pe.matmul(D[0][:, 1, 0:P], TT[:, w, :], Xs[:], start=True, stop=True), f"u{w}")
                        Vt.wait(pe, f"us{w}", p)
                        pe.matmul(D[1][:, 0, 0:P], TM[:, w, 0, :], Us[:], start=True, stop=False)
                        Qt.did(pe.matmul(D[1][:, 0, 0:P], TM[:, w, 1, :], TM[:, w, 2, :], start=False, stop=True), f"st{w}")
                        if w:
                            At.wait(pe, f"yo{w - 1}", p)
                        pe.matmul(D[1][:, 1, 0:W], s[:], AR[:, w, P:], start=True, stop=False)
                        pe.matmul(D[1][:, 1, 0:W], Us[:], GM[:, w, 0, P:], start=False, stop=False)
                        Qt.did(pe.matmul(D[1][:, 1, 0:W], TM[:, w, 2, :], GM[:, w, 1, P:], start=False, stop=True), f"y{w}")
                    w = NW - 1
                    Vt.wait(pe, f"s{w}", p)
                    Qt.did(pe.transpose(E[0][:, 0, 0:P], S[w % 2][:], self.ident[:]), "final")
                    pe.wait_ge(sload, p * 32 + 32)
                    for b in range(NB):
                        tr = pe.transpose(E[1][:, b // 4, b % 4 * P:(b % 4 + 1) * P], Bb[:, b, :], self.ident[:])
                    Qt.did(tr, "sturn")
                    At.wait(pe, "s0s", p)
                    heads = lambda t: t.rearrange("p (h s) -> p h s", h=2)
                    for b in range(NB):
                        t = slice(b * TS, (b + 1) * TS)
                        mm = pe.matmul(heads(D[0][:, 0, 0:P])[:, :, t], Kb[:, b, :], heads(AR[:, w, 0:P])[:, :, t],
                                       start=(b == 0), stop=(b == NB - 1), skip_group_check=True)
                    Qt.did(mm, "from_states")
                    At.wait(pe, "from_states", p)
                    pe.matmul(D[0][:, 1, 0:P], so[:], self.ident[:], start=True, stop=False)
                    Qt.did(pe.matmul(D[0][:, 1, 0:P], GM[:, w, 1, 0:P], TM[:, w, 2, :], start=False, stop=True), f"x{w}")
                    At.wait(pe, f"xs{w}", p)
                    Qt.did(pe.matmul(D[1][:, 0, 0:P], TT[:, w, :], Xs[:], start=True, stop=True), f"u{w}")
                    At.wait(pe, f"yo{w - 1}", p)
                    Vt.wait(pe, f"us{w}", p)
                    for b in range(NB):
                        t = slice(b * TS, (b + 1) * TS)
                        pe.matmul(D[1][:, 1, t], Kb[:, b, :], AR[:, w, P + b * TS:P + (b + 1) * TS],
                                  start=(b == 0), stop=False, skip_group_check=True)
                    pe.matmul(D[1][:, 1, 0:W], Us[:], GM[:, w, 0, P:], start=False, stop=False, skip_group_check=True)
                    Qt.did(pe.matmul(D[1][:, 1, 0:W], TM[:, w, 2, :], GM[:, w, 1, P:], start=False, stop=True,
                                     skip_group_check=True), f"y{w}")
                    Vt.wait(pe, "masked", p)
                    At.wait(pe, "final", p)
                    for half in range(2):
                        r = slice(4 * half, 4 * half + 4)
                        pe.matmul(E[0][:, half, :], TM[:, w, 0, :], Bb[:, r, :].rearrange("p b n -> p (b n)"),
                                  start=True, stop=False)
                        mm = pe.matmul(E[0][:, half, :], TM[:, w, 1, :], Vb[:, r, :].rearrange("p b n -> p (b n)"),
                                       start=False, stop=True)
                    Qt.did(mm, f"st{w}")
                    Vt.wait(pe, "snew", p)
                    for b in range(NB):
                        tr = pe.transpose(E[1][:, b // 4, b % 4 * P:(b % 4 + 1) * P], Kb[:, b, :], self.ident[:])
                    Qt.did(tr, "finals")
                    At.wait(pe, f"yo{w}", p)
                    spread(D[0], self.halves[:], yt[:], "mean")
                    At.wait(pe, "ysq", p)
                    spread(D[1], self.halves[:], sq[:], "var")
                Qt.end(CB)

            @block.scalar
            def _(act):
                with act.Fori(0, CB) as p:
                    At.loop(p)
                    Vt.wait(act, "out", p - 1)
                    v0 = lambda n: self.vec[:, ds(p + VEC[n][0], 1)]
                    Qt.wait(act, "w", p)
                    At.own(act)
                    At.did(act.activation(two(lw[:]), D[0][:, :, 0:NH], ACT.Sigmoid, bias=v0("w0"), scale=1.0), "decay")
                    Qt.wait(act, "a", p)
                    At.own(act)
                    At.did(act.activation(two(a[:]), D[1][:, :, 0:NH], ACT.Sigmoid, bias=v0("a0"), scale=1.0), "a")
                    Vt.wait(act, "kk", p)
                    At.own(act)
                    At.did(act.activation(sq[:], kk[:], ACT.Square), "kksq")
                    Qt.wait(act, "g", p)
                    At.own(act)
                    At.did(act.activation(two(gg[:]), E[1][:, :, 0:NH], ACT.Copy), "gg")
                    Vt.wait(act, "ssmax", p)
                    At.own(act)
                    At.did(act.activation(pprev[:], pprev[:], ACT.Sqrt), "ssroot")
                    Vt.wait(act, "cum", p)
                    act.activation(pin[:], cum[:], ACT.Exp)
                    At.own(act)
                    At.did(act.activation(pinv[:], cum[:], ACT.Exp, scale=-1.0), "pinv")
                    Vt.wait(act, "rss", p)
                    At.own(act)
                    At.did(act.activation(pprev[:], lw[:], ACT.Exp), "pprev")
                    for w in range(NW):
                        Qt.wait(act, f"tok{w}", p)
                        At.own(act)
                        At.did(act.activation(TM[:, w].rearrange("p i n -> p (i n)"), tok_bank(w), ACT.Copy), f"tm{w}")
                    for j in range(5):
                        for g in range(NG):
                            Qt.wait(act, f"tr{j}_{g}", p)
                            At.own(act)
                            At.did(act.activation(T[:, grp(g), :], blocks(inv_bank(g)), ACT.Copy), f"t{j}_{g}")
                    for w in range(NW - 1):
                        Qt.wait(act, f"x{w}", p)
                        At.own(act)
                        At.did(act.activation(Xs[:], D[0][:, 0, 0:P], ACT.Copy), f"xs{w}")
                        Qt.wait(act, f"y{w}", p)
                        At.own(act)
                        At.did(act.activation(yt[:, w * W:(w + 1) * W], D[1][:, 1, 0:W], ACT.Copy), f"yo{w}")
                    w = NW - 1
                    Qt.wait(act, "final", p)
                    act.wait_ge(store, p * 64 + 64)
                    At.own(act)
                    At.did(act.activation(so[:], E[0][:, 0, 0:P], ACT.Copy), "final")
                    Qt.wait(act, "sturn", p)
                    At.own(act)
                    At.did(act.activation(Kb[:, 0:NB, :].rearrange("p (a b) n -> p a (b n)", a=2), E[1][:], ACT.Copy), "s0s")
                    Qt.wait(act, "from_states", p)
                    act.wait_ge(store, p * 64 + 96)
                    At.own(act)
                    At.did(act.activation(so[:], D[0][:, 0, 0:P], ACT.Copy), "from_states")
                    Qt.wait(act, f"x{w}", p)
                    At.own(act)
                    At.did(act.activation(Xs[:], D[0][:, 1, 0:P], ACT.Copy), f"xs{w}")
                    Qt.wait(act, f"y{w}", p)
                    At.own(act)
                    At.did(act.activation(yt[:, w * W:(w + 1) * W], D[1][:, 1, 0:W], ACT.Copy), f"yo{w}")
                    Qt.wait(act, "finals", p)
                    At.own(act)
                    At.did(act.activation(Bb[:, 0:NB, :].rearrange("p (a b) n -> p a (b n)", a=2), E[1][:], ACT.Copy), "finals")
                    Vt.wait(act, "centred", p)
                    At.own(act)
                    At.did(act.activation(sq[:], yt[:], ACT.Square), "ysq")
                    Qt.wait(act, "var", p)
                    At.own(act)
                    At.did(act.activation(two(pin[:]), D[1][:, :, 0:NH], ACT.Sqrt, bias=self.eps[:, 2:3], scale=1.0 / W), "ydev")
                At.end(CB)

            @block.vector
            def _(dve):
                dve.wait_ge(tables, 64)
                ka0 = VEC["k_a"][0]
                V.own(dve)
                V.did(dve.tensor_scalar(omka[:], self.vec[:, ka0:ka0 + CB], -1.0, 1.0, ALU.mult, ALU.add), "omka")
                G.wait(dve, "zero")
                with dve.Fori(0, CB) as p:
                    Vt.loop(p)
                    v0 = lambda n: self.vec[:, ds(p + VEC[n][0], 1)]
                    zr = lambda i, r=slice(0, P): z[r, ds(p + i * CB, 1), :].rearrange("p a t -> p (a t)")
                    Vt.own(dve)
                    Vt.did(dve.tensor_scalar(kk[:], zr(1), v0("k_k"), None, ALU.mult), "kk")
                    At.wait(dve, "decay", p)
                    Vt.own(dve)
                    Vt.did(dve.tensor_scalar(lw[:], lw[:], cmul, None, ALU.mult))
                    Vt.own(dve)
                    Vt.did(dve.tensor_tensor_scan(cum[:], carry[:], lw[:], 0.0, ALU.mult, ALU.add), "cum")
                    Vt.own(dve)
                    Qt.wait(dve, "ss", p)
                    Vt.did(dve.tensor_scalar(two(pprev[:]), E[0][:, :, 0:NH], 1e-24, None, ALU.max), "ssmax")
                    Vt.own(dve)
                    Vt.did(dve.tensor_tensor(lw[:], cum[:], lw[:], ALU.subtract), "before")
                    At.wait(dve, "ssroot", p)
                    Vt.own(dve)
                    Vt.did(dve.reciprocal(sq[:], pprev[:]), "rss")
                    Vt.own(dve)
                    Vt.did(dve.tensor_tensor(kk[:], kk[:], sq[:], ALU.mult), "kkn")
                    Vt.own(dve)
                    Qt.wait(dve, "bonus", p)
                    Vt.did(dve.tensor_tensor(two(bonus[:]), D[0][:, :, 0:NH], two(zr(2)), ALU.mult), "bonus")
                    At.wait(dve, "pprev", p)
                    for hf in range(2):
                        r = slice(64 * hf, 64 * hf + 64)
                        dve.scalar_tensor_tensor(AR[r, :, r], win(kk, r), -1.0, win(pprev, r), ALU.mult, ALU.mult)
                    Gt.wait(dve, "kp", p)
                    for hf in range(2):
                        r = slice(64 * hf, 64 * hf + 64)
                        o = dve.tensor_tensor(Kb[r, :, r], win(kp, r), win(pinv, r), ALU.mult)
                    Vt.did(o)
                    Vt.own(dve)
                    Vt.did(dve.tensor_tensor(kk[:], kk[:], a[:], ALU.mult))
                    Vt.own(dve)
                    dve.wait_ge(store, p * 64 + 64)
                    for hf in range(2):
                        r = slice(64 * hf, 64 * hf + 64)
                        o = dve.tensor_tensor(Bb[r, :, r], win(kk, r), win(pinv, r), ALU.mult)
                    Vt.did(o, "operands")
                    for w in range(NW):
                        Qt.wait(dve, f"gram{w}", p)
                        m = gmask[:, w // (NW - 1):w // (NW - 1) + 1, :].to_broadcast([P, 2, P + W])
                        Vt.own(dve)
                        Vt.did(dve.tensor_tensor(GM[:, w], gram_bank(w).rearrange("p (i n) -> p i n", i=2), m, ALU.mult), f"gm{w}")
                    for j in range(1, 6):
                        for g in range(NG):
                            Qt.wait(dve, f"w{j}_{g}", p)
                            Vt.own(dve)
                            Vt.did(dve.tensor_copy(W1[:, grp(g), :], blocks(inv_bank(g))), f"w{j}_{g}")
                        for g in range(NG):
                            Qt.wait(dve, f"dt{j}_{g}", p)
                            if j > 1:
                                Vt.own(dve)
                            Vt.did(dve.tensor_tensor(TT[:, grp(g), :], TT[:, grp(g), :], blocks(inv_bank(g)), ALU.add), f"tt{j}_{g}")
                    for w in range(NW - 1):
                        Qt.wait(dve, f"u{w}", p)
                        Vt.own(dve)
                        Vt.did(dve.tensor_copy(Us[:], D[0][:, 1, 0:P]), f"us{w}")
                        Qt.wait(dve, f"st{w}", p)
                        Gt.wait(dve, f"sp{w}", p)
                        e = w * W + W - 1
                        Vt.own(dve)
                        Vt.did(dve.scalar_tensor_tensor(S[(w + 1) % 2][:], D[1][:, 0, 0:P], pin[:, e:e + 1], SP[:],
                                                        ALU.mult, ALU.add), f"s{w + 1}")
                        Qt.wait(dve, f"y{w}", p)
                    w = NW - 1
                    Qt.wait(dve, f"u{w}", p)
                    Vt.own(dve)
                    Vt.did(dve.tensor_copy(Us[:], D[1][:, 0, 0:P]), f"us{w}")
                    Vt.own(dve)
                    bm = bmask[:].unsqueeze(2).to_broadcast([P, NB, P])
                    dve.tensor_tensor(Bb[:, 0:NB, :], Us[:].unsqueeze(1).to_broadcast([P, NB, P]), bm, ALU.mult)
                    Vt.own(dve)
                    Vt.did(dve.tensor_tensor(Vb[:, 0:NB, :], TM[:, w, 2:3, :].to_broadcast([P, NB, P]), bm, ALU.mult), "masked")
                    Qt.wait(dve, f"st{w}", p)
                    kv = Kb[:, 0:NB, :].rearrange("p (a b) n -> p a (b n)", a=2)
                    Vt.own(dve)
                    Vt.did(dve.tensor_tensor(kv, kv, E[0][:], ALU.add))
                    Vt.own(dve)
                    pe_ = pin[:, TP + TS - 1:NT:TS].unsqueeze(2).to_broadcast([P, NB, P])
                    Vt.own(dve)
                    Vt.did(dve.tensor_tensor(Kb[:, 0:NB, :], Kb[:, 0:NB, :], pe_, ALU.mult), "snew")
                    Qt.wait(dve, "mean", p)
                    Vt.own(dve)
                    Vt.did(dve.scalar_tensor_tensor(two(yt[:]), D[0][:, :, 0:NH], -1.0 / W, two(yt[:]), ALU.mult, ALU.add), "centred")
                    At.wait(dve, "ydev", p)
                    Vt.own(dve)
                    Vt.did(dve.reciprocal(pin[:], pin[:]))
                    Vt.own(dve)
                    Vt.did(dve.tensor_tensor(yt[:], yt[:], pin[:], ALU.mult))
                    Vt.own(dve)
                    Vt.did(dve.tensor_scalar(yt[:], yt[:], v0("lnx_w"), v0("lnx_b"), ALU.mult, ALU.add))
                    Vt.own(dve)
                    Vt.did(dve.tensor_tensor(yt[:], yt[:], bonus[:], ALU.add))
                    Vt.own(dve)
                    At.wait(dve, "finals", p)
                    Vt.did(dve.tensor_tensor(y[:, ds(p + 4, 1), :].rearrange("p a t -> p (a t)"), yt[:], gg[:], ALU.mult), "out")
                Vt.end(CB)

            @block.gpsimd
            def _(pool):
                self.credits(pool, (At, Vt, Qt, Gt))
                pool.memset(self.junk[:, 14:15], 0.0).then_inc(store, 64)
                for t in (AR, Bb, Kb, Vb, wa):
                    G.own(pool)
                    G.did(pool.memset(t[:], 0.0), "zero" if t is wa else None)
                G.own(pool)
                pool.wait_ge(tables, 64)
                V.wait(pool, "omka")
                for p in range(CB):
                    Gt.loop(p)
                    v0 = lambda n: self.vec[:, ds(p + VEC[n][0], 1)]
                    zr = lambda i, r=slice(0, P): z[r, ds(p + i * CB, 1), :].rearrange("p a t -> p (a t)")
                    Vt.wait(pool, "out", p - 1)
                    for hf in range(2):
                        r = slice(64 * hf, 64 * hf + 64)
                        Gt.own(pool)
                        Gt.did(pool.tensor_copy(Vb[r, :, r], zr(2, r).rearrange("p (w s) -> p w s", w=NW)))
                    Gt.own(pool)
                    Gt.did(pool.memset(S[0][:], 0.0), "s0")
                    At.wait(pool, "a", p)
                    Gt.own(pool)
                    Gt.did(pool.tensor_scalar(kp[:], a[:], v0("k_a"), omka[:, ds(p, 1)], ALU.mult, ALU.add))
                    Gt.own(pool)
                    Gt.did(pool.tensor_tensor(kp[:], kp[:], zr(1), ALU.mult), "kp")
                    Gt.own(pool)
                    Gt.did(pool.tensor_tensor(tmp[:], kp[:], zr(0), ALU.mult))
                    Gt.own(pool)
                    Gt.did(pool.tensor_scalar(tmp[:], tmp[:], v0("r_k"), None, ALU.mult), "rkr")
                    At.wait(pool, "pinv", p)
                    Gt.own(pool)
                    Gt.did(pool.tensor_tensor(AR[:, :, P:], zr(0).rearrange("p (w s) -> p w s", w=NW), win(pin[:]), ALU.mult), "r")
                    Vt.wait(pool, "operands", p)
                    Qt.wait(pool, "bonus", p)
                    for g in range(NG):
                        Vt.wait(pool, f"gm{g * GW + GW - 1}", p)
                        LT = GM[:, grp(g), 0, 0:P]
                        m = lambda j: lev[:, j:j + 1, :].to_broadcast([P, GW, P])
                        Gt.own(pool)
                        Gt.did(pool.tensor_tensor(TT[:, grp(g), :], LT, m(0), ALU.mult))
                        Gt.own(pool)
                        Gt.did(pool.tensor_tensor(TT[:, grp(g), :], TT[:, grp(g), :],
                                                  self.ident[:].unsqueeze(1).to_broadcast([P, GW, P]), ALU.add), f"tt0_{g}")
                        Gt.own(pool)
                        Gt.did(pool.tensor_tensor(Lm[:, grp(g), :], LT, m(1), ALU.mult), f"lm1_{g}")
                    for j in range(2, 6):
                        for g in range(NG):
                            LT = GM[:, grp(g), 0, 0:P]
                            m = lev[:, j:j + 1, :].to_broadcast([P, GW, P])
                            Qt.wait(pool, f"w{j - 1}_{g}", p)
                            Gt.own(pool)
                            Gt.did(pool.tensor_tensor(Lm[:, grp(g), :], LT, m, ALU.mult), f"lm{j}_{g}")
                    for w in range(NW - 1):
                        e = w * W + W - 1
                        if w:
                            Vt.wait(pool, f"s{w}", p)
                        else:
                            Gt.own(pool)
                        Gt.did(pool.tensor_scalar(SP[:], S[w % 2][:], pin[:, e:e + 1], None, ALU.mult), f"sp{w}")
                Gt.end(CB)

    def split_branches(self, y, y_hi, y_lo):
        A, V, Q, G = self.stage_steps("splity")
        with self.nc.Block() as block:
            @block.scalar
            def _(act):
                for c in range(12):
                    A.own(act)
                    A.did(act.activation(y_hi[:, c, :], y[:, c, :], ACT.Copy), f"hi{c}")

            @block.vector
            def _(dve):
                for c in range(12):
                    A.wait(dve, f"hi{c}")
                    V.own(dve)
                    V.did(dve.tensor_tensor(y_lo[:, c, :], y[:, c, :], y_hi[:, c, :].bitcast(F32), ALU.subtract), f"lo{c}")

    def merge(self, l, y_hi, y_lo, m_hi, m_lo, tile):
        nc, io, ev = self.nc, self.io, self.evac
        gates = [tile(f"gate{i}", [P, NT]) for i in range(3)]
        part, acc = tile("part", [P, NT]), tile("acc", [P, NT])
        win = io["w_in"].rearrange("l (c p) n -> p (l c) n", p=P)
        wb = [io[f"w_branch_{b}"].rearrange("l (c p) n -> p (l c) n", p=P) for b in "abc"]
        wo = io["w_out"].rearrange("l (c p) n -> p (l c) n", p=P)
        two = lambda t: t.rearrange("p (a t) -> p a t", a=2)
        GP = 3 * KD

        with nc.Block() as block:
            @block.gpsimd
            def _(pool):
                self.credits(pool)

            @block.sync
            def _(sp):
                with sp.Fori(0, KD) as c:
                    for j in range(6):
                        src = win[:, ds(l * KD, KD), ds((c + (COL_G + KD * j)) * P, P)] if j < 3 else \
                            wb[j - 3][:, ds(l * CB, CB), ds(c * P, P)]
                        self.load_w(sp, c * 3 + j // 2, j % 2, src)
                with sp.Fori(0, KD // 2) as c:
                    for s in range(2):
                        self.load_w(sp, c + GP, s, wo[:, ds(l * KD, KD), ds((c * 2 + s) * P, P)])

            @block.tensor
            def _(pe):
                with pe.Fori(0, KD) as c:
                    for j in range(6):
                        k, s = c * 3 + j // 2, j % 2
                        use = (s, c * 3 + (j // 2 + 1))
                        if j < 3:
                            self.products(pe, k, s, self.h_hi, self.h_lo, self.D[s], use)
                        else:
                            r = slice((j - 3) * CB, (j - 2) * CB)
                            self.products(pe, k, s, y_hi[:, r, :], y_lo[:, r, :], self.D[s], use)
                pe.wait_ge(self.part_lo, KD + 1)
                with pe.Fori(0, KD // 2) as c:
                    for s in range(2):
                        self.products(pe, c + GP, s, m_hi, m_lo, self.D[s], (s, c + (GP + 1)))

            @block.scalar
            def _(act):
                def gate(i, j, c, s):
                    if 2 * j + s < 3:
                        act.wait_ge(self.mm_done, i * 2 + (s + 3))
                        act.activation(two(gates[2 * j + s][:]), self.D[s][:, :, 0:NH], ACT.Sigmoid).then_inc(ev[s], 1)
                    elif j == 2 and s == 1:
                        act.wait_ge(self.dve_turns, c * 2 + 2)
                        act.activation(m_hi[:, ds(c, 1), :].rearrange("p a t -> p (a t)"), acc[:], ACT.Copy)\
                           .then_inc(self.part_hi, 1)
                self.chase(act, lambda k, s: self.split_hi(act, k, s), [(GP, 3, gate), (KD // 2, 1, lambda i, j, c, s: None)])

            @block.vector
            def _(dve):
                def branch(i, j, c, s):
                    n = i * 2
                    if j == 1 and s == 1:
                        dve.wait_ge(self.mm_done, n + 4)
                        dve.wait_ge(ev[0], c * 3 + 2)
                        dve.wait_ge(self.part_lo, c + 1)
                        dve.tensor_tensor(two(acc[:]), self.D[1][:, :, 0:NH], two(gates[0][:]), ALU.mult).then_inc(ev[1], 1)
                    if j == 2 and s == 0:
                        dve.wait_ge(self.mm_done, n + 3)
                        dve.wait_ge(ev[1], c * 3 + 3)
                        dve.tensor_tensor(two(part[:]), self.D[0][:, :, 0:NH], two(gates[1][:]), ALU.mult).then_inc(ev[0], 1)
                        dve.wait_ge(ev[0], c * 3 + 4)
                        dve.tensor_tensor(acc[:], acc[:], part[:], ALU.add).then_inc(self.dve_turns, 1)
                    if j == 2 and s == 1:
                        dve.wait_ge(self.mm_done, n + 4)
                        dve.wait_ge(self.dve_turns, c * 2 + 1)
                        dve.tensor_tensor(two(part[:]), self.D[1][:, :, 0:NH], two(gates[2][:]), ALU.mult).then_inc(ev[1], 1)
                        dve.wait_ge(ev[1], c * 3 + 4)
                        dve.tensor_tensor(acc[:], acc[:], part[:], ALU.add).then_inc(self.dve_turns, 1)
                        dve.wait_ge(self.part_hi, c + 1)
                        dve.tensor_tensor(m_lo[:, ds(c, 1), :].rearrange("p a t -> p (a t)"), acc[:],
                                          m_hi[:, ds(c, 1), :].rearrange("p a t -> p (a t)").bitcast(F32),
                                          ALU.subtract).then_inc(self.part_lo, 1)

                def add_out(i, j, c, s):
                    dve.wait_ge(self.mm_done, i * 2 + (2 * GP + s + 3))
                    xs = self.x[:, ds(i * 2 + s, 1), :].rearrange("p a (b t) -> p (a b) t", b=2)
                    dve.tensor_tensor(xs, self.D[s][:, :, 0:NH], xs, ALU.add).then_inc(ev[s], 1)
                self.chase(dve, lambda k, s: self.split_lo(dve, k, s), [(GP, 3, branch), (KD // 2, 1, add_out)])

    def finish(self):
        nc, io = self.nc, self.io
        tile = self.region("final", self.r0)
        self.norm_tiles(tile)
        A, V, Q, G = self.stage_steps("final")
        out = tile("out", [P, TP // P + 1, D])
        nblk = TP // P + 1
        with nc.Block() as block:
            @block.tensor
            def _(pe):
                self.norm_pe(pe, A, Q)
                V.wait(pe, "y")
                for b in range(nblk):
                    m = P if b < nblk - 1 else NS
                    if b >= 2:
                        (A, V)[b % 2].wait(pe, f"out{b - 2}")
                    for c in range(KD):
                        tr = pe.transpose(self.D[b % 2][0:m, c // 4, c % 4 * P:(c % 4 + 1) * P],
                                          self.x[:, c, b * P:b * P + m], self.ident[:])
                    Q.did(tr, f"turn{b}")

            @block.scalar
            def _(act):
                self.norm_act(act, A, V, Q)
                for b in range(0, nblk, 2):
                    m = P if b < nblk - 1 else NS
                    Q.wait(act, f"turn{b}")
                    A.own(act)
                    A.did(act.activation(out[0:m, b, :].rearrange("p (a n) -> p a n", a=2), self.D[0][0:m], ACT.Copy), f"out{b}")

            @block.vector
            def _(dve):
                A.wait(dve, "root")
                V.own(dve)
                V.did(dve.reciprocal(self.rstd[:], self.rstd[:]))
                V.own(dve)
                for c in range(KD):
                    o = dve.scalar_tensor_tensor(self.x[:, c, :], self.x[:, c, :], self.vec_all[:, L - 1, NVEC + c:NVEC + c + 1],
                                                 self.rstd[:], ALU.mult, ALU.mult)
                V.did(o, "y")
                for b in range(1, nblk, 2):
                    Q.wait(dve, f"turn{b}")
                    V.own(dve)
                    V.did(dve.tensor_copy(out[:, b, :].rearrange("p (a n) -> p a n", a=2), self.D[1][:]), f"out{b}")

            @block.sync
            def _(sp):
                A.wait(sp, f"out{nblk - 1}")
                V.wait(sp, f"out{nblk - 2}")
                sp.dma_start(io["y_prompt"].rearrange("a (b p) d -> p (a b) d", p=P), out[:, 0:nblk - 1, :])\
                  .then_inc(self.stores[0], 16)
                sp.dma_start(io["y_sample"].rearrange("b s d -> (b s) d"), out[0:NS, nblk - 1, :]).then_inc(self.stores[0], 16)
                sp.wait_ge(self.stores[0], 32)

    def build(self):
        nc = self.nc
        KB = 4 * NT
        y = self.place("y", [P, 12, NT], self.r0)
        proj = self.place("proj", [P, 24, NT], self.r0 + 12 * KB)
        z = self.place("z", [P, CZ, NT], self.r0 + 12 * KB)
        m_hi = self.place("m_hi", [P, KD, NT], self.r0, F32R)
        m_lo = self.place("m_lo", [P, KD, NT], self.r0 + KD * KB, F32R)
        y_hi = self.place("y_hi", [P, 12, NT], self.r0 + 16 * KB, F32R)
        y_lo = self.place("y_lo", [P, 12, NT], self.r0 + 28 * KB, F32R)
        self.setup()
        with nc.Fori(0, L) as l:
            self.barrier()
            self.layer_vectors(l)
            self.barrier()
            self.ffn(l, "ffn1")
            self.barrier()
            tile = self.region("proj", self.r0 + 36 * KB)
            self.norm_tiles(tile)
            self.project(l, "proj", [(0, 12), (COL_Q, 12)], proj, True)
            self.barrier()
            tile = self.region("attn", self.r0 + 36 * KB)
            vtok = tile("vtok", [P, TP // P + 1, DB])
            after = tile.at[0]
            self.prompt_attention(l, proj, y, vtok, tile)
            self.barrier()
            self.sample_attention(l, proj, y, vtok, self.region("sample", after))
            self.barrier()
            self.project(l, "z", [(COL_Z, CZ)], z, False)
            self.barrier()
            self.token_shift(l, z)
            self.barrier()
            self.recurrence(l, z, y, self.region("rwkv", self.r0 + (12 + CZ) * KB))
            self.barrier()
            self.split_branches(y, y_hi, y_lo)
            self.barrier()
            self.merge(l, y_hi, y_lo, m_hi, m_lo, self.region("merge", self.r0 + 40 * KB))
            self.barrier()
            self.ffn(l, "ffn2")
        self.barrier()
        self.finish()


def program(make_nc, io_of):
    book = {}
    for _ in range(2):
        nc = make_nc()
        io = io_of(nc)
        with ExitStack() as ctx:
            core = Core(nc, ctx, io, book)
            core.build()
            assert _ == 0 or core.new == book
        book = core.new
    return nc


_INS = ['x_prompt', 'x_sample', 'cache_k', 'cache_v', 'state_wkv', 'state_shift', 'state_conv', 'page_table',
        'ffn1_norm', 'ffn1_w_gate', 'ffn1_w_up', 'ffn1_w_down', 'mix_norm', 'w_in', 'conv_w', 'tm_mu',
        'w_up_w', 'w0', 'a_up_w', 'a0', 'g_up_w', 'k_k', 'k_a', 'r_k', 'lnx_w', 'lnx_b',
        'lam_q1', 'lam_k1', 'lam_q2', 'lam_k2', 'subln_w', 'w_branch_a', 'w_branch_b', 'w_branch_c', 'w_out',
        'ffn2_norm', 'ffn2_w_gate', 'ffn2_w_up', 'ffn2_w_down', 'final_norm']
_OUTS = [('y_prompt', (1, TP, D)), ('y_sample', (NB, TS, D)),
         ('k_prompt', (L, 1, TP, MAPS, 64)), ('v_prompt', (L, 1, TP, HC, P)),
         ('k_sample', (L, NB, TS, MAPS, 64)), ('v_sample', (L, NB, TS, HC, P)),
         ('wkv_prompt', (L, 1, 8, 64, 64)), ('wkv_sample', (L, NB, 8, 64, 64)),
         ('shift_prompt', (L, 1, NSHIFT)), ('shift_sample', (L, NB, NSHIFT)),
         ('conv_prompt', (L, 1, 2, DB)), ('conv_sample', (L, NB, 2, DB))]


def kernel(**inputs):
    import concourse.bacc as _bacc
    from concourse.bass_utils import run_bass_kernel_spmd as _run

    arrays = {n: np.ascontiguousarray(inputs[n]) for n in _INS}
    arrays.update(shape_constants())

    def io_of(nc):
        io = {n: nc.dram_tensor(f"in_{n}_dram", a.shape, mybir.dt.from_np(a.dtype), kind="ExternalInput").ap()
              for n, a in arrays.items()}
        io.update({n: nc.dram_tensor(f"out_{n}_dram", shape, F32, kind="ExternalOutput").ap() for n, shape in _OUTS})
        return io
    nc = program(lambda: _bacc.Bacc("TRN2", target_bir_lowering=False, num_devices=1), io_of)
    r = _run(nc, [{f"in_{n}_dram": a for n, a in arrays.items()}], core_ids=[0])
    return tuple(r.results[0][f"out_{n}_dram"] for n, _ in _OUTS)
```

```python
import math
from contextlib import ExitStack

import numpy as np
import concourse.bass as bass
from concourse import mybir

F32 = mybir.dt.float32
F32R = mybir.dt.float32r
I32 = mybir.dt.int32
ALU = mybir.AluOpType
ACT = mybir.ActivationFunctionType
AX = mybir.AxisListType
ds = bass.ds

P = 128
L = 2
D = 1024
KD = D // P
FF = 2816
KF = FF // P
HF = KF // 2
TP, NB, TS = 512, 8, 8
NS = NB * TS
NT = TP + NS
NH = NT // 2
DB = 512
CB = DB // P
NSHIFT = 3 * DB + 256
CZ = NSHIFT // P
N_IN = 3 * DB + NSHIFT + 3 * DB + 3 * D
COL_Z = 3 * DB // P
COL_Q = COL_Z + CZ
COL_G = COL_Q + 3 * CB
PAST, PAGE = 1024, 128
NPG = PAST // PAGE
HC, MAPS = 4, 8
W = 64
NW = NT // W
NEG = -1.0e30
BASE, LIMIT = 16512, 229344
VEC = {}
_at = 0
for _n, _c in (("ffn1_norm", KD), ("mix_norm", KD), ("ffn2_norm", KD), ("tm_mu", CZ), ("w0", CB), ("a0", CB),
               ("k_k", CB), ("k_a", CB), ("r_k", CB), ("lnx_w", CB), ("lnx_b", CB), ("conv_w", 3 * CB), ("subln_w", 1)):
    VEC[_n] = (_at, _c)
    _at += _c
NVEC = _at


def shape_constants():
    p = np.arange(P)
    half = p // W
    s64 = p % W
    same = (half[:, None] == half[None, :])
    c = {}
    c["ident"] = np.eye(P)
    c["halves"] = same
    slopes = np.array([2.0 ** (-8.0 * (h + 1) / HC) for h in range(HC)])
    t = np.arange(TP)
    dist = p[:, None] - (t[None, :] - (TP - P))
    c["alibi_prompt"] = np.stack([np.where(dist >= 0, -s * dist, NEG) for s in slopes], 1).reshape(P, -1)
    row = np.arange(P)
    m, q = (row % 64) // TS, row % TS
    sl = slopes[m // 2]
    c["alibi_past"] = -sl[:, None] * (PAST + q[:, None] - np.arange(PAST)[None, :])
    kb, ks = np.arange(NS) // TS, np.arange(NS) % TS
    new = np.full((P, NB, NS), NEG)
    for b in range(NB):
        ok = (kb[None, :] == b) & (ks[None, :] <= q[:, None])
        new[:, b] = np.where(ok, -sl[:, None] * (q[:, None] - ks[None, :]), NEG)
    c["alibi_new"] = new.reshape(P, -1)
    s_, t_ = s64[:, None], s64[None, :]
    strict = same & (s_ < t_)
    incl = s_ <= np.arange(W)[None, :]
    sb = (s_ // TS == t_ // TS)
    sbi = (s_ // TS == np.arange(W)[None, :] // TS)
    c["gram_mask"] = np.stack([np.concatenate([strict, incl], 1), np.concatenate([strict & sb, incl & sbi], 1)], 1).reshape(P, -1)
    lev = []
    for j in range(6):
        z = 1 << j
        lev.append(same & (s_ // (2 * z) == t_ // (2 * z)) & (s_ // z % 2 == 0) & (t_ // z % 2 == 1))
    c["level_mask"] = np.stack(lev, 1).reshape(P, -1)
    tt = np.arange(NT)
    first = np.where(tt < TP, tt % W == 0, tt % TS == 0)
    c["carry"] = np.broadcast_to(1.0 - first, (P, NT))
    c["batch_mask"] = (s64[:, None] // TS == np.arange(NB)[None, :])
    e = np.zeros((P, 2, HC * TS))
    for r in range(64):
        mm, qq = r // TS, r % TS
        e[r, mm % 2, (mm // 2) * TS + qq] = 1.0
    c["combine"] = e.reshape(P, -1)
    li = np.array([0.8 - 0.6 * math.exp(-0.3 * l) for l in range(L)])
    c["lam_init"] = np.broadcast_to(np.concatenate([li, 1.0 - li])[None, :], (P, 2 * L))
    return {k: np.ascontiguousarray(v, dtype=np.float32) for k, v in c.items()}


class Steps:

    def __init__(self, sem, stage, book, new):
        self.sem, self.stage, self.book, self.new = sem, stage, book, new
        self.n, self.per, self.it, self.start = 0, 0, None, 0
        self.credit = book.get((stage, "per"), 0)

    def loop(self, it):
        if self.it is None:
            self.start = self.n
        self.it, self.n = it, self.start
        self.per = self.book.get((self.stage, "per"), 0)

    def end(self, turns):
        per = self.n - self.start
        self.new[(self.stage, "per")] = per
        self.it, self.n = None, self.start + turns * per

    def did(self, ins, name=None):
        ins.then_inc(self.sem, 1)
        self.n += 1
        if name is not None:
            assert self.new.get((self.stage, name), self.n) == self.n, (self.stage, name)
            self.new[(self.stage, name)] = self.n

    def own(self, eng):
        v = self.credit + self.n
        if self.it is not None:
            v = self.it * self.per + v
        elif v == 0:
            return
        eng.wait_ge(self.sem, v)

    def wait(self, eng, name, it=0):
        v = self.credit + self.book.get((self.stage, name), 1)
        per = self.book.get((self.stage, "per"), 0)
        if not isinstance(it, int) or it:
            v = it * per + v
        eng.wait_ge(self.sem, v)


class Core:

    def __init__(self, nc, ctx, io, book):
        self.nc, self.io, self.book, self.new = nc, io, book, {}

        def sem(name):
            return ctx.enter_context(nc.semaphore(name))

        self.w_loaded = [sem("w_loaded0"), sem("w_loaded1")]
        self.w_hi = sem("w_hi")
        self.w_split = sem("w_split")
        self.mm_done = sem("mm_done")
        self.evac = [sem("evac0"), sem("evac1")]
        self.part_hi = sem("part_hi")
        self.part_lo = sem("part_lo")
        self.pe_steps, self.act_steps = sem("pe_steps"), sem("act_steps")
        self.dve_steps, self.pool_steps = sem("dve_steps"), sem("pool_steps")
        self.pe_turns, self.act_turns = sem("pe_turns"), sem("act_turns")
        self.dve_turns, self.pool_turns = sem("dve_turns"), sem("pool_turns")
        self.loads = [sem(f"loads{i}") for i in range(5)]
        self.stores = [sem(f"stores{i}") for i in range(2)]
        every = [self.w_hi, self.w_split, self.mm_done, self.part_hi, self.part_lo, self.pe_steps, self.act_steps,
                 self.dve_steps, self.pool_steps, self.pe_turns, self.act_turns, self.dve_turns, self.pool_turns,
                 *self.w_loaded, *self.evac, *self.loads, *self.stores]
        nums = sorted(s.num for s in every)
        assert nums == list(range(nums[0], nums[0] + len(nums)))
        self.all_sems = range(nums[0], nums[-1] + 1)

        at = BASE

        def fixed(name, shape, dt=F32):
            nonlocal at
            t = self.place(name, shape, at, dt)
            at += (4 * int(np.prod(shape[1:])) + 31) // 32 * 32
            return t

        self.ident = fixed("ident", [P, P])
        self.ones = fixed("ones", [P, P])
        self.halves = fixed("halves", [P, P])
        self.vec_all = fixed("vec_all", [P, L, NVEC + KD])
        self.vec = fixed("vec", [P, NVEC])
        self.neg_lam = fixed("neg_lam", [P, L])
        self.lam_init = fixed("lam_init", [P, 2 * L])
        self.nlam = fixed("nlam", [P, 1])
        self.one_li = fixed("one_li", [P, 1])
        self.eps = fixed("eps", [P, 4])
        self.pages = fixed("pages", [1, NB * NPG], I32)
        self.junk = fixed("junk", [P, 16])
        assert at <= BASE + 5120
        at = BASE + 5120
        self.x = fixed("x", [P, KD, NT])
        self.h_hi = fixed("h_hi", [P, KD, NT], F32R)
        self.h_lo = fixed("h_lo", [P, KD, NT], F32R)
        self.ring = at
        self.raw = [fixed(f"raw{s}", [P, KD, P]) for s in range(2)]
        self.whi = [fixed(f"whi{s}", [P, KD, P], F32R) for s in range(2)]
        self.wlo = [fixed(f"wlo{s}", [P, KD, P], F32R) for s in range(2)]
        self.r0 = at
        self.D = [ctx.enter_context(nc.psum_tensor(f"dense{s}", [P, 2, 512], F32)) for s in range(2)]
        self.E = [ctx.enter_context(nc.psum_tensor(f"extra{s}", [P, 2, 512], F32)) for s in range(2)]

    def place(self, name, shape, offset, dt=F32):
        return self.nc.alloc_sbuf_tensor_at(name, shape, dt, offset=offset)

    def region(self, prefix, at):
        here = [at]

        def tile(name, shape, dt=F32):
            t = self.place(f"{prefix}_{name}", shape, here[0], dt)
            here[0] += (4 * int(np.prod(shape[1:])) + 31) // 32 * 32
            assert here[0] <= LIMIT, (prefix, name, here[0])
            return t
        tile.at = here
        return tile

    def steps(self, sem, stage):
        return Steps(sem, stage, self.book, self.new)

    def barrier(self):
        self.nc.all_engine_barrier(sems_to_clear=self.all_sems)

    def credits(self, pool, steps=()):
        give = [(self.part_lo, 1), (self.w_split, 2), (self.mm_done, 2), (self.evac[0], 1), (self.evac[1], 1)]
        give += [(s.sem, s.credit) for s in steps if s.credit]
        for i, (s, n) in enumerate(give):
            pool.memset(self.junk[:, i:i + 1], 0.0).then_inc(s, n)

    def load_w(self, sp, k, s, src):
        sp.wait_ge(self.w_split, 2 * k + s + 1)
        sp.dma_start(self.raw[s][:, 0:src.shape[1], :], src).then_inc(self.w_loaded[s], 16)

    def split_hi(self, act, k, s):
        act.wait_ge(self.w_loaded[s], 16 * k + 16)
        act.wait_ge(self.mm_done, 2 * k + s + 1)
        act.activation(self.whi[s][:], self.raw[s][:], ACT.Copy).then_inc(self.w_hi, 1)

    def split_lo(self, dve, k, s):
        dve.wait_ge(self.w_hi, 2 * k + s + 1)
        dve.tensor_tensor(self.wlo[s][:], self.raw[s][:], self.whi[s][:].bitcast(F32), ALU.subtract)\
           .then_inc(self.w_split, 1)

    def products(self, pe, k, s, hi, lo, out, bank_use=None, first=True, last=True, ready=None):
        pe.wait_ge(self.w_split, 2 * k + s + 3)
        if bank_use is not None:
            pe.wait_ge(self.evac[bank_use[0]], bank_use[1])
        chunks = hi.shape[1]
        for c in range(chunks):
            if ready is not None:
                ready(c)
            w_hi, w_lo = self.whi[s][:, c, :], self.wlo[s][:, c, :]
            for half in range(2):
                t = slice(half * NH, (half + 1) * NH)
                o = out[:, half, 0:NH]
                pe.matmul(o, w_hi, hi[:, c, t], start=(first and c == 0), stop=False)
                pe.matmul(o, w_hi, lo[:, c, t], start=False, stop=False)
                mm = pe.matmul(o, w_lo, hi[:, c, t], start=False, stop=(last and c == chunks - 1))
        mm.then_inc(self.mm_done, 1)

    @staticmethod
    def chase(eng, split, segments, begun=False):
        if not begun:
            for s in range(2):
                split(0, s)
        k0 = 0
        for n, (pairs, unroll, finish) in enumerate(segments):
            last = n == len(segments) - 1
            turns = pairs // unroll - last

            def turn(i, final=False):
                for j in range(unroll):
                    for s in range(2):
                        if not (final and j == unroll - 1):
                            split(i * unroll + (k0 + j + 1), s)
                        finish(i * unroll + j, j, i, s)
            if turns:
                with eng.Fori(0, turns) as i:
                    turn(i)
            if last:
                turn(pairs // unroll - 1, True)
            k0 += pairs

    def norm_tiles(self, tile):
        self.sq = [tile(f"sq{i}", [P, NT]) for i in range(2)]
        self.rstd = tile("rstd", [P, NT])
        self.hf = [tile(f"hf{i}", [P, NT]) for i in range(2)]

    def norm_act(self, act, A, V, Q, split=False):
        act.preload_act_table_set("sqrt_and_others")
        for j in range(KD // 2):
            if j >= 2:
                Q.wait(act, f"sum{j - 2}")
            A.did(act.activation(self.sq[j % 2][:], self.x[:, 2 * j, :], ACT.Square), f"sq{j}")
        if split:
            for s in range(2):
                self.split_hi(act, 0, s)
        Q.wait(act, f"sum{KD // 2 - 1}")
        A.own(act)
        A.did(act.activation(self.rstd[:].rearrange("p (a t) -> p a t", a=2), self.E[0][:, :, 0:NH], ACT.Sqrt,
                             bias=self.eps[:, 0:1], scale=1.0 / D), "root")

    def norm_dve(self, dve, A, V):
        for j in range(KD // 2):
            V.own(dve)
            V.did(dve.tensor_tensor(self.hf[j % 2][:], self.x[:, 2 * j + 1, :], self.x[:, 2 * j + 1, :], ALU.mult))
            A.wait(dve, f"sq{j}")
            V.own(dve)
            V.did(dve.tensor_tensor(self.sq[j % 2][:], self.sq[j % 2][:], self.hf[j % 2][:], ALU.add), f"pair{j}")

    def norm_pe(self, pe, V, Q):
        for c in range(KD // 2):
            V.wait(pe, f"pair{c}")
            for half in range(2):
                mm = pe.matmul(self.E[0][:, half, 0:NH], self.ones[:], self.sq[c % 2][:, half * NH:(half + 1) * NH],
                               start=(c == 0), stop=(c == KD // 2 - 1))
            Q.did(mm, f"sum{c}")

    def h_act(self, act, A, V):
        for c in range(KD):
            V.wait(act, f"h{c}")
            A.did(act.activation(self.h_hi[:, c, :], self.hf[c % 2][:], ACT.Copy), f"hhi{c}")

    def h_dve(self, dve, A, V, vec):
        self.norm_dve(dve, A, V)
        for s in range(2):
            self.split_lo(dve, 0, s)
        A.wait(dve, "root")
        V.did(dve.reciprocal(self.rstd[:], self.rstd[:]), "rstd")
        V.own(dve)

        def low(c):
            A.wait(dve, f"hhi{c}")
            V.did(dve.tensor_tensor(self.h_lo[:, c, :], self.hf[c % 2][:], self.h_hi[:, c, :].bitcast(F32),
                                    ALU.subtract), f"hlo{c}")
        for c in range(KD):
            V.own(dve)
            V.did(dve.scalar_tensor_tensor(self.hf[c % 2][:], self.x[:, c, :], vec[:, c:c + 1], self.rstd[:],
                                           ALU.mult, ALU.mult), f"h{c}")
            if c >= 1:
                low(c - 1)
        low(KD - 1)

    def ffn(self, l, which):
        nc, io, ev = self.nc, self.io, self.evac
        tile = self.region(which, self.r0)
        self.norm_tiles(tile)
        a_hi, a_lo = tile("a_hi", [P, HF, NT], F32R), tile("a_lo", [P, HF, NT], F32R)
        gate, prod = tile("gate", [P, NT]), tile("prod", [P, NT])
        wg = io[which + "_w_gate"].rearrange("l (c p) n -> p (l c) n", p=P)
        wu = io[which + "_w_up"].rearrange("l (c p) n -> p (l c) n", p=P)
        wd = io[which + "_w_down"].rearrange("l (c p) n -> p (l c) n", p=P)
        v0 = VEC[which + "_norm"][0]
        vec = self.vec[:, v0:v0 + KD]
        A, V, Q = (self.steps(s, which + n) for s, n in
                   ((self.act_steps, "A"), (self.dve_steps, "V"), (self.pe_steps, "Q")))
        KS = (HF + 1) // 2
        PAIRS = HF + KD
        pair = [h * PAIRS for h in range(2)]
        used = [h * (HF + KD // 2) for h in range(2)]

        with nc.Block() as block:
            @block.gpsimd
            def _(pool):
                self.credits(pool)

            @block.sync
            def _(sp):
                for h in range(2):
                    with sp.Fori(0, HF) as f:
                        for s, w in enumerate((wg, wu)):
                            self.load_w(sp, f + pair[h], s, w[:, ds(l * KD, KD), ds((f + h * HF) * P, P)])
                    with sp.Fori(0, KD) as c:
                        for s, (a, n) in enumerate(((0, KS), (KS, HF - KS))):
                            self.load_w(sp, c + (pair[h] + HF), s, wd[:, ds(l * KF + (h * HF + a), n), ds(c * P, P)])

            @block.tensor
            def _(pe):
                self.norm_pe(pe, V, Q)
                for h in range(2):
                    with pe.Fori(0, HF) as f:
                        for s in range(2):
                            self.products(pe, f + pair[h], s, self.h_hi, self.h_lo, self.D[s], (s, f + (used[h] + 1)),
                                          ready=(lambda c: V.wait(pe, f"hlo{c}")) if h == s == 0 else None)
                    with pe.Fori(0, KD // 2) as c:
                        for u in range(2):
                            k = c * 2 + (pair[h] + HF + u)
                            out, use = self.D[u], (u, c + (used[h] + HF + 1))
                            for s, r in enumerate((slice(0, KS), slice(KS, HF))):
                                def there(c, a=h * HF + r.start):
                                    pe.wait_ge(self.part_lo, a + c + 2)
                                self.products(pe, k, s, a_hi[:, r], a_lo[:, r], out, use if s == 0 else None,
                                              first=(s == 0), last=(s == 1), ready=there if u == 0 else None)

            @block.scalar
            def _(act):
                self.norm_act(act, A, V, Q, split=True)
                self.h_act(act, A, V)
                act.preload_act_table_set("silu_and_others")

                def silu_and_high(h):
                    def finish(f, j, _, s):
                        if s == 0:
                            act.wait_ge(self.mm_done, f * 2 + (2 * pair[h] + 3))
                            act.wait_ge(ev[1], f + (used[h] + 1))
                            act.activation(gate[:].rearrange("p (a t) -> p a t", a=2), self.D[0][:, :, 0:NH], ACT.Silu)\
                               .then_inc(ev[0], 1)
                            return
                        act.wait_ge(ev[1], f + (used[h] + 2))
                        act.activation(a_hi[:, ds(f, 1), :].rearrange("p a t -> p (a t)"), prod[:], ACT.Copy)\
                           .then_inc(self.part_hi, 1)
                    return finish
                none = lambda i, j, c, s: None
                self.chase(act, lambda k, s: self.split_hi(act, k, s),
                           [(HF, 1, silu_and_high(0)), (KD, 2, none), (HF, 1, silu_and_high(1)), (KD, 2, none)],
                           begun=True)

            @block.vector
            def _(dve):
                if which == "ffn1":
                    dve.tensor_copy(self.vec[:], self.vec_all[:, ds(l, 1), 0:NVEC].rearrange("p a n -> p (a n)"))
                    dve.tensor_copy(self.nlam[:], self.neg_lam[:, ds(l, 1)])
                    V.did(dve.tensor_copy(self.one_li[:], self.lam_init[:, ds(l + L, 1)]))
                self.h_dve(dve, A, V, vec)

                def times_up(h):
                    def finish(f, j, _, s):
                        if s == 0:
                            return
                        dve.wait_ge(self.mm_done, f * 2 + (2 * pair[h] + 4))
                        dve.wait_ge(ev[0], f + (used[h] + 2))
                        dve.wait_ge(self.part_lo, f + (h * HF + 1))
                        dve.tensor_tensor(prod[:].rearrange("p (a t) -> p a t", a=2), self.D[1][:, :, 0:NH],
                                          gate[:].rearrange("p (a t) -> p a t", a=2), ALU.mult).then_inc(ev[1], 1)
                        dve.wait_ge(self.part_hi, f + (h * HF + 1))
                        dve.tensor_tensor(a_lo[:, ds(f, 1), :].rearrange("p a t -> p (a t)"), prod[:],
                                          a_hi[:, ds(f, 1), :].rearrange("p a t -> p (a t)").bitcast(F32),
                                          ALU.subtract).then_inc(self.part_lo, 1)
                    return finish

                def add_down(h):
                    def finish(c, u, _, s):
                        if s == 0:
                            return
                        dve.wait_ge(self.mm_done, c * 2 + (2 * (pair[h] + HF) + 4))
                        xs = self.x[:, ds(c, 1), :].rearrange("p a (b t) -> p (a b) t", b=2)
                        dve.scalar_tensor_tensor(xs, self.D[u][:, :, 0:NH], 0.5, xs, ALU.mult, ALU.add)\
                           .then_inc(ev[u], 1)
                    return finish
                self.chase(dve, lambda k, s: self.split_lo(dve, k, s),
                           [(HF, 1, times_up(0)), (KD, 2, add_down(0)), (HF, 1, times_up(1)), (KD, 2, add_down(1))],
                           begun=True)

    def setup(self):
        nc, io, ev = self.nc, self.io, self.evac
        tile = self.region("setup", self.r0)
        rows = [tile(f"rows{l}", [P, P]) for l in range(L)]
        xt = tile("xt", [P, TP // P + 1, D])
        lam = tile("lam", [1, 4, L * 64])
        lprod = tile("lprod", [1, 2, L * 64])
        lsum, lexp, lrow = tile("lsum", [1, 2 * L]), tile("lexp", [1, 2 * L]), tile("lrow", [1, L])
        A, V, Q, G = self.stage_steps("setup")
        consts, vectors, tokens, lams = self.loads[0:4]
        views = {n: io[n].rearrange({"conv_w": "l j (c p) -> (l j c) p", "r_k": "l (c h) k -> (l c) (h k)"}
                                    .get(n, "l (c p) -> (l c) p"), **({"h": 2} if n == "r_k" else {"p": P})) for n in VEC}

        with nc.Block() as block:
            @block.gpsimd
            def _(pool):
                pool.memset(self.ones[:], 1.0)
                pool.memset(self.eps[:, 0:1], 1e-6)
                pool.memset(self.eps[:, 1:2], 1e-5)
                G.own(pool)
                G.did(pool.memset(self.eps[:, 2:3], 64e-5), "ones")

            @block.sync
            def _(sp):
                for n, t in (("ident", self.ident), ("halves", self.halves), ("lam_init", self.lam_init)):
                    sp.dma_start(t[:], io[n]).then_inc(consts, 16)
                for l in range(L):
                    for n, (r, c) in VEC.items():
                        sp.dma_start(rows[l][r:r + c, :], views[n][l * c:(l + 1) * c, :]).then_inc(vectors, 16)
                sp.dma_start(rows[L - 1][NVEC:NVEC + KD, :], io["final_norm"].rearrange("(c p) -> c p", p=P))\
                  .then_inc(vectors, 16)
                sp.dma_start(xt[:, 0:TP // P, :], io["x_prompt"].rearrange("a (b p) d -> p (a b) d", p=P))\
                  .then_inc(tokens, 16)
                sp.dma_start(xt[0:NS, TP // P, :], io["x_sample"].rearrange("b s d -> (b s) d")).then_inc(tokens, 16)
                for i, n in enumerate(("lam_q1", "lam_k1", "lam_q2", "lam_k2")):
                    sp.dma_start(lam[0:1, i, :], io[n].rearrange("(a l) d -> a (l d)", a=1)).then_inc(lams, 16)
                sp.dma_start(self.pages[:], io["page_table"].rearrange("(a b) n -> a (b n)", a=1)).then_inc(lams, 16)

            @block.tensor
            def _(pe):
                pe.wait_ge(consts, 16 * 3)
                pe.wait_ge(vectors, 16 * (L * len(VEC) + 1))
                for l in range(L):
                    n = NVEC + (KD if l == L - 1 else 0)
                    Q.did(pe.transpose(self.E[l][:, 0, 0:n], rows[l][0:n, :], self.ident[0:n, 0:n]), f"vec{l}")
                G.wait(pe, "ones")
                V.wait(pe, "lam")
                Q.did(pe.matmul(self.E[0][:, 1, 0:L], self.ones[0:1, :], lrow[:], start=True, stop=True), "lam")
                pe.wait_ge(tokens, 32)
                for c in range(KD):
                    if c >= 2:
                        V.wait(pe, f"x{c - 2}")
                    for b in range(TP // P):
                        pe.transpose(self.D[c % 2][:, 0, b * P:(b + 1) * P], xt[:, b, c * P:(c + 1) * P], self.ident[:])
                    Q.did(pe.transpose(self.D[c % 2][:, 1, 0:NS], xt[0:NS, TP // P, c * P:(c + 1) * P],
                                       self.ident[0:NS, 0:NS]), f"x{c}")

            @block.scalar
            def _(act):
                V.wait(act, "dots")
                A.own(act)
                A.did(act.activation(lexp[:], lsum[:], ACT.Exp), "exp")
                for l in range(L):
                    n = NVEC + (KD if l == L - 1 else 0)
                    Q.wait(act, f"vec{l}")
                    A.own(act)
                    A.did(act.activation(self.vec_all[:, l, 0:n], self.E[l][:, 0, 0:n], ACT.Copy), f"vec{l}")

            @block.vector
            def _(dve):
                dve.wait_ge(lams, 16 * 5)
                lv = lam[:].rearrange("a (i j) n -> a i j n", j=2)
                V.own(dve)
                V.did(dve.tensor_tensor(lprod[:], lv[:, :, 0, :], lv[:, :, 1, :], ALU.mult), "prods")
                V.own(dve)
                V.did(dve.tensor_reduce(lsum[:], lprod[:].rearrange("a i (l d) -> a (i l) d", l=L), AX.X, ALU.add), "dots")
                A.wait(dve, "exp")
                dve.wait_ge(consts, 16 * 3)
                V.own(dve)
                V.did(dve.tensor_tensor(lrow[:], lexp[:, L:2 * L], lexp[:, 0:L], ALU.subtract), "diff")
                V.own(dve)
                V.did(dve.tensor_tensor(lrow[:], lrow[:], self.lam_init[0:1, 0:L], ALU.subtract), "lam")
                Q.wait(dve, "lam")
                A.wait(dve, "vec0")
                V.own(dve)
                V.did(dve.tensor_copy(self.neg_lam[:], self.E[0][:, 1, 0:L]), "neg_lam")
                for c in range(KD):
                    Q.wait(dve, f"x{c}")
                    dve.tensor_copy(self.x[:, c, 0:TP], self.D[c % 2][:, 0, :])
                    V.own(dve)
                    V.did(dve.tensor_copy(self.x[:, c, TP:NT], self.D[c % 2][:, 1, 0:NS]), f"x{c}")

    def stage_steps(self, stage, turns=False):
        kinds = (self.act_turns, self.dve_turns, self.pe_turns, self.pool_turns) if turns else \
                (self.act_steps, self.dve_steps, self.pe_steps, self.pool_steps)
        return [self.steps(s, stage + n + "t" * turns) for s, n in zip(kinds, "AVQG")]

    def project(self, l, name, runs, dest):
        nc, io, ev = self.nc, self.io, self.evac
        A, V, Q, G = self.stage_steps(name)
        win = io["w_in"].rearrange("l (c p) n -> p (l c) n", p=P)
        pairs = sum(n for _, n in runs) // 2
        v0 = VEC["mix_norm"][0]

        with nc.Block() as block:
            @block.gpsimd
            def _(pool):
                self.credits(pool)

            @block.sync
            def _(sp):
                k0 = 0
                for first, count in runs:
                    with sp.Fori(0, count // 2) as k:
                        for s in range(2):
                            self.load_w(sp, k + k0, s, win[:, ds(l * KD, KD), ds((k * 2 + (first + s)) * P, P)])
                    k0 += count // 2

            @block.tensor
            def _(pe):
                self.norm_pe(pe, V, Q)
                with pe.Fori(0, pairs) as k:
                    for s in range(2):
                        self.products(pe, k, s, self.h_hi, self.h_lo, self.D[s], (s, k + 1),
                                      ready=(lambda c: V.wait(pe, f"hlo{c}")) if s == 0 else None)

            @block.scalar
            def _(act):
                self.norm_act(act, A, V, Q, split=True)
                self.h_act(act, A, V)

                def copy_even(k, j, _, s):
                    if s == 1:
                        return
                    act.wait_ge(self.mm_done, k * 2 + 3)
                    act.activation(dest[:, ds(k * 2, 1), :].rearrange("p a (b t) -> p (a b) t", b=2),
                                   self.D[0][:, :, 0:NH], ACT.Copy).then_inc(ev[0], 1)
                self.chase(act, lambda k, s: self.split_hi(act, k, s), [(pairs, 1, copy_even)], begun=True)

            @block.vector
            def _(dve):
                self.h_dve(dve, A, V, self.vec[:, v0:v0 + KD])

                def copy_odd(k, j, _, s):
                    if s == 0:
                        return
                    dve.wait_ge(self.mm_done, k * 2 + 4)
                    dve.tensor_copy(dest[:, ds(k * 2 + 1, 1), :].rearrange("p a (b t) -> p (a b) t", b=2),
                                    self.D[1][:, :, 0:NH]).then_inc(ev[1], 1)
                self.chase(dve, lambda k, s: self.split_lo(dve, k, s), [(pairs, 1, copy_odd)], begun=True)

    def prompt_attention(self, l, proj, y, vtok, tile):
        nc, io = self.nc, self.io
        A, V, Q, G = self.stage_steps("prompt")
        At, Vt, Qt, Gt = self.stage_steps("prompt", True)
        alibi = tile("alibi", [P, HC, TP])
        ring = self.region("prompt_ring", self.ring)
        ktok = ring("ktok", [P, TP // P + 1, DB])
        S = [tile(f"S{i}", [P, 2, TP]) for i in range(2)]
        qm = [tile(f"qm{i}", [P, 2, TP]) for i in range(2)]
        vh = [tile(f"vh{i}", [P, TP // P, P]) for i in range(2)]
        attn_t = [tile(f"attn_t{i}", [P, TP]) for i in range(2)]
        mx, ex, ri = ([tile(f"{n}{i}", [P, w]) for i in range(2)] for n, w in (("mx", 4), ("ex", 2), ("ri", 2)))
        rows_in = ring("rows_in", [NB * 2, DB])
        state = ring("state", [P, CB, NB * 2])
        ext = ring("ext", [P, 2 + TP])
        ext_s = ring("ext_s", [P, NB, 2 + TS])
        tmp, tmp2 = ring("tmp", [P, NT]), ring("tmp2", [P, NT])
        last = ring("last", [P, CB, 2 + NB * 2])
        rows_out = ring("rows_out", [2 + NB * 2, DB])
        tables, states = self.loads[0:2]
        kv_out, conv_out = self.stores
        nblk = TP // P + 1
        cw = VEC["conv_w"][0]
        NU = 2 * (TP // P)
        keys = lambda u: (u % (TP // P) + 1) * P
        bank = lambda pair, u, n: pair[:, u % 2, 0:n]
        kv = [(b, w) for b in range(nblk) for w in range(2)]
        slot = lambda n: self.E[n % 4 // 2][:, n % 2, :]

        def evac_kv(eng, w):
            for n, (b, w_) in enumerate(kv):
                if w_ != w:
                    continue
                m = P if b < nblk - 1 else NS
                Q.wait(eng, f"kv{n}")
                dst = (ktok, vtok)[w][0:m, b, :]
                if w == 0:
                    A.own(eng)
                    A.did(eng.activation(dst, slot(n)[0:m, :], ACT.Copy), f"kv{n}")
                else:
                    V.own(eng)
                    V.did(eng.tensor_copy(dst, slot(n)[0:m, :]), f"kv{n}")

        with nc.Block() as block:
            @block.sync
            def _(sp):
                sp.dma_start(rows_in[:], io["state_conv"].rearrange("l b j n -> (l b j) n")[ds(l * (2 * NB), 2 * NB), :])\
                  .then_inc(states, 16)
                sp.dma_start(alibi[:].rearrange("p h t -> p (h t)"), io["alibi_prompt"]).then_inc(tables, 16)
                for eng, led, t, out in ((None, A, ktok, "k"), (None, V, vtok, "v")):
                    w = 0 if t is ktok else 1
                    led.wait(sp, f"kv{2 * (nblk - 1) + w}")
                    sp.dma_start(io[f"{out}_prompt"].rearrange("l a (b p) h d -> p (l a b) (h d)", p=P)
                                 [:, ds(l * (nblk - 1), nblk - 1), :], t[:, 0:nblk - 1, :]).then_inc(kv_out, 16)
                    sp.dma_start(io[f"{out}_sample"].rearrange("l b s h d -> (l b s) (h d)")[ds(l * NS, NS), :],
                                 t[0:NS, nblk - 1, :]).then_inc(kv_out, 16)
                A.wait(sp, "conv_rows")
                sp.dma_start(io["conv_prompt"].rearrange("l a j n -> (l a j) n")[ds(l * 2, 2), :], rows_out[0:2, :])\
                  .then_inc(conv_out, 16)
                sp.dma_start(io["conv_sample"].rearrange("l b j n -> (l b j) n")[ds(l * (2 * NB), 2 * NB), :],
                             rows_out[2:2 + 2 * NB, :]).then_inc(conv_out, 16)
                sp.wait_ge(kv_out, 64)
                sp.wait_ge(conv_out, 32)

            @block.tensor
            def _(pe):
                for n, (b, w) in enumerate(kv):
                    m = P if b < nblk - 1 else NS
                    if n >= 4:
                        (A, V)[w].wait(pe, f"kv{n - 4}")
                    for c in range(CB):
                        tr = pe.transpose(slot(n)[0:m, c * P:(c + 1) * P],
                                          proj[:, 16 + 4 * w + c, b * P:b * P + m], self.ident[:])
                    Q.did(tr, f"kv{n}")
                pe.wait_ge(states, 16)
                for c in range(CB):
                    tr = pe.transpose(self.D[0][:, 0, c * 16:(c + 1) * 16], rows_in[:, c * P:(c + 1) * P],
                                      self.ident[0:16, 0:16])
                Q.did(tr, "state")
                V.wait(pe, f"kv{len(kv) - 1}")
                A.wait(pe, "state")
                with pe.Fori(0, HC // 2) as t:
                    Qt.loop(t)

                    def scores(u):
                        g, i = divmod(u, TP // P)
                        if i == 0:
                            Gt.wait(pe, f"staged{g}", t)
                        for m in range(2):
                            k_h = proj[:, ds(t * 2 + (16 + g), 1), 0:keys(u)].rearrange("p a k -> p (a k)")
                            mm = pe.matmul(self.E[u % 2][:, m, 0:keys(u)], qm[g][:, m, i * P:(i + 1) * P], k_h,
                                           start=True, stop=True)
                        Qt.did(mm, f"scores{u}")
                    scores(0)
                    scores(1)
                    for u in range(NU):
                        g, i = divmod(u, TP // P)
                        if u + 2 < NU:
                            Vt.wait(pe, f"scaled{u}", t)
                            scores(u + 2)
                        Vt.wait(pe, f"attn{u}", t)
                        for b in range(i + 1):
                            tr = pe.transpose(bank(self.D[0], u, TP)[:, b * P:(b + 1) * P], S[u % 2][:, 0, b * P:(b + 1) * P],
                                              self.ident[:])
                        Qt.did(tr, f"turn{u}")
                        if u >= 2:
                            At.wait(pe, f"out{u - 2}", t)
                        else:
                            At.wait(pe, f"out{u + NU - 2}", t - 1)
                        At.wait(pe, f"turned{u}", t)
                        for b in range(i + 1):
                            mm = pe.matmul(bank(self.D[1], u, P), vh[g][:, b, :], attn_t[u % 2][:, b * P:(b + 1) * P],
                                           start=(b == 0), stop=(b == i))
                        Qt.did(mm, f"pv{u}")
                Qt.end(HC // 2)
                Gt.wait(pe, "conv1", HC // 2 - 1)
                A.wait(pe, "outs")
                for c in range(CB):
                    tr = pe.transpose(self.D[0][0:18, 1, c * P:(c + 1) * P], last[:, c, :], self.ident[:])
                Q.did(tr, "conv_rows")

            @block.scalar
            def _(act):
                evac_kv(act, 0)
                Q.wait(act, "state")
                A.own(act)
                A.did(act.activation(state[:].rearrange("p c n -> p (c n)"), self.D[0][:, 0, 0:CB * 16], ACT.Copy), "state")
                with act.Fori(0, HC // 2) as t:
                    At.loop(t)

                    def exp(u):
                        Vt.wait(act, f"negmax{u}", t)
                        At.own(act)
                        for m in range(2):
                            e = act.activation(S[u % 2][:, m, 0:keys(u)], S[u % 2][:, m, 0:keys(u)], ACT.Exp,
                                               bias=mx[u % 2][:, 2 + m:3 + m], scale=1.0, accum_out=ex[u % 2][:, m:m + 1])
                        At.did(e, f"exp{u}")

                    def out(u):
                        g, i = divmod(u, TP // P)
                        Qt.wait(act, f"pv{u}", t)
                        At.own(act)
                        At.did(act.activation(y[:, ds(t * 2 + (8 + g), 1), i * P:(i + 1) * P].rearrange("p a t -> p (a t)"),
                                              bank(self.D[1], u, P), ACT.Copy), f"out{u}")
                    exp(0)
                    for u in range(NU):
                        if u + 1 < NU:
                            exp(u + 1)
                        Qt.wait(act, f"turn{u}", t)
                        At.own(act)
                        At.did(act.activation(attn_t[u % 2][:, 0:keys(u)], bank(self.D[0], u, keys(u)), ACT.Copy), f"turned{u}")
                        if u:
                            out(u - 1)
                    out(NU - 1)
                At.end(HC // 2)
                At.wait(act, f"out{NU - 1}", HC // 2 - 1)
                A.did(act.activation(self.junk[:, 14:15], self.eps[:, 0:1], ACT.Copy), "outs")
                Q.wait(act, "conv_rows")
                A.own(act)
                A.did(act.activation(rows_out[:], self.D[0][0:18, 1, :], ACT.Copy), "conv_rows")

            @block.vector
            def _(dve):
                evac_kv(dve, 1)
                dve.wait_ge(self.loads[0], 16)
                with dve.Fori(0, HC // 2) as t:
                    Vt.loop(t)

                    def maxima(u):
                        g, n, s = u // (TP // P), keys(u), S[u % 2]
                        Qt.wait(dve, f"scores{u}", t)
                        if u >= 2:
                            Qt.wait(dve, f"turn{u - 2}", t)
                        else:
                            Qt.wait(dve, f"turn{u + NU - 2}", t - 1)
                        bias = alibi[:, ds(t * 2 + g, 1), TP - n:TP].to_broadcast([P, 2, n])
                        Vt.own(dve)
                        Vt.did(dve.scalar_tensor_tensor(s[:, :, 0:n], self.E[u % 2][:, :, 0:n], 0.125, bias,
                                                        ALU.mult, ALU.add), f"scaled{u}")
                        Vt.own(dve)
                        Vt.did(dve.tensor_reduce(mx[u % 2][:, 0:2], s[:, :, 0:n], AX.X, ALU.max))
                        Vt.own(dve)
                        Vt.did(dve.tensor_scalar(mx[u % 2][:, 2:4], mx[u % 2][:, 0:2], -1.0, None, ALU.mult), f"negmax{u}")
                    maxima(0)
                    for u in range(NU):
                        if u + 1 < NU:
                            maxima(u + 1)
                        n, s, r = keys(u), S[u % 2], ri[u % 2]
                        At.wait(dve, f"exp{u}", t)
                        Vt.own(dve)
                        Vt.did(dve.reciprocal(r[:], ex[u % 2][:]))
                        Vt.own(dve)
                        Vt.did(dve.tensor_scalar(r[:, 1:2], r[:, 1:2], self.nlam[:], None, ALU.mult))
                        Vt.own(dve)
                        Vt.did(dve.tensor_scalar(s[:, 0, 0:n], s[:, 0, 0:n], r[:, 0:1], None, ALU.mult))
                        Vt.own(dve)
                        Vt.did(dve.scalar_tensor_tensor(s[:, 0, 0:n], s[:, 1, 0:n], r[:, 1:2], s[:, 0, 0:n],
                                                        ALU.mult, ALU.add), f"attn{u}")
                Vt.end(HC // 2)

            @block.gpsimd
            def _(pool):
                self.credits(pool, (At, Vt, Qt, Gt))
                G.own(pool)
                G.did(pool.memset(qm[0][:], 0.0))
                G.own(pool)
                G.did(pool.memset(qm[1][:], 0.0))
                G.own(pool)
                G.did(pool.memset(ext[:, 0:2], 0.0), "zero")
                G.own(pool)
                A.wait(pool, "state")
                V.wait(pool, f"kv{len(kv) - 1}")
                for h in range(HC):
                    t, g = divmod(h, 2)
                    flat = lambda j, t=slice(0, TP), r=slice(0, P): proj[r, ds(h + j, 1), t].rearrange("p a t -> p (a t)")
                    if g == 0:
                        Gt.loop(t)
                        for n in range(2):
                            hn = h + n
                            Qt.wait(pool, f"pv{(n + 1) * (TP // P) - 1}", t - 1)
                            Gt.own(pool)
                            Gt.did(pool.tensor_copy(qm[n][0:64, 0, :], proj[0:64, 12 + hn, 0:TP]))
                            Gt.own(pool)
                            Gt.did(pool.tensor_copy(qm[n][64:128, 1, :], proj[64:128, 12 + hn, 0:TP]))
                            Gt.own(pool)
                            Gt.did(pool.tensor_copy(vh[n][:], vtok[:, 0:TP // P, hn * P:(hn + 1) * P]), f"staged{n}")
                    xs = lambda j: flat(j, slice(TP, NT)).rearrange("p (b s) -> p b s", b=NB)
                    Gt.own(pool)
                    Gt.did(pool.tensor_copy(ext_s[:, :, 0:2], state[:, ds(h, 1), :].rearrange("p a (b j) -> p (a b) j", b=NB)))
                    Gt.own(pool)
                    Gt.did(pool.tensor_tensor(ext[:, 2:], flat(8), flat(0), ALU.mult))
                    Gt.own(pool)
                    Gt.did(pool.tensor_tensor(ext_s[:, :, 2:], xs(8), xs(0), ALU.mult))
                    Gt.own(pool)
                    ty, tys = tmp[:, 0:TP], tmp[:, TP:NT].rearrange("p (b s) -> p b s", b=NB)
                    for j in range(3):
                        wj = self.vec[:, ds(h + (cw + CB * j), 1)]
                        o, os = (ty, tys) if j == 0 else (tmp2[:, 0:TP], tmp2[:, TP:NT].rearrange("p (b s) -> p b s", b=NB))
                        Gt.own(pool)
                        Gt.did(pool.tensor_scalar(o, ext[:, j:j + TP], wj, None, ALU.mult))
                        Gt.own(pool)
                        Gt.did(pool.tensor_scalar(os, ext_s[:, :, j:j + TS], wj, None, ALU.mult))
                        Gt.own(pool)
                        if j:
                            Gt.own(pool)
                            Gt.did(pool.tensor_tensor(tmp[:], tmp[:], tmp2[:], ALU.add))
                            Gt.own(pool)
                    Gt.own(pool)
                    Gt.did(pool.tensor_tensor(y[:, ds(h, 1), :].rearrange("p a t -> p (a t)"), tmp[:], flat(4, slice(0, NT)), ALU.mult))
                    Gt.own(pool)
                    Gt.did(pool.tensor_copy(last[:, ds(h, 1), 0:2].rearrange("p a j -> p (a j)"), ext[:, TP:TP + 2]))
                    Gt.own(pool)
                    Gt.did(pool.tensor_copy(last[:, ds(h, 1), 2:18].rearrange("p a (b j) -> p (a b) j", b=NB),
                                            ext_s[:, :, TS:TS + 2]), f"conv{g}")
                    Gt.own(pool)
                    Gt.did(pool.memset(self.junk[:, 15:16], 0.0))
                Gt.end(HC // 2)

    def sample_attention(self, l, proj, y, vtok, tile):
        nc, io = self.nc, self.io
        A, V, Q, G = self.stage_steps("sample")
        At, Vt, Qt, Gt = self.stage_steps("sample", True)
        KB, n_at, NU = 4 * NT, HC * TS, 4
        kt_at = tile.at[0]
        kt = tile("kt", [P, CB, PAST])
        past, new = tile("past", [64, PAST]), tile("new", [64, NB, NS])
        S = tile("S", [64, PAST + NS])
        qs = tile("qs", [P, 80 * CB])
        comb = tile("comb", [64, 2, HC * TS])
        e0, e1 = tile("e0", [64, HC * TS]), tile("e1", [64, HC * TS])
        mx, ex = tile("mx", [64, 2]), tile("ex", [64, 2])
        at = tile("at", [P, (NPG + 1) * HC * TS])
        rows = tile("rows", [n_at, DB])
        norm = self.region("subnorm", kt_at)
        sq, rstd = ([norm(f"{n}{i}", [P, NT]) for i in range(2)] for n in ("sq", "rstd"))
        places = []
        for a, b in ((self.r0 + 12 * KB, self.r0 + 24 * KB), (self.r0 + 32 * KB, self.r0 + 36 * KB),
                     (self.r0 + 4 * KB, self.r0 + 8 * KB), (self.ring, self.r0), (tile.at[0], LIMIT)):
            places += range(a, b - 4 * DB + 1, 4 * DB)
        page = [self.place(f"page{i}", [P, DB], a) for i, a in enumerate(places[:4 * NPG])]
        kp, vp = ([page[(2 * w + s) * NPG:(2 * w + s + 1) * NPG] for s in range(2)] for w in range(2))
        tables, kload, vload = self.loads[0], self.loads[1:3], self.loads[3:5]
        who = lambda n: (At, Vt)[n in (5, 7)]

        with nc.Block() as block:
            @block.sync
            def _(sp):
                ck = io["cache_k"].rearrange("l g t m d -> t (l g) (m d)")
                cv = io["cache_v"].rearrange("l g t m d -> t (l g) (m d)")
                pool_n = io["cache_k"].shape[1]
                with sp.Fori(0, NB // NU) as t:
                    for u in range(NU):
                        turn, v, s = (t, u - 2, u % 2) if u >= 2 else (t - 1, u + NU - 2, u % 2)
                        pg = []
                        for j in range(NPG):
                            pg.append(sp.value_load(self.pages[0:1, ds(t * (NU * NPG) + (u * NPG + j), 1)],
                                                    min_val=0, max_val=pool_n - 1))
                            if j == 0:
                                Qt.wait(sp, f"kturn{v}_7", turn)
                            sp.dma_start(kp[s][j][:], ck[:, ds(l * pool_n + pg[j], 1), :].rearrange("t a n -> t (a n)"))\
                              .then_inc(kload[s], 16)
                        for j in range(NPG):
                            if j == 0:
                                Qt.wait(sp, f"pv{v}", turn)
                            sp.dma_start(vp[s][j][:], cv[:, ds(l * pool_n + pg[j], 1), :].rearrange("t a n -> t (a n)"))\
                              .then_inc(vload[s], 16)

            @block.gpsimd
            def _(pool):
                self.credits(pool, (At, Vt, Qt, Gt))
                G.own(pool)
                G.did(pool.memset(qs[:], 0.0), "zero")
                G.own(pool)
                qv = qs[:].rearrange("p (c x) -> p c x", c=CB)
                with pool.Fori(0, NB // NU) as t:
                    Gt.loop(t)
                    for u in range(NU):
                        if u:
                            Qt.wait(pool, f"scores{u - 1}", t)
                        else:
                            Qt.wait(pool, f"scores{NU - 1}", t - 1)
                        for hf in range(2):
                            r = slice(64 * hf, 64 * hf + 64)
                            Gt.own(pool)
                            Gt.did(pool.tensor_copy(qv[r, :, hf * TS:hf * TS + TS],
                                                    proj[r, 12:16, ds(t * (NU * TS) + (u * TS + TP), TS)]),
                                   f"q{u}" if hf else None)
                Gt.end(NB // NU)

            @block.tensor
            def _(pe):
                with pe.Fori(0, NB // NU) as t:
                    Qt.loop(t)

                    def turn_keys(u):
                        s = u % 2
                        for n in range(2 * CB):
                            hf, c = divmod(n, CB)
                            if n == 0:
                                pe.wait_ge(kload[s], t * (16 * NPG * NU // 2) + 16 * NPG * (u // 2 + 1))
                            if n >= 2:
                                who(n - 2).wait(pe, f"kt{u}_{n - 2}", t)
                            elif u:
                                who(n + 6).wait(pe, f"kt{u - 1}_{n + 6}", t)
                            else:
                                who(n + 6).wait(pe, f"kt{NU - 1}_{n + 6}", t - 1)
                            for j in range(4):
                                tr = pe.transpose(self.E[n % 2][:, 0, j * P:(j + 1) * P],
                                                  kp[s][hf * 4 + j][:, c * P:(c + 1) * P], self.ident[:])
                            Qt.did(tr, f"kturn{u}_{n}")

                    def scores(u):
                        Gt.wait(pe, f"q{u}", t)
                        At.wait(pe, f"kt{u}_6", t)
                        Vt.wait(pe, f"kt{u}_7", t)
                        for hf in range(2):
                            for c in range(CB):
                                pe.matmul(self.D[0][0:64, hf, :], qs[:, c * 64:(c + 1) * 64], kt[:, c, hf * 512:(hf + 1) * 512],
                                          start=(c == 0), stop=(c == CB - 1))
                        for c in range(CB):
                            mm = pe.matmul(self.D[1][0:64, 0, 0:NS], qs[:, c * 64:(c + 1) * 64], proj[:, 16 + c, TP:NT],
                                           start=(c == 0), stop=(c == CB - 1))
                        Qt.did(mm, f"scores{u}")

                    def back(u):
                        At.wait(pe, f"rows{u}", t)
                        for h in range(HC):
                            mm = pe.matmul(self.D[1][:, 1, h * n_at:(h + 1) * n_at], rows[:, h * P:(h + 1) * P],
                                           self.ident[0:n_at, 0:n_at], start=True, stop=True)
                        Qt.did(mm, f"back{u}")
                    turn_keys(0)
                    scores(0)
                    for u in range(NU):
                        if u + 1 < NU:
                            turn_keys(u + 1)
                        Vt.wait(pe, f"weights{u}", t)
                        for j in range(NPG + 1):
                            m = P if j < NPG else NS
                            mm = pe.matmul(self.E[0][0:m, 1, j * n_at:(j + 1) * n_at], S[:, j * P:j * P + m], e1[:],
                                           start=True, stop=True)
                        Qt.did(mm, f"turn{u}")
                        if u:
                            back(u - 1)
                        if u + 1 < NU:
                            scores(u + 1)
                        pe.wait_ge(vload[u % 2], t * (16 * NPG * NU // 2) + 16 * NPG * (u // 2 + 1))
                        At.wait(pe, f"turned{u}", t)
                        for j in range(NPG + 1):
                            m = P if j < NPG else NS
                            v = vp[u % 2][j][:] if j < NPG else vtok[0:NS, TP // P, :]
                            mm = pe.matmul(self.E[1][0:n_at, 1, :], at[0:m, j * n_at:(j + 1) * n_at], v,
                                           start=(j == 0), stop=(j == NPG))
                        Qt.did(mm, f"pv{u}")
                    back(NU - 1)
                Qt.end(NB // NU)
                for h in range(HC):
                    A.wait(pe, f"sq{h}")
                    for half in range(2):
                        mm = pe.matmul(self.D[h % 2][:, half, 0:NH], self.ones[:], sq[h % 2][:, half * NH:(half + 1) * NH],
                                       start=True, stop=True)
                    Q.did(mm, f"sum{h}")

            @block.scalar
            def _(act):
                act.dma_start(past[:], io["alibi_past"][0:64, :]).then_inc(tables, 16)
                act.dma_start(new[:].rearrange("p b k -> p (b k)"), io["alibi_new"][0:64, :]).then_inc(tables, 16)
                act.dma_start(comb[:].rearrange("p b k -> p (b k)"), io["combine"][0:64, :]).then_inc(tables, 16)
                act.preload_act_table_set("natural_log_exp_and_others")
                with act.Fori(0, NB // NU) as t:
                    At.loop(t)

                    def keys(u, ns):
                        for n in ns:
                            hf, c = divmod(n, CB)
                            Qt.wait(act, f"kturn{u}_{n}", t)
                            if n == 0:
                                if u:
                                    Qt.wait(act, f"scores{u - 1}", t)
                                else:
                                    Qt.wait(act, f"scores{NU - 1}", t - 1)
                            At.own(act)
                            At.did(act.activation(kt[:, c, hf * 512:(hf + 1) * 512], self.E[n % 2][:, 0, :], ACT.Copy),
                                   f"kt{u}_{n}")

                    def out(u):
                        Qt.wait(act, f"back{u}", t)
                        At.own(act)
                        own = self.D[1][:, 1, 0:HC * (n_at + TS)].rearrange("p (h x) -> p h x", h=HC)[:, :, 0:TS]
                        At.did(act.activation(y[:, 8:12, ds(t * (NU * TS) + (u * TS + TP), TS)], own, ACT.Copy), f"out{u}")
                    keys(0, (0, 1, 2, 3, 4, 6))
                    for u in range(NU):
                        if u == 0:
                            keys(1, (0, 1, 2, 3))
                        Vt.wait(act, f"negmax{u}", t)
                        At.own(act)
                        At.did(act.activation(S[:], S[:], ACT.Exp, bias=mx[:, 1:2], scale=1.0, accum_out=ex[:, 0:1]), f"exp{u}")
                        if u == 0:
                            keys(1, (4, 6))
                        elif u + 1 < NU:
                            keys(u + 1, (0, 1, 2, 3, 4, 6))
                        Qt.wait(act, f"turn{u}", t)
                        act.activation(at[:, 0:NPG * n_at], self.E[0][:, 1, 0:NPG * n_at], ACT.Copy)
                        At.own(act)
                        At.did(act.activation(at[0:NS, NPG * n_at:], self.E[0][0:NS, 1, NPG * n_at:(NPG + 1) * n_at], ACT.Copy),
                               f"turned{u}")
                        if u:
                            out(u - 1)
                        Qt.wait(act, f"pv{u}", t)
                        At.own(act)
                        At.did(act.activation(rows[:], self.E[1][0:n_at, 1, :], ACT.Copy), f"rows{u}")
                    out(NU - 1)
                At.end(NB // NU)
                At.own(act)

                def square(h):
                    if h >= 2:
                        Q.wait(act, f"sum{h - 2}")
                    A.did(act.activation(sq[h % 2][:], y[:, 8 + h, :], ACT.Square), f"sq{h}")
                square(0)
                for h in range(HC):
                    if h + 1 < HC:
                        square(h + 1)
                    Q.wait(act, f"sum{h}")
                    if h >= 2:
                        V.wait(act, f"y{h - 2}")
                    A.did(act.activation(rstd[h % 2][:].rearrange("p (a t) -> p a t", a=2), self.D[h % 2][:, :, 0:NH], ACT.Ln,
                                         bias=self.eps[:, 1:2], scale=1.0 / P))
                    A.own(act)
                    A.did(act.activation(rstd[h % 2][:], rstd[h % 2][:], ACT.Exp, scale=-0.5), f"rstd{h}")

            @block.vector
            def _(dve):
                dve.wait_ge(tables, 48)
                V.own(dve)
                V.did(dve.scalar_tensor_tensor(e0[:], comb[:, 1, :], self.nlam[0:64, :], comb[:, 0, :], ALU.mult, ALU.add))
                with dve.Fori(0, NB // NU) as t:
                    Vt.loop(t)

                    def keys(u):
                        for n in (5, 7):
                            hf, c = divmod(n, CB)
                            Qt.wait(dve, f"kturn{u}_{n}", t)
                            Vt.own(dve)
                            Vt.did(dve.tensor_copy(kt[:, c, hf * 512:(hf + 1) * 512], self.E[1][:, 0, :]), f"kt{u}_{n}")
                    keys(0)
                    for u in range(NU):
                        Qt.wait(dve, f"scores{u}", t)
                        dve.scalar_tensor_tensor(S[:, 0:PAST].rearrange("p (a k) -> p a k", a=2), self.D[0][0:64, :, :], 0.125,
                                                 past[:].rearrange("p (a k) -> p a k", a=2), ALU.mult, ALU.add)
                        Vt.own(dve)
                        Vt.did(dve.scalar_tensor_tensor(S[:, PAST:], self.D[1][0:64, 0, 0:NS], 0.125,
                                                        new[:, ds(t * NU + u, 1), :].rearrange("p a k -> p (a k)"),
                                                        ALU.mult, ALU.add), f"scaled{u}")
                        Vt.own(dve)
                        Vt.did(dve.tensor_reduce(mx[:, 0:1], S[:], AX.X, ALU.max))
                        Vt.own(dve)
                        Vt.did(dve.tensor_scalar(mx[:, 1:2], mx[:, 0:1], -1.0, None, ALU.mult), f"negmax{u}")
                        if u == 0:
                            keys(1)
                        At.wait(dve, f"exp{u}", t)
                        Vt.own(dve)
                        Vt.did(dve.reciprocal(ex[:, 1:2], ex[:, 0:1]))
                        Vt.own(dve)
                        Vt.did(dve.tensor_scalar(e1[:], e0[:], ex[:, 1:2], None, ALU.mult), f"weights{u}")
                        if u and u + 1 < NU:
                            keys(u + 1)
                Vt.end(NB // NU)
                sw = VEC["subln_w"][0]
                for h in range(HC):
                    yh, r = y[:, 8 + h, :], rstd[h % 2][:]
                    A.wait(dve, f"rstd{h}")
                    V.did(dve.tensor_tensor(r, r, yh, ALU.mult))
                    V.own(dve)
                    V.did(dve.tensor_scalar(yh, r, self.vec[:, sw:sw + 1], self.one_li[:], ALU.mult, ALU.mult), f"y{h}")

    def project_shifted(self, l, z, last, tile):
        nc, io, ev = self.nc, self.io, self.evac
        A, V, Q, G = self.stage_steps("z")
        rows_in, state = tile("rows_in", [NB, NSHIFT]), tile("state", [P, CZ, NB])
        diff = [tile(f"diff{i}", [P, NT]) for i in range(2)]
        win = io["w_in"].rearrange("l (c p) n -> p (l c) n", p=P)
        pairs, mu0 = CZ // 2, VEC["tm_mu"][0]

        with nc.Block() as block:
            @block.gpsimd
            def _(pool):
                self.credits(pool)
                pool.memset(self.junk[:, 15:16], 0.0).then_inc(self.pool_turns, 1)

            @block.sync
            def _(sp):
                sp.dma_start(rows_in[:], io["state_shift"].rearrange("l b n -> (l b) n")[ds(l * NB, NB), :])\
                  .then_inc(self.loads[0], 16)
                with sp.Fori(0, pairs) as k:
                    for s in range(2):
                        self.load_w(sp, k, s, win[:, ds(l * KD, KD), ds((k * 2 + (COL_Z + s)) * P, P)])

            @block.tensor
            def _(pe):
                pe.wait_ge(self.loads[0], 16)
                for c in range(CZ):
                    tr = pe.transpose(self.E[0][:, 0, c * NB:(c + 1) * NB], rows_in[:, c * P:(c + 1) * P],
                                      self.ident[0:NB, 0:NB])
                Q.did(tr, "state")
                with pe.Fori(0, pairs) as k:
                    for s in range(2):
                        self.products(pe, k, s, self.h_hi, self.h_lo, self.D[s], (s, k + 1))

            @block.scalar
            def _(act):
                Q.wait(act, "state")
                A.did(act.activation(state[:].rearrange("p c b -> p (c b)"), self.E[0][:, 0, 0:CZ * NB], ACT.Copy), "state")

                def copy_even(k, j, _, s):
                    if s == 1:
                        return
                    act.wait_ge(self.mm_done, k * 2 + 3)
                    act.activation(z[:, ds(k * 2, 1), :].rearrange("p a (b t) -> p (a b) t", b=2),
                                   self.D[0][:, :, 0:NH], ACT.Copy).then_inc(ev[0], 1)
                self.chase(act, lambda k, s: self.split_hi(act, k, s), [(pairs, 1, copy_even)])

            @block.vector
            def _(dve):
                def shift(k, j, _, s):
                    c = k * 2 + s
                    zc = z[:, ds(c, 1), :].rearrange("p a t -> p (a t)")
                    d = diff[s]
                    done = lambda i: k * 12 + (6 * s + i)
                    if s == 0:
                        dve.wait_ge(ev[0], k + 2)
                    else:
                        dve.wait_ge(self.mm_done, k * 2 + 4)
                        dve.tensor_copy(z[:, ds(c, 1), :].rearrange("p a (b t) -> p (a b) t", b=2), self.D[1][:, :, 0:NH])\
                           .then_inc(ev[1], 1)
                        dve.wait_ge(ev[1], k + 2)
                    zs, dsm = (t[:, TP:NT].rearrange("p (b s) -> p b s", b=NB) for t in (zc, d))
                    step = lambda ins: ins.then_inc(self.dve_turns, 1)
                    dve.wait_ge(self.pool_turns, k * 2 + (s + 1))
                    step(dve.tensor_copy(last[:, ds(c, 1), 0:1], z[:, ds(c, 1), TP - 1:TP]))
                    step(dve.tensor_copy(last[:, ds(c, 1), 1:], z[:, ds(c, 1), TP + TS - 1:NT:TS]))
                    step(dve.tensor_tensor(d[:, 1:TP], zc[:, 0:TP - 1], zc[:, 1:TP], ALU.subtract))
                    step(dve.tensor_scalar(d[:, 0:1], zc[:, 0:1], -1.0, None, ALU.mult))
                    step(dve.tensor_tensor(dsm[:, :, 1:TS], zs[:, :, 0:TS - 1], zs[:, :, 1:TS], ALU.subtract))
                    step(dve.tensor_tensor(dsm[:, :, 0:1], state[:, ds(c, 1), :].rearrange("p a (b o) -> p (a b) o", o=1),
                                           zs[:, :, 0:1], ALU.subtract))
                    dve.wait_ge(self.dve_turns, done(6))
                    dve.scalar_tensor_tensor(zc, d[:], self.vec[:, ds(c + mu0, 1)], zc, ALU.mult, ALU.add)\
                       .then_inc(self.pool_turns, 1)
                A.wait(dve, "state")
                self.chase(dve, lambda k, s: self.split_lo(dve, k, s), [(pairs, 1, shift)])

    def recurrence(self, l, z, y, last, rows_out, tile):
        nc, io = self.nc, self.io
        A, V, Q, G = self.stage_steps("rwkv")
        At, Vt, Qt, Gt = self.stage_steps("rwkv", True)
        E, D = self.E, self.D
        ring = self.region("rwkv_ring", self.ring)
        NG, GW = 3, 3
        temps = tile.at[0]
        kk, kp, a, lw, cum, pinv, pprev, tmp = (tile(n, [P, NT]) for n in
                                                ("kk", "kp", "a", "lw", "cum", "pinv", "pprev", "tmp"))
        over = self.region("rwkv_over", temps)
        T, TT, W1, Lm = (over(n, [P, NW, P]) for n in ("T", "TT", "W1", "Lm"))
        assert over.at[0] <= tile.at[0]
        AR = tile("AR", [P, NW, P + W])
        Bb, Kb, Vb = (tile(n, [P, NW, P]) for n in ("Bb", "Kb", "Vb"))
        GM = tile("GM", [P, NW, 2, P + W])
        TM = ring("TM", [P, NW, 3, P])
        gg, bonus = tile("gg", [P, NT]), tile("bonus", [P, NT])
        pin, yt = tile("pin", [P, NT]), tile("yt", [P, NT])
        sq = ring("sq", [P, NT])
        carry = ring("carry", [P, NT])
        lev = ring("lev", [P, 6, P])
        gmask = ring("gmask", [P, 2, P + W])
        bmask = ring("bmask", [P, NB])
        wa, gup = tile("wa", [P, 2, P]), tile("gup", [P, P])
        S = [tile(f"S{i}", [P, P]) for i in range(2)]
        SP, Xs, Us, so = (tile(n, [P, P]) for n in ("SP", "Xs", "Us", "so"))
        omka = tile("omka", [P, CB])
        low, glow = z[:, 3 * CB, :], z[:, 3 * CB + 1, :]
        tables, wload, sload = self.loads[0:3]
        store = self.stores[0]
        two = lambda t: t.rearrange("p (a t) -> p a t", a=2)
        win = lambda t, r=slice(0, P): t[r, :].rearrange("p (w s) -> p w s", w=NW)
        cmul = -math.exp(-0.5)
        tok_bank = lambda w: D[w % 2][:, 0, 0:3 * P]
        gram_bank = lambda w: E[w % 2][:, 0, 0:2 * (P + W)]
        grp = lambda g: slice(g * GW, (g + 1) * GW)
        inv_bank = lambda g: (E[0][:, 1, 0:GW * P], E[1][:, 1, 0:GW * P], D[0][:, 1, 0:GW * P])[g]
        blocks = lambda t: t.rearrange("p (i n) -> p i n", n=P)
        row_banks = [E[1][:, 0, :], E[1][:, 1, :], D[0][:, 0, :], D[0][:, 1, :]]
        rows_store = self.stores[1]

        with nc.Block() as block:
            @block.sync
            def _(sp):
                for n, t in (("carry", carry[:]), ("batch_mask", bmask[:]), ("level_mask", lev[:].rearrange("p j n -> p (j n)")),
                             ("gram_mask", gmask[:].rearrange("p j n -> p (j n)"))):
                    sp.dma_start(t, io[n]).then_inc(tables, 16)
                G.wait(sp, "wa")
                with sp.Fori(0, CB) as p:
                    Qt.wait(sp, "g", p - 1)
                    sp.dma_start(wa[0:64, 0, :], io["w_up_w"].rearrange("l r n -> r l n")[:, ds(l, 1), ds(p * P, P)]
                                 .rearrange("r a n -> r (a n)")).then_inc(wload, 16)
                    sp.dma_start(wa[64:128, 1, :], io["a_up_w"].rearrange("l r n -> r l n")[:, ds(l, 1), ds(p * P, P)]
                                 .rearrange("r a n -> r (a n)")).then_inc(wload, 16)
                    sp.dma_start(gup[:], io["g_up_w"].rearrange("l r n -> r l n")[:, ds(l, 1), ds(p * P, P)]
                                 .rearrange("r a n -> r (a n)")).then_inc(wload, 16)
                    Vt.wait(sp, f"gm{NW - 1}", p)
                    At.wait(sp, f"tm{NW - 1}", p)
                    st = io["state_wkv"].rearrange("l b h v k -> h v (l b) k")
                    po_d = io["wkv_prompt"].rearrange("l a h v k -> (l a h) v k")
                    for hf in range(2):
                        r = slice(64 * hf, 64 * hf + 64)
                        sp.dma_start(Bb[r, 0:NB, r], st[ds(p * 2 + hf, 1), :, ds(l * NB, NB), :]
                                     .rearrange("a v b k -> (a v) b k")).then_inc(sload, 16)
                    At.wait(sp, "final", p)
                    for hf in range(2):
                        r = slice(64 * hf, 64 * hf + 64)
                        sp.dma_start(po_d[ds(l * (2 * CB) + p * 2 + hf, 1), :, :].rearrange("a v k -> (a v) k"), so[r, r])\
                          .then_inc(store, 16)
                sp.wait_ge(store, 64 * CB + 64)
                sp.wait_ge(rows_store, 32)

            @block.tensor
            def _(pe):
                for c in range(CZ):
                    tr = pe.transpose(row_banks[c // 4][0:1 + NB, c % 4 * P:(c % 4 + 1) * P], last[:, c, :], self.ident[:])
                Q.did(tr, "rows")
                A.wait(pe, "rows")
                with pe.Fori(0, CB) as p:
                    Qt.loop(p)
                    At.wait(pe, "finals", p - 1)

                    def spread(out, lhs, rhs, name):
                        for half in range(2):
                            mm = pe.matmul(out[:, half, 0:NH], lhs, rhs[:, half * NH:(half + 1) * NH], start=True, stop=True)
                        Qt.did(mm, name)
                    Gt.wait(pe, "kksq", p)
                    spread(E[0], self.halves[:], pprev[:], "ss")
                    pe.wait_ge(wload, p * 48 + 48)
                    spread(D[0], wa[:, 0, :], low, "w")
                    spread(D[1], wa[:, 1, :], low, "a")
                    spread(E[1], gup[:], glow, "g")
                    Vt.wait(pe, "rkr", p)
                    At.wait(pe, "decay", p)
                    spread(D[0], self.halves[:], tmp, "bonus")
                    Gt.wait(pe, "r", p)
                    Vt.wait(pe, "ar", p)
                    At.wait(pe, "gg", p)
                    for w in range(NW):
                        if w >= 2:
                            Vt.wait(pe, f"gm{w - 2}", p)
                        for i, b in ((1, Kb), (0, Bb)):
                            if w == i == 0:
                                Vt.wait(pe, "operands", p)
                            mm = pe.matmul(gram_bank(w)[:, i * (P + W):(i + 1) * (P + W)], b[:, w, :], AR[:, w, :],
                                           start=True, stop=True)
                        Qt.did(mm, f"gram{w}")
                        if w >= 2:
                            At.wait(pe, f"tm{w - 2}", p)
                        elif w == 0:
                            Vt.wait(pe, "bonus", p)
                        for i, b in enumerate((Bb, Kb, Vb)):
                            tr = pe.transpose(tok_bank(w)[:, i * P:(i + 1) * P], b[:, w, :], self.ident[:])
                        Qt.did(tr, f"tok{w}")

                    def turn(j, g):
                        for i in range(GW):
                            tr = pe.transpose(inv_bank(g)[:, i * P:(i + 1) * P], TT[:, g * GW + i, :], self.ident[:])
                        Qt.did(tr, f"tr{j}_{g}")
                    for g in range(NG):
                        Gt.wait(pe, f"tt0_{g}", p)
                        turn(0, g)
                    for j in range(1, 6):
                        for g in range(NG):
                            At.wait(pe, f"t{j - 1}_{g}", p)
                            Gt.wait(pe, f"lm{j}_{g}", p)
                            for i in range(GW):
                                mm = pe.matmul(inv_bank(g)[:, i * P:(i + 1) * P], Lm[:, g * GW + i, :], T[:, g * GW + i, :],
                                               start=True, stop=True)
                            Qt.did(mm, f"w{j}_{g}")
                        for g in range(NG):
                            Vt.wait(pe, f"w{j}_{g}", p)
                            for i in range(GW):
                                mm = pe.matmul(inv_bank(g)[:, i * P:(i + 1) * P], W1[:, g * GW + i, :], TT[:, g * GW + i, :],
                                               start=True, stop=True)
                            Qt.did(mm, f"dt{j}_{g}")
                        for g in range(NG):
                            Vt.wait(pe, f"tt{j}_{g}", p)
                            if j < 5:
                                turn(j, g)
                    At.wait(pe, f"tm{NW - 1}", p)
                    for w in range(NW - 1):
                        s = S[w % 2]
                        pe.matmul(D[0][:, 0, 0:P], GM[:, w, 1, 0:P], TM[:, w, 2, :], start=True, stop=False)
                        if w:
                            Vt.wait(pe, f"s{w}", p)
                        else:
                            Gt.wait(pe, "s0", p)
                        Qt.did(pe.matmul(D[0][:, 0, 0:P], AR[:, w, 0:P], s[:], start=False, stop=True), f"x{w}")
                        pe.matmul(D[1][:, 0, 0:P], TM[:, w, 1, :], TM[:, w, 2, :], start=True, stop=False)
                        At.wait(pe, f"xs{w}", p)
                        Qt.did(pe.matmul(D[0][:, 1, 0:P], TT[:, w, :], Xs[:], start=True, stop=True), f"u{w}")
                        if w:
                            At.wait(pe, f"yo{w - 1}", p)
                        pe.matmul(D[1][:, 1, 0:W], s[:], AR[:, w, P:], start=True, stop=False)
                        pe.matmul(D[1][:, 1, 0:W], TM[:, w, 2, :], GM[:, w, 1, P:], start=False, stop=False)
                        Vt.wait(pe, f"us{w}", p)
                        Qt.did(pe.matmul(D[1][:, 0, 0:P], TM[:, w, 0, :], Us[:], start=False, stop=True), f"st{w}")
                        Qt.did(pe.matmul(D[1][:, 1, 0:W], Us[:], GM[:, w, 0, P:], start=False, stop=True), f"y{w}")
                    w = NW - 1
                    Vt.wait(pe, f"s{w}", p)
                    Qt.did(pe.transpose(E[0][:, 0, 0:P], S[w % 2][:], self.ident[:]), "final")
                    pe.wait_ge(sload, p * 32 + 32)
                    for b in range(NB):
                        tr = pe.transpose(E[1][:, b // 4, b % 4 * P:(b % 4 + 1) * P], Bb[:, b, :], self.ident[:])
                    Qt.did(tr, "sturn")
                    At.wait(pe, "s0s", p)
                    heads = lambda t: t.rearrange("p (h s) -> p h s", h=2)
                    for b in range(NB):
                        t = slice(b * TS, (b + 1) * TS)
                        mm = pe.matmul(heads(D[0][:, 0, 0:P])[:, :, t], Kb[:, b, :], heads(AR[:, w, 0:P])[:, :, t],
                                       start=(b == 0), stop=(b == NB - 1), skip_group_check=True)
                    Qt.did(mm, "from_states")
                    At.wait(pe, "from_states", p)
                    pe.matmul(D[0][:, 1, 0:P], so[:], self.ident[:], start=True, stop=False)
                    Qt.did(pe.matmul(D[0][:, 1, 0:P], GM[:, w, 1, 0:P], TM[:, w, 2, :], start=False, stop=True), f"x{w}")
                    At.wait(pe, f"xs{w}", p)
                    Qt.did(pe.matmul(D[1][:, 0, 0:P], TT[:, w, :], Xs[:], start=True, stop=True), f"u{w}")
                    At.wait(pe, f"yo{w - 1}", p)
                    Vt.wait(pe, f"us{w}", p)
                    for b in range(NB):
                        t = slice(b * TS, (b + 1) * TS)
                        pe.matmul(D[1][:, 1, t], Kb[:, b, :], AR[:, w, P + b * TS:P + (b + 1) * TS],
                                  start=(b == 0), stop=False, skip_group_check=True)
                    pe.matmul(D[1][:, 1, 0:W], Us[:], GM[:, w, 0, P:], start=False, stop=False, skip_group_check=True)
                    Qt.did(pe.matmul(D[1][:, 1, 0:W], TM[:, w, 2, :], GM[:, w, 1, P:], start=False, stop=True,
                                     skip_group_check=True), f"y{w}")
                    At.wait(pe, f"yo{w}", p)
                    spread(D[0], self.halves[:], yt[:], "mean")
                    Vt.wait(pe, "masked", p)
                    At.wait(pe, "final", p)
                    for half in range(2):
                        r = slice(4 * half, 4 * half + 4)
                        pe.matmul(E[0][:, half, :], TM[:, w, 0, :], Bb[:, r, :].rearrange("p b n -> p (b n)"),
                                  start=True, stop=False)
                        mm = pe.matmul(E[0][:, half, :], TM[:, w, 1, :], Vb[:, r, :].rearrange("p b n -> p (b n)"),
                                       start=False, stop=True)
                    Qt.did(mm, f"st{w}")
                    At.wait(pe, "ysq", p)
                    spread(D[1], self.halves[:], sq[:], "var")
                    Vt.wait(pe, "snew", p)
                    for b in range(NB):
                        tr = pe.transpose(E[1][:, b // 4, b % 4 * P:(b % 4 + 1) * P], Kb[:, b, :], self.ident[:])
                    Qt.did(tr, "finals")
                Qt.end(CB)

            @block.scalar
            def _(act):
                act.preload_act_table_set("sigmoid_and_others")
                act.activation(z[0:64, 3 * CB, :], z[0:64, 3 * CB, :], ACT.Tanh)
                A.did(act.activation(z[:, 3 * CB + 1, :], z[:, 3 * CB + 1, :], ACT.Sigmoid), "low")
                Q.wait(act, "rows")
                for i, bank in enumerate(row_banks):
                    n = min(512, NSHIFT - i * 512)
                    row = act.activation(rows_out[:, i * 512:i * 512 + n], bank[0:1 + NB, 0:n], ACT.Copy)
                A.did(row, "rows")
                A.own(act)
                act.dma_start(io["shift_prompt"].rearrange("l b n -> (l b) n")[ds(l, 1), :], rows_out[0:1, :])\
                   .then_inc(rows_store, 16)
                act.dma_start(io["shift_sample"].rearrange("l b n -> (l b) n")[ds(l * NB, NB), :], rows_out[1:1 + NB, :])\
                   .then_inc(rows_store, 16)
                with act.Fori(0, CB) as p:
                    At.loop(p)
                    act.preload_act_table_set("sigmoid_and_others")
                    v0 = lambda n: self.vec[:, ds(p + VEC[n][0], 1)]
                    Qt.wait(act, "w", p)
                    At.own(act)
                    At.did(act.activation(two(lw[:]), D[0][:, :, 0:NH], ACT.Sigmoid, bias=v0("w0"), scale=1.0), "decay")
                    Qt.wait(act, "a", p)
                    At.own(act)
                    At.did(act.activation(two(a[:]), D[1][:, :, 0:NH], ACT.Sigmoid, bias=v0("a0"), scale=1.0), "a")
                    act.preload_act_table_set("natural_log_exp_and_others")
                    Vt.wait(act, "ssmax", p)
                    At.own(act)
                    At.did(act.activation(pprev[:], pprev[:], ACT.Ln))
                    At.own(act)
                    At.did(act.activation(sq[:], pprev[:], ACT.Exp, scale=-0.5), "rss")
                    Qt.wait(act, "g", p)
                    At.own(act)
                    At.did(act.activation(two(gg[:]), E[1][:, :, 0:NH], ACT.Copy), "gg")
                    Vt.wait(act, "cum", p)
                    act.activation(pin[:], cum[:], ACT.Exp)
                    At.own(act)
                    At.did(act.activation(pinv[:], cum[:], ACT.Exp, scale=-1.0), "pinv")
                    Vt.wait(act, "before", p)
                    At.own(act)
                    At.did(act.activation(pprev[:], lw[:], ACT.Exp), "pprev")
                    for w in range(NW):
                        Qt.wait(act, f"tok{w}", p)
                        At.own(act)
                        At.did(act.activation(TM[:, w].rearrange("p i n -> p (i n)"), tok_bank(w), ACT.Copy), f"tm{w}")
                    for j in range(5):
                        for g in range(NG):
                            Qt.wait(act, f"tr{j}_{g}", p)
                            At.own(act)
                            At.did(act.activation(T[:, grp(g), :], blocks(inv_bank(g)), ACT.Copy), f"t{j}_{g}")
                    for w in range(NW - 1):
                        Qt.wait(act, f"x{w}", p)
                        At.own(act)
                        At.did(act.activation(Xs[:], D[0][:, 0, 0:P], ACT.Copy), f"xs{w}")
                        Qt.wait(act, f"y{w}", p)
                        At.own(act)
                        At.did(act.activation(yt[:, w * W:(w + 1) * W], D[1][:, 1, 0:W], ACT.Copy), f"yo{w}")
                    w = NW - 1
                    Qt.wait(act, "final", p)
                    act.wait_ge(store, p * 64 + 64)
                    At.own(act)
                    At.did(act.activation(so[:], E[0][:, 0, 0:P], ACT.Copy), "final")
                    Qt.wait(act, "sturn", p)
                    At.own(act)
                    At.did(act.activation(Kb[:, 0:NB, :].rearrange("p (a b) n -> p a (b n)", a=2), E[1][:], ACT.Copy), "s0s")
                    Qt.wait(act, "from_states", p)
                    act.wait_ge(store, p * 64 + 96)
                    At.own(act)
                    At.did(act.activation(so[:], D[0][:, 0, 0:P], ACT.Copy), "from_states")
                    Qt.wait(act, f"x{w}", p)
                    At.own(act)
                    At.did(act.activation(Xs[:], D[0][:, 1, 0:P], ACT.Copy), f"xs{w}")
                    Qt.wait(act, f"y{w}", p)
                    At.own(act)
                    At.did(act.activation(yt[:, w * W:(w + 1) * W], D[1][:, 1, 0:W], ACT.Copy), f"yo{w}")
                    Vt.wait(act, "centred", p)
                    At.own(act)
                    At.did(act.activation(sq[:], yt[:], ACT.Square), "ysq")
                    Qt.wait(act, "var", p)
                    At.own(act)
                    At.did(act.activation(two(cum[:]), D[1][:, :, 0:NH], ACT.Ln, bias=self.eps[:, 2:3], scale=1.0 / W))
                    At.own(act)
                    At.did(act.activation(cum[:], cum[:], ACT.Exp, scale=-0.5), "yrstd")
                    Qt.wait(act, "finals", p)
                    At.own(act)
                    At.did(act.activation(Bb[:, 0:NB, :].rearrange("p (a b) n -> p a (b n)", a=2), E[1][:], ACT.Copy), "finals")
                    At.own(act)
                    so_d = io["wkv_sample"].rearrange("l b h v k -> h v (l b) k")
                    for hf in range(2):
                        r = slice(64 * hf, 64 * hf + 64)
                        act.dma_start(so_d[ds(p * 2 + hf, 1), :, ds(l * NB, NB), :].rearrange("a v b k -> (a v) b k"),
                                      Bb[r, 0:NB, r]).then_inc(store, 16)
                At.end(CB)

            @block.vector
            def _(dve):
                dve.wait_ge(tables, 64)
                ka0 = VEC["k_a"][0]
                V.own(dve)
                V.did(dve.tensor_scalar(omka[:], self.vec[:, ka0:ka0 + CB], -1.0, 1.0, ALU.mult, ALU.add), "omka")
                dve.wait_ge(rows_store, 32)
                with dve.Fori(0, CB) as p:
                    Vt.loop(p)
                    v0 = lambda n: self.vec[:, ds(p + VEC[n][0], 1)]
                    zr = lambda i, r=slice(0, P): z[r, ds(p + i * CB, 1), :].rearrange("p a t -> p (a t)")
                    Qt.wait(dve, "ss", p)
                    Vt.own(dve)
                    Vt.did(dve.tensor_scalar(two(pprev[:]), E[0][:, :, 0:NH], 1e-24, None, ALU.max), "ssmax")
                    At.wait(dve, "decay", p)
                    Vt.own(dve)
                    Vt.did(dve.tensor_scalar(lw[:], lw[:], cmul, None, ALU.mult))
                    Vt.own(dve)
                    Vt.did(dve.tensor_tensor_scan(cum[:], carry[:], lw[:], 0.0, ALU.mult, ALU.add), "cum")
                    Vt.own(dve)
                    Vt.did(dve.tensor_tensor(lw[:], cum[:], lw[:], ALU.subtract), "before")
                    At.wait(dve, "rss", p)
                    Vt.own(dve)
                    Vt.did(dve.tensor_tensor(kk[:], kk[:], sq[:], ALU.mult), "kkn")
                    Gt.wait(dve, "kp", p)
                    Vt.own(dve)
                    Vt.did(dve.scalar_tensor_tensor(tmp[:], kp[:], v0("r_k"), zr(0), ALU.mult, ALU.mult), "rkr")
                    At.wait(dve, "pprev", p)
                    G.wait(dve, "zero")
                    Vt.own(dve)
                    for hf in range(2):
                        r = slice(64 * hf, 64 * hf + 64)
                        o = dve.tensor_tensor(Kb[r, :, r], win(kp, r), win(pinv, r), ALU.mult)
                    Vt.did(o)
                    Vt.own(dve)
                    for hf in range(2):
                        r = slice(64 * hf, 64 * hf + 64)
                        o = dve.scalar_tensor_tensor(AR[r, :, r], win(kk, r), -1.0, win(pprev, r), ALU.mult, ALU.mult)
                    Vt.did(o, "ar")
                    Gt.wait(dve, "kka", p)
                    Vt.own(dve)
                    dve.wait_ge(store, p * 64 + 64)
                    for hf in range(2):
                        r = slice(64 * hf, 64 * hf + 64)
                        o = dve.tensor_tensor(Bb[r, :, r], win(a, r), win(pinv, r), ALU.mult)
                    Vt.did(o, "operands")
                    Qt.wait(dve, "bonus", p)
                    Vt.own(dve)
                    Vt.did(dve.tensor_tensor(two(bonus[:]), D[0][:, :, 0:NH], two(zr(2)), ALU.mult), "bonus")
                    for w in range(NW):
                        Qt.wait(dve, f"gram{w}", p)
                        m = gmask[:, w // (NW - 1):w // (NW - 1) + 1, :].to_broadcast([P, 2, P + W])
                        Vt.own(dve)
                        Vt.did(dve.tensor_tensor(GM[:, w], gram_bank(w).rearrange("p (i n) -> p i n", i=2), m, ALU.mult), f"gm{w}")
                    for j in range(1, 6):
                        for g in range(NG):
                            Qt.wait(dve, f"w{j}_{g}", p)
                            Vt.own(dve)
                            Vt.did(dve.tensor_copy(W1[:, grp(g), :], blocks(inv_bank(g))), f"w{j}_{g}")
                        for g in range(NG):
                            Qt.wait(dve, f"dt{j}_{g}", p)
                            if j > 1:
                                Vt.own(dve)
                            Vt.did(dve.tensor_tensor(TT[:, grp(g), :], TT[:, grp(g), :], blocks(inv_bank(g)), ALU.add), f"tt{j}_{g}")
                    for w in range(NW - 1):
                        Qt.wait(dve, f"u{w}", p)
                        Vt.own(dve)
                        Vt.did(dve.tensor_copy(Us[:], D[0][:, 1, 0:P]), f"us{w}")
                        Qt.wait(dve, f"st{w}", p)
                        Gt.wait(dve, f"sp{w}", p)
                        e = w * W + W - 1
                        Vt.own(dve)
                        Vt.did(dve.scalar_tensor_tensor(S[(w + 1) % 2][:], D[1][:, 0, 0:P], pin[:, e:e + 1], SP[:],
                                                        ALU.mult, ALU.add), f"s{w + 1}")
                        Qt.wait(dve, f"y{w}", p)
                    w = NW - 1
                    Qt.wait(dve, f"u{w}", p)
                    Vt.own(dve)
                    Vt.did(dve.tensor_copy(Us[:], D[1][:, 0, 0:P]), f"us{w}")
                    Vt.own(dve)
                    bm = bmask[:].unsqueeze(2).to_broadcast([P, NB, P])
                    dve.tensor_tensor(Bb[:, 0:NB, :], Us[:].unsqueeze(1).to_broadcast([P, NB, P]), bm, ALU.mult)
                    Vt.own(dve)
                    Vt.did(dve.tensor_tensor(Vb[:, 0:NB, :], TM[:, w, 2:3, :].to_broadcast([P, NB, P]), bm, ALU.mult), "masked")
                    Qt.wait(dve, "mean", p)
                    Vt.own(dve)
                    Vt.did(dve.scalar_tensor_tensor(two(yt[:]), D[0][:, :, 0:NH], -1.0 / W, two(yt[:]), ALU.mult, ALU.add), "centred")
                    Qt.wait(dve, f"st{w}", p)
                    kv = Kb[:, 0:NB, :].rearrange("p (a b) n -> p a (b n)", a=2)
                    Vt.own(dve)
                    Vt.did(dve.tensor_tensor(kv, kv, E[0][:], ALU.add))
                    Vt.own(dve)
                    pe_ = pin[:, TP + TS - 1:NT:TS].unsqueeze(2).to_broadcast([P, NB, P])
                    Vt.own(dve)
                    Vt.did(dve.tensor_tensor(Kb[:, 0:NB, :], Kb[:, 0:NB, :], pe_, ALU.mult), "snew")
                    At.wait(dve, "yrstd", p)
                    Vt.own(dve)
                    Vt.did(dve.tensor_tensor(yt[:], yt[:], cum[:], ALU.mult))
                    Vt.own(dve)
                    Vt.did(dve.tensor_scalar(yt[:], yt[:], v0("lnx_w"), v0("lnx_b"), ALU.mult, ALU.add))
                    Vt.own(dve)
                    Vt.did(dve.tensor_tensor(yt[:], yt[:], bonus[:], ALU.add))
                    Vt.own(dve)
                    At.wait(dve, "finals", p)
                    Vt.did(dve.tensor_tensor(y[:, ds(p + 4, 1), :].rearrange("p a t -> p (a t)"), yt[:], gg[:], ALU.mult), "out")
                Vt.end(CB)

            @block.gpsimd
            def _(pool):
                self.credits(pool, (At, Vt, Qt, Gt))
                pool.memset(self.junk[:, 14:15], 0.0).then_inc(store, 64)
                G.own(pool)
                G.did(pool.memset(wa[:], 0.0), "wa")
                for p in range(CB):
                    Gt.loop(p)
                    v0 = lambda n: self.vec[:, ds(p + VEC[n][0], 1)]
                    zr = lambda i, r=slice(0, P): z[r, ds(p + i * CB, 1), :].rearrange("p a t -> p (a t)")
                    Vt.wait(pool, f"us{NW - 1}", p - 1)
                    Gt.own(pool)
                    Gt.did(pool.tensor_scalar(kk[:], zr(1), v0("k_k"), None, ALU.mult))
                    Gt.own(pool)
                    Gt.did(pool.tensor_tensor(pprev[:], kk[:], kk[:], ALU.mult), "kksq")
                    Vt.wait(pool, "snew", p - 1)
                    if p == 0:
                        for t, n in ((Vb, None), (AR, None), (Kb, None), (Bb, "zero")):
                            G.own(pool)
                            G.did(pool.memset(t[:], 0.0), n)
                        G.own(pool)
                        pool.wait_ge(tables, 64)
                        V.wait(pool, "omka")
                    for hf in range(2):
                        r = slice(64 * hf, 64 * hf + 64)
                        Gt.own(pool)
                        Gt.did(pool.tensor_copy(Vb[r, :, r], zr(2, r).rearrange("p (w s) -> p w s", w=NW)))
                    Gt.own(pool)
                    Gt.did(pool.memset(S[0][:], 0.0), "s0")
                    At.wait(pool, "a", p)
                    Gt.own(pool)
                    Gt.did(pool.tensor_scalar(kp[:], a[:], v0("k_a"), omka[:, ds(p, 1)], ALU.mult, ALU.add))
                    Gt.own(pool)
                    Gt.did(pool.tensor_tensor(kp[:], kp[:], zr(1), ALU.mult), "kp")
                    Vt.wait(pool, "kkn", p)
                    Gt.own(pool)
                    Gt.did(pool.tensor_tensor(a[:], kk[:], a[:], ALU.mult), "kka")
                    At.wait(pool, "pinv", p)
                    Gt.own(pool)
                    Gt.did(pool.tensor_tensor(AR[:, :, P:], zr(0).rearrange("p (w s) -> p w s", w=NW), win(pin[:]), ALU.mult), "r")
                    Vt.wait(pool, "operands", p)
                    Qt.wait(pool, "bonus", p)
                    for g in range(NG):
                        Vt.wait(pool, f"gm{g * GW + GW - 1}", p)
                        LT = GM[:, grp(g), 0, 0:P]
                        m = lambda j: lev[:, j:j + 1, :].to_broadcast([P, GW, P])
                        Gt.own(pool)
                        Gt.did(pool.tensor_tensor(TT[:, grp(g), :], LT, m(0), ALU.mult))
                        Gt.own(pool)
                        Gt.did(pool.tensor_tensor(TT[:, grp(g), :], TT[:, grp(g), :],
                                                  self.ident[:].unsqueeze(1).to_broadcast([P, GW, P]), ALU.add), f"tt0_{g}")
                        Gt.own(pool)
                        Gt.did(pool.tensor_tensor(Lm[:, grp(g), :], LT, m(1), ALU.mult), f"lm1_{g}")
                    for j in range(2, 6):
                        for g in range(NG):
                            LT = GM[:, grp(g), 0, 0:P]
                            m = lev[:, j:j + 1, :].to_broadcast([P, GW, P])
                            Qt.wait(pool, f"w{j - 1}_{g}", p)
                            Gt.own(pool)
                            Gt.did(pool.tensor_tensor(Lm[:, grp(g), :], LT, m, ALU.mult), f"lm{j}_{g}")
                    for w in range(NW - 1):
                        e = w * W + W - 1
                        if w:
                            Vt.wait(pool, f"s{w}", p)
                        else:
                            Gt.own(pool)
                        Gt.did(pool.tensor_scalar(SP[:], S[w % 2][:], pin[:, e:e + 1], None, ALU.mult), f"sp{w}")
                Gt.end(CB)

    def merge(self, l, y, y_hi, y_lo, m_hi, m_lo, tile):
        nc, io, ev = self.nc, self.io, self.evac
        gates = [tile(f"gate{i}", [P, NT]) for i in range(3)]
        part, acc = tile("part", [P, NT]), tile("acc", [P, NT])
        win = io["w_in"].rearrange("l (c p) n -> p (l c) n", p=P)
        wb = [io[f"w_branch_{b}"].rearrange("l (c p) n -> p (l c) n", p=P) for b in "abc"]
        wo = io["w_out"].rearrange("l (c p) n -> p (l c) n", p=P)
        two = lambda t: t.rearrange("p (a t) -> p a t", a=2)
        GP = 3 * KD
        A, V, Q, G = self.stage_steps("merge")

        with nc.Block() as block:
            @block.gpsimd
            def _(pool):
                self.credits(pool)

            @block.sync
            def _(sp):
                with sp.Fori(0, KD) as c:
                    for j in range(6):
                        src = win[:, ds(l * KD, KD), ds((c + (COL_G + KD * j)) * P, P)] if j < 3 else \
                            wb[j - 3][:, ds(l * CB, CB), ds(c * P, P)]
                        self.load_w(sp, c * 3 + j // 2, j % 2, src)
                with sp.Fori(0, KD // 2) as c:
                    for s in range(2):
                        self.load_w(sp, c + GP, s, wo[:, ds(l * KD, KD), ds((c * 2 + s) * P, P)])

            @block.tensor
            def _(pe):
                with pe.Fori(0, KD) as c:
                    for j in range(6):
                        k, s = c * 3 + j // 2, j % 2
                        use = (s, c * 3 + (j // 2 + 1))
                        if j < 3:
                            self.products(pe, k, s, self.h_hi, self.h_lo, self.D[s], use)
                        else:
                            r = slice((j - 3) * CB, (j - 2) * CB)
                            self.products(pe, k, s, y_hi[:, r, :], y_lo[:, r, :], self.D[s], use,
                                          ready=lambda n, j=j: V.wait(pe, f"lo{(j - 3) * CB + n}"))
                with pe.Fori(0, KD // 2) as c:
                    for s in range(2):
                        self.products(pe, c + GP, s, m_hi, m_lo, self.D[s], (s, c + (GP + 1)),
                                      ready=(lambda n: pe.wait_ge(self.part_lo, n + 2)) if s == 0 else None)

            @block.scalar
            def _(act):
                act.preload_act_table_set("sigmoid_and_others")
                for s in range(2):
                    self.split_hi(act, 0, s)
                for c in range(3 * CB):
                    A.did(act.activation(y_hi[:, c, :], y[:, c, :], ACT.Copy), f"hi{c}")
                def gate(i, j, c, s):
                    if 2 * j + s < 3:
                        act.wait_ge(self.mm_done, i * 2 + (s + 3))
                        act.activation(two(gates[2 * j + s][:]), self.D[s][:, :, 0:NH], ACT.Sigmoid).then_inc(ev[s], 1)
                    elif j == 2 and s == 1:
                        act.wait_ge(self.dve_turns, c * 2 + 2)
                        act.activation(m_hi[:, ds(c, 1), :].rearrange("p a t -> p (a t)"), acc[:], ACT.Copy)\
                           .then_inc(self.part_hi, 1)
                self.chase(act, lambda k, s: self.split_hi(act, k, s), [(GP, 3, gate), (KD // 2, 1, lambda i, j, c, s: None)],
                           begun=True)

            @block.vector
            def _(dve):
                def branch(i, j, c, s):
                    n = i * 2
                    if j == 1 and s == 1:
                        dve.wait_ge(self.mm_done, n + 4)
                        dve.wait_ge(ev[0], c * 3 + 2)
                        dve.wait_ge(self.part_lo, c + 1)
                        dve.tensor_tensor(two(acc[:]), self.D[1][:, :, 0:NH], two(gates[0][:]), ALU.mult).then_inc(ev[1], 1)
                    if j == 2 and s == 0:
                        dve.wait_ge(self.mm_done, n + 3)
                        dve.wait_ge(ev[1], c * 3 + 3)
                        dve.tensor_tensor(two(part[:]), self.D[0][:, :, 0:NH], two(gates[1][:]), ALU.mult).then_inc(ev[0], 1)
                        dve.wait_ge(ev[0], c * 3 + 4)
                        dve.tensor_tensor(acc[:], acc[:], part[:], ALU.add).then_inc(self.dve_turns, 1)
                    if j == 2 and s == 1:
                        dve.wait_ge(self.mm_done, n + 4)
                        dve.wait_ge(self.dve_turns, c * 2 + 1)
                        dve.tensor_tensor(two(part[:]), self.D[1][:, :, 0:NH], two(gates[2][:]), ALU.mult).then_inc(ev[1], 1)
                        dve.wait_ge(ev[1], c * 3 + 4)
                        dve.tensor_tensor(acc[:], acc[:], part[:], ALU.add).then_inc(self.dve_turns, 1)
                        dve.wait_ge(self.part_hi, c + 1)
                        dve.tensor_tensor(m_lo[:, ds(c, 1), :].rearrange("p a t -> p (a t)"), acc[:],
                                          m_hi[:, ds(c, 1), :].rearrange("p a t -> p (a t)").bitcast(F32),
                                          ALU.subtract).then_inc(self.part_lo, 1)

                def add_out(i, j, c, s):
                    dve.wait_ge(self.mm_done, i * 2 + (2 * GP + s + 3))
                    xs = self.x[:, ds(i * 2 + s, 1), :].rearrange("p a (b t) -> p (a b) t", b=2)
                    dve.tensor_tensor(xs, self.D[s][:, :, 0:NH], xs, ALU.add).then_inc(ev[s], 1)
                for s in range(2):
                    self.split_lo(dve, 0, s)
                for c in range(3 * CB):
                    A.wait(dve, f"hi{c}")
                    V.did(dve.tensor_tensor(y_lo[:, c, :], y[:, c, :], y_hi[:, c, :].bitcast(F32), ALU.subtract), f"lo{c}")
                self.chase(dve, lambda k, s: self.split_lo(dve, k, s), [(GP, 3, branch), (KD // 2, 1, add_out)], begun=True)

    def finish(self):
        nc, io = self.nc, self.io
        tile = self.region("final", self.r0)
        self.norm_tiles(tile)
        A, V, Q, G = self.stage_steps("final")
        out = tile("out", [P, TP // P + 1, D])
        nblk = TP // P + 1
        with nc.Block() as block:
            @block.tensor
            def _(pe):
                self.norm_pe(pe, V, Q)
                V.wait(pe, "y")
                for b in range(nblk):
                    m = P if b < nblk - 1 else NS
                    if b >= 2:
                        (A, V)[b % 2].wait(pe, f"out{b - 2}")
                    for c in range(KD):
                        tr = pe.transpose(self.D[b % 2][0:m, c // 4, c % 4 * P:(c % 4 + 1) * P],
                                          self.x[:, c, b * P:b * P + m], self.ident[:])
                    Q.did(tr, f"turn{b}")

            @block.scalar
            def _(act):
                self.norm_act(act, A, V, Q)
                for b in range(0, nblk, 2):
                    m = P if b < nblk - 1 else NS
                    Q.wait(act, f"turn{b}")
                    A.own(act)
                    A.did(act.activation(out[0:m, b, :].rearrange("p (a n) -> p a n", a=2), self.D[0][0:m], ACT.Copy), f"out{b}")

            @block.vector
            def _(dve):
                self.norm_dve(dve, A, V)
                A.wait(dve, "root")
                V.own(dve)
                V.did(dve.reciprocal(self.rstd[:], self.rstd[:]))
                V.own(dve)
                for c in range(KD):
                    o = dve.scalar_tensor_tensor(self.x[:, c, :], self.x[:, c, :], self.vec_all[:, L - 1, NVEC + c:NVEC + c + 1],
                                                 self.rstd[:], ALU.mult, ALU.mult)
                V.did(o, "y")
                for b in range(1, nblk, 2):
                    Q.wait(dve, f"turn{b}")
                    V.own(dve)
                    V.did(dve.tensor_copy(out[:, b, :].rearrange("p (a n) -> p a n", a=2), self.D[1][:]), f"out{b}")

            @block.sync
            def _(sp):
                A.wait(sp, f"out{nblk - 1}")
                V.wait(sp, f"out{nblk - 2}")
                sp.dma_start(io["y_prompt"].rearrange("a (b p) d -> p (a b) d", p=P), out[:, 0:nblk - 1, :])\
                  .then_inc(self.stores[0], 16)
                sp.dma_start(io["y_sample"].rearrange("b s d -> (b s) d"), out[0:NS, nblk - 1, :]).then_inc(self.stores[0], 16)
                sp.wait_ge(self.stores[0], 32)

    def build(self):
        nc = self.nc
        KB = 4 * NT
        y = self.place("y", [P, 12, NT], self.r0)
        proj = self.place("proj", [P, 24, NT], self.r0 + 12 * KB)
        z = self.place("z", [P, CZ, NT], self.r0 + 12 * KB)
        tile = self.region("last", self.r0 + 4 * KB)
        last, rows_out = tile("last", [P, CZ, 1 + NB]), tile("rows_out", [1 + NB, NSHIFT])
        m_hi = self.place("m_hi", [P, KD, NT], self.r0, F32R)
        m_lo = self.place("m_lo", [P, KD, NT], self.r0 + KD * KB, F32R)
        y_hi = self.place("y_hi", [P, 12, NT], self.r0 + 16 * KB, F32R)
        y_lo = self.place("y_lo", [P, 12, NT], self.r0 + 28 * KB, F32R)
        self.setup()
        with nc.Fori(0, L) as l:
            self.barrier()
            self.ffn(l, "ffn1")
            self.barrier()
            tile = self.region("proj", self.r0 + 36 * KB)
            self.norm_tiles(tile)
            self.project(l, "proj", [(0, 12), (COL_Q, 12)], proj)
            self.barrier()
            tile = self.region("attn", self.r0 + 36 * KB)
            vtok = tile("vtok", [P, TP // P + 1, DB])
            after = tile.at[0]
            self.prompt_attention(l, proj, y, vtok, tile)
            self.barrier()
            self.sample_attention(l, proj, y, vtok, self.region("sample", after))
            self.barrier()
            self.project_shifted(l, z, last, self.region("z", self.r0 + (12 + CZ) * KB))
            self.barrier()
            self.recurrence(l, z, y, last, rows_out, self.region("rwkv", self.r0 + (12 + CZ) * KB))
            self.barrier()
            self.merge(l, y, y_hi, y_lo, m_hi, m_lo, self.region("merge", self.r0 + 40 * KB))
            self.barrier()
            self.ffn(l, "ffn2")
        self.barrier()
        self.finish()


def program(make_nc, io_of):
    book = {}
    for _ in range(2):
        nc = make_nc()
        io = io_of(nc)
        with ExitStack() as ctx:
            core = Core(nc, ctx, io, book)
            core.build()
            assert _ == 0 or core.new == book
        book = core.new
    return nc


_INS = ['x_prompt', 'x_sample', 'cache_k', 'cache_v', 'state_wkv', 'state_shift', 'state_conv', 'page_table',
        'ffn1_norm', 'ffn1_w_gate', 'ffn1_w_up', 'ffn1_w_down', 'mix_norm', 'w_in', 'conv_w', 'tm_mu',
        'w_up_w', 'w0', 'a_up_w', 'a0', 'g_up_w', 'k_k', 'k_a', 'r_k', 'lnx_w', 'lnx_b',
        'lam_q1', 'lam_k1', 'lam_q2', 'lam_k2', 'subln_w', 'w_branch_a', 'w_branch_b', 'w_branch_c', 'w_out',
        'ffn2_norm', 'ffn2_w_gate', 'ffn2_w_up', 'ffn2_w_down', 'final_norm']
_OUTS = [('y_prompt', (1, TP, D)), ('y_sample', (NB, TS, D)),
         ('k_prompt', (L, 1, TP, MAPS, 64)), ('v_prompt', (L, 1, TP, HC, P)),
         ('k_sample', (L, NB, TS, MAPS, 64)), ('v_sample', (L, NB, TS, HC, P)),
         ('wkv_prompt', (L, 1, 8, 64, 64)), ('wkv_sample', (L, NB, 8, 64, 64)),
         ('shift_prompt', (L, 1, NSHIFT)), ('shift_sample', (L, NB, NSHIFT)),
         ('conv_prompt', (L, 1, 2, DB)), ('conv_sample', (L, NB, 2, DB))]


def kernel(**inputs):
    import concourse.bacc as _bacc
    from concourse.bass_utils import run_bass_kernel_spmd as _run

    arrays = {n: np.ascontiguousarray(inputs[n]) for n in _INS}
    arrays.update(shape_constants())

    def io_of(nc):
        io = {n: nc.dram_tensor(f"in_{n}_dram", a.shape, mybir.dt.from_np(a.dtype), kind="ExternalInput").ap()
              for n, a in arrays.items()}
        io.update({n: nc.dram_tensor(f"out_{n}_dram", shape, F32, kind="ExternalOutput").ap() for n, shape in _OUTS})
        return io
    nc = program(lambda: _bacc.Bacc("TRN2", target_bir_lowering=False, num_devices=1), io_of)
    r = _run(nc, [{f"in_{n}_dram": a for n, a in arrays.items()}], core_ids=[0])
    return tuple(r.results[0][f"out_{n}_dram"] for n, _ in _OUTS)
```
